# Optimizing a Trainium2 kernel written in Bass

```python
import math
import jax, jax.numpy as jnp
from jax import lax
import numpy as np

D_MODEL = 1024
BATCH = 1
SEQ = 256
DEPTH = 1

GLA_HEADS = 4
GLA_DK = 64
GLA_DV = 128
GLA_RANK = 16
GLA_TAU = 16.0
GLA_CHUNK = 64
MOBA_HEADS = 8
MOBA_HD = 64
MOBA_BLOCK = 256
MOBA_TOPK = 3
MOBA_QCHUNK = 64
ROPE_THETA = 10000.0
MIX_WIDTH = GLA_HEADS * GLA_DV + MOBA_HEADS * MOBA_HD
IN_SPLITS = (GLA_HEADS * GLA_DK, GLA_HEADS * GLA_DK, GLA_HEADS * GLA_DV, GLA_HEADS * GLA_DV,
             GLA_RANK, MOBA_HEADS * MOBA_HD, MOBA_HEADS * MOBA_HD, MOBA_HEADS * MOBA_HD)
IN_WIDTH = sum(IN_SPLITS)
PEER_HEADS = 8
PEER_NKEYS = 128
PEER_N = PEER_NKEYS * PEER_NKEYS
PEER_QDIM = 256
PEER_TOPK = 16
PEER_TOKCHUNK = 128
EPS = 1e-6


def rmsnorm(x, w):
    xf = x.astype(jnp.float32)
    y = xf * lax.rsqrt(jnp.mean(xf * xf, axis=-1, keepdims=True) + EPS)
    return (y * w.astype(jnp.float32)).astype(x.dtype)

def rope(x, pos):
    hd = x.shape[-1]
    half = hd // 2
    inv = ROPE_THETA ** (-jnp.arange(half, dtype=jnp.float32) / half)
    ang = pos.astype(jnp.float32)[:, None] * inv[None, :]
    cos, sin = jnp.cos(ang), jnp.sin(ang)
    xf = x.astype(jnp.float32)
    x1, x2 = xf[..., :half], xf[..., half:]
    return jnp.concatenate([x1 * cos - x2 * sin, x2 * cos + x1 * sin], axis=-1).astype(x.dtype)

def to_heads(t, h):
    b, s, _ = t.shape
    return t.reshape(b, s, h, -1).transpose(0, 2, 1, 3)

def from_heads(t):
    b, h, s, d = t.shape
    return t.transpose(0, 2, 1, 3).reshape(b, s, h * d)

def gla_chunked(q, k, v, log_a):
    B, H, S, dk = q.shape
    dv = v.shape[-1]
    C = GLA_CHUNK
    nc = S // C
    q, k, g = (t.reshape(B, H, nc, C, dk) for t in (q, k, log_a))
    v = v.reshape(B, H, nc, C, dv)
    b = jnp.cumsum(g, axis=3)
    b_last = b[:, :, :, -1:, :]
    q_d = q * jnp.exp(b) * (dk ** -0.5)
    k_in = k * jnp.exp(-b)
    k_st = k * jnp.exp(b_last - b)
    causal = jnp.tril(jnp.ones((C, C), dtype=bool))
    A = jnp.where(causal, jnp.einsum('bhnid,bhnjd->bhnij', q_d, k_in), 0.0)
    o_intra = jnp.einsum('bhnij,bhnje->bhnie', A, v)
    upd = jnp.einsum('bhncd,bhnce->bhnde', k_st, v)
    decay = jnp.exp(b_last[:, :, :, 0, :])

    def step(state, inp):
        dec, u = inp
        return dec[..., None] * state + u, state

    init = jnp.zeros((B, H, dk, dv), jnp.float32)
    _, s_before = lax.scan(step, init, (jnp.moveaxis(decay, 2, 0), jnp.moveaxis(upd, 2, 0)))
    s_before = jnp.moveaxis(s_before, 0, 2)
    o_inter = jnp.einsum('bhncd,bhnde->bhnce', q_d, s_before)
    return (o_intra + o_inter).reshape(B, H, S, dv)

def moba_attention(q, k, v):
    B, H, S, hd = q.shape
    Sp = ((S + MOBA_BLOCK - 1) // MOBA_BLOCK) * MOBA_BLOCK
    padw = ((0, 0), (0, 0), (0, Sp - S), (0, 0))
    q, k, v = (jnp.pad(t, padw) for t in (q, k, v))
    nb = Sp // MOBA_BLOCK
    K = min(MOBA_TOPK, nb)
    kb = k.reshape(B, H, nb, MOBA_BLOCK, hd)
    vb = v.reshape(B, H, nb, MOBA_BLOCK, hd)
    kbar = jnp.mean(kb.astype(jnp.float32), axis=3)
    scale = hd ** -0.5
    bi = jnp.arange(B)[:, None, None, None]
    hi = jnp.arange(H)[None, :, None, None]
    nq = Sp // MOBA_QCHUNK

    def one_chunk(c):
        q0 = c * MOBA_QCHUNK
        qc = lax.dynamic_slice_in_dim(q, q0, MOBA_QCHUNK, axis=2)
        blk = q0 // MOBA_BLOCK
        bscore = jnp.einsum('bhqd,bhnd->bhqn', qc.astype(jnp.float32), kbar)
        bscore = jnp.where(jnp.arange(nb) < blk, bscore, -jnp.inf)
        _, idx = lax.top_k(bscore, K)
        valid = jnp.arange(K) < blk
        kg = kb[bi, hi, idx]
        vg = vb[bi, hi, idx]
        s_sel = jnp.einsum('bhqd,bhqkld->bhqkl', qc, kg).astype(jnp.float32) * scale
        s_sel = jnp.where(valid[:, None], s_sel, -jnp.inf)
        k_own = lax.dynamic_index_in_dim(kb, blk, axis=2, keepdims=False)
        v_own = lax.dynamic_index_in_dim(vb, blk, axis=2, keepdims=False)
        s_own = jnp.einsum('bhqd,bhld->bhql', qc, k_own).astype(jnp.float32) * scale
        qpos = q0 + jnp.arange(MOBA_QCHUNK)
        kpos = blk * MOBA_BLOCK + jnp.arange(MOBA_BLOCK)
        s_own = jnp.where(kpos[None, :] <= qpos[:, None], s_own, -jnp.inf)
        logits = jnp.concatenate([s_sel.reshape(B, H, MOBA_QCHUNK, K * MOBA_BLOCK), s_own], axis=-1)
        p = jax.nn.softmax(logits, axis=-1).astype(v.dtype)
        p_sel = p[..., :K * MOBA_BLOCK].reshape(B, H, MOBA_QCHUNK, K, MOBA_BLOCK)
        p_own = p[..., K * MOBA_BLOCK:]
        return (jnp.einsum('bhqkl,bhqkld->bhqd', p_sel, vg)
                + jnp.einsum('bhql,bhld->bhqd', p_own, v_own))

    out = lax.map(one_chunk, jnp.arange(nq))
    out = jnp.moveaxis(out, 0, 2).reshape(B, H, Sp, hd)
    return out[:, :, :S]

def peer_ffn(xn, w_query, subkeys, u_tab, v_tab):
    B, S, D = xn.shape
    T = B * S
    xt = xn.reshape(T, D)
    q = (xt @ w_query).reshape(T, PEER_HEADS, 2, PEER_QDIM // 2)
    s = jnp.einsum('thpd,hpkd->thpk', q, subkeys).astype(jnp.float32)
    sv, si = lax.top_k(s, PEER_TOPK)
    cand = (sv[:, :, 0, :, None] + sv[:, :, 1, None, :]).reshape(T, PEER_HEADS, PEER_TOPK * PEER_TOPK)
    cand_id = (si[:, :, 0, :, None] * PEER_NKEYS + si[:, :, 1, None, :]).reshape(T, PEER_HEADS, PEER_TOPK * PEER_TOPK)
    top_s, pos = lax.top_k(cand, PEER_TOPK)
    expert = jnp.take_along_axis(cand_id, pos, axis=-1)
    gate = jax.nn.softmax(top_s, axis=-1)
    nchunk = T // PEER_TOKCHUNK

    def apply(args):
        xc, ec, gc = args
        ug = u_tab[ec]
        vg = v_tab[ec]
        act = jax.nn.gelu(jnp.einsum('thkd,td->thk', ug, xc).astype(jnp.float32), approximate=False)
        w = (gc * act).astype(vg.dtype)
        return jnp.einsum('thk,thkd->td', w, vg)

    out = lax.map(apply, (xt.reshape(nchunk, PEER_TOKCHUNK, D),
                          expert.reshape(nchunk, PEER_TOKCHUNK, PEER_HEADS, PEER_TOPK),
                          gate.reshape(nchunk, PEER_TOKCHUNK, PEER_HEADS, PEER_TOPK)))
    return out.reshape(B, S, D)

def first_inputs(seed: int = 0) -> dict:
    key = jax.random.key(seed)
    ks = jax.random.split(key, 15)
    L, D = DEPTH, D_MODEL
    nrm = jax.random.normal
    return {
        "x": nrm(ks[0], (BATCH, SEQ, D), jnp.float32),
        "norm1_w": 1.0 + 0.02 * nrm(ks[1], (L, D), jnp.float32),
        "w_in": nrm(ks[2], (L, D, IN_WIDTH), jnp.float32) * D ** -0.5,
        "gla_w_alpha": nrm(ks[3], (L, GLA_RANK, GLA_HEADS * GLA_DK), jnp.float32) * GLA_RANK ** -0.5,
        "gla_b_alpha": 0.1 * nrm(ks[4], (L, GLA_HEADS * GLA_DK), jnp.float32),
        "gla_out_norm_w": 1.0 + 0.02 * nrm(ks[5], (L, GLA_DV), jnp.float32),
        "moba_q_norm_w": 1.0 + 0.02 * nrm(ks[6], (L, MOBA_HD), jnp.float32),
        "moba_k_norm_w": 1.0 + 0.02 * nrm(ks[7], (L, MOBA_HD), jnp.float32),
        "mix_scale": 1.0 + 0.02 * nrm(ks[8], (L, MIX_WIDTH), jnp.float32),
        "w_out": nrm(ks[9], (L, MIX_WIDTH, D), jnp.float32) * MIX_WIDTH ** -0.5,
        "norm2_w": 1.0 + 0.02 * nrm(ks[10], (L, D), jnp.float32),
        "peer_w_query": nrm(ks[11], (L, D, PEER_HEADS * PEER_QDIM), jnp.float32) * D ** -0.5,
        "peer_subkeys": nrm(ks[12], (L, PEER_HEADS, 2, PEER_NKEYS, PEER_QDIM // 2), jnp.float32) * (PEER_QDIM // 2) ** -0.5,
        "peer_u": nrm(ks[13], (L, PEER_N, D), jnp.float32) * D ** -0.5,
        "peer_v": nrm(ks[14], (L, PEER_N, D), jnp.float32) * (PEER_HEADS * PEER_TOPK) ** -0.5,
    }

def first_block(x, norm1_w, w_in, gla_w_alpha, gla_b_alpha, gla_out_norm_w, moba_q_norm_w,
              moba_k_norm_w, mix_scale, w_out, norm2_w, peer_w_query, peer_subkeys, peer_u, peer_v):
    B, S, _ = x.shape
    pos = jnp.arange(S)
    offsets = []
    acc = 0
    for w in IN_SPLITS[:-1]:
        acc += w
        offsets.append(acc)
    for l in range(DEPTH):
        xn = rmsnorm(x, norm1_w[l])
        proj = xn @ w_in[l]
        gq, gk, gv, ggate, gr, mq, mk, mv = jnp.split(proj, offsets, axis=-1)
        log_a = jax.nn.log_sigmoid((gr @ gla_w_alpha[l] + gla_b_alpha[l]).astype(jnp.float32)) / GLA_TAU
        o_gla = gla_chunked(to_heads(gq, GLA_HEADS).astype(jnp.float32),
                            to_heads(gk, GLA_HEADS).astype(jnp.float32),
                            to_heads(gv, GLA_HEADS).astype(jnp.float32),
                            to_heads(log_a, GLA_HEADS))
        o_gla = from_heads(rmsnorm(o_gla, gla_out_norm_w[l])).astype(x.dtype)
        o_gla = o_gla * jax.nn.silu(ggate)
        qh = rope(rmsnorm(to_heads(mq, MOBA_HEADS), moba_q_norm_w[l]), pos)
        kh = rope(rmsnorm(to_heads(mk, MOBA_HEADS), moba_k_norm_w[l]), pos)
        o_moba = from_heads(moba_attention(qh, kh, to_heads(mv, MOBA_HEADS)))
        mixed = jnp.concatenate([o_gla, o_moba], axis=-1) * mix_scale[l]
        x = x + mixed @ w_out[l]
        x = x + peer_ffn(rmsnorm(x, norm2_w[l]), peer_w_query[l], peer_subkeys[l], peer_u[l], peer_v[l])
    return x


DEPTH_2 = 2

PLE_DIM = 256
BLOCK = 128
SB_HEADS = 8
SB_DIM = 64
SB_WIDTH = SB_HEADS * SB_DIM
HG_HEADS = 4
HG_DK = 128
HG_DV = 128
HG_QK = HG_HEADS * HG_DK
HG_V = HG_HEADS * HG_DV
HG_CHUNK = 64
AB_SPLITS = [SB_WIDTH] * 3 + [HG_QK] * 2 + [HG_V] * 2
AB_IN = sum(AB_SPLITS)
AB_OUT = SB_WIDTH + HG_V
SW_HEADS = 16
SW_KV_HEADS = 4
SW_DIM = 64
SW_GROUP = SW_HEADS // SW_KV_HEADS
WINDOW = 128
C_IN = (SW_HEADS + 2 * SW_KV_HEADS) * SW_DIM
C_OUT = SW_HEADS * SW_DIM
N_BUCKETS = 32
MAX_DISTANCE = 128
D_FF = 2816
CONV_W = 3
N_EVEN = (DEPTH_2 + 1) // 2
N_ODD = DEPTH_2 // 2


def rmsnorm_2(x, g):
    xf = x.astype(jnp.float32)
    y = xf * lax.rsqrt(jnp.mean(xf * xf, axis=-1, keepdims=True) + EPS)
    return (y * g.astype(jnp.float32)).astype(x.dtype)

def stick_breaking_attention(q, k, v):
    S = q.shape[1]
    qf = jnp.swapaxes(q, 1, 2).astype(jnp.float32)
    kf = jnp.swapaxes(k, 1, 2).astype(jnp.float32)
    vf = jnp.swapaxes(v, 1, 2).astype(jnp.float32)
    scale = SB_DIM ** -0.5
    outs = []
    for n in range(S // BLOCK):
        t0 = n * BLOCK
        kn = t0 + BLOCK
        z = jnp.einsum('bhtd,bhsd->bhts', qf[:, :, t0:kn], kf[:, :, :kn]) * scale
        t_pos = t0 + jnp.arange(BLOCK)[:, None]
        s_pos = jnp.arange(kn)[None, :]
        mask = s_pos < t_pos
        log_keep = jnp.where(mask, jax.nn.log_sigmoid(-z), 0.0)
        later = lax.cumsum(log_keep, axis=3, reverse=True) - log_keep
        w = jnp.where(mask, jnp.exp(jax.nn.log_sigmoid(z) + later), 0.0)
        outs.append(jnp.einsum('bhts,bhsd->bhtd', w, vf[:, :, :kn]))
    o = jnp.concatenate(outs, axis=2)
    return jnp.swapaxes(o, 1, 2)

def hgrn2(q, f_pre, i, lb):
    B, S = q.shape[:2]
    lb = lb.reshape(HG_HEADS, HG_DK).astype(jnp.float32)
    fp = f_pre.astype(jnp.float32)
    log_f = jnp.log(lb + (1.0 - lb) * jax.nn.sigmoid(fp))
    kk = (1.0 - lb) * jax.nn.sigmoid(-fp)
    qf = jax.nn.silu(q.astype(jnp.float32))
    nc = S // HG_CHUNK

    def to_chunks(a):
        return a.reshape(B, nc, HG_CHUNK, HG_HEADS, a.shape[-1]).transpose(1, 0, 3, 2, 4)

    causal = jnp.tril(jnp.ones((HG_CHUNK, HG_CHUNK), dtype=bool))

    def step(state, xs):
        qc, kc, lfc, ic = xs
        b = jnp.cumsum(lfc, axis=2)
        o_inter = jnp.einsum('bhtk,bhkv->bhtv', qc * jnp.exp(b), state)
        rel = jnp.where(causal[:, :, None], b[:, :, :, None, :] - b[:, :, None, :, :], -jnp.inf)
        scores = jnp.einsum('bhtk,bhsk,bhtsk->bhts', qc, kc, jnp.exp(rel))
        o = o_inter + jnp.einsum('bhts,bhsv->bhtv', scores, ic)
        b_last = b[:, :, -1:, :]
        state = jnp.exp(b_last[:, :, 0, :, None]) * state + jnp.einsum('bhsk,bhsv->bhkv', kc * jnp.exp(b_last - b), ic)
        return state, o

    s0 = jnp.zeros((B, HG_HEADS, HG_DK, HG_DV), jnp.float32)
    _, o = lax.scan(step, s0, (to_chunks(qf), to_chunks(kk), to_chunks(log_f), to_chunks(i.astype(jnp.float32))))
    return o.transpose(1, 0, 3, 2, 4).reshape(B, S, HG_HEADS, HG_DV)

def t5_band_buckets():
    t = np.arange(WINDOW)[:, None]
    s = np.arange(2 * WINDOW)[None, :]
    dist = t + WINDOW - s
    band = (dist >= 0) & (dist < WINDOW)
    max_exact = N_BUCKETS // 2
    large = max_exact + (np.log(np.maximum(dist, max_exact) / max_exact) / math.log(MAX_DISTANCE / max_exact) * (N_BUCKETS - max_exact)).astype(np.int32)
    large = np.minimum(large, N_BUCKETS - 1)
    bucket = np.where(dist < max_exact, np.maximum(dist, 0), large).astype(np.int32)
    return bucket, band

def sliding_window_attention(q, k, v, sinks, rel_bias):
    B, S = q.shape[:2]
    nb = S // WINDOW
    bucket, band = t5_band_buckets()
    bias = rel_bias.astype(jnp.float32)[bucket]
    bias = bias.transpose(2, 0, 1).reshape(SW_KV_HEADS, SW_GROUP, WINDOW, 2 * WINDOW)
    key_pos = np.arange(nb)[:, None] * WINDOW - WINDOW + np.arange(2 * WINDOW)[None, :]
    mask = jnp.asarray(band[None] & (key_pos >= 0)[:, None, :])
    qb = q.astype(jnp.float32).reshape(B, nb, WINDOW, SW_KV_HEADS, SW_GROUP, SW_DIM).transpose(1, 0, 2, 3, 4, 5)

    def band_keys(a):
        ap = jnp.pad(a.astype(jnp.float32), ((0, 0), (WINDOW, 0), (0, 0), (0, 0)))
        ap = ap.reshape(B, nb + 1, WINDOW, SW_KV_HEADS, SW_DIM)
        return jnp.concatenate([ap[:, :-1], ap[:, 1:]], axis=2).transpose(1, 0, 2, 3, 4)

    kb, vb = band_keys(k), band_keys(v)
    sink = sinks.astype(jnp.float32).reshape(SW_KV_HEADS, SW_GROUP, 1, 1)
    scale = SW_DIM ** -0.5

    def block_attn(args):
        qn, kn, vn, mn = args
        logits = jnp.einsum('bqhgd,bkhd->bhgqk', qn, kn) * scale + bias
        logits = jnp.where(mn, logits, -jnp.inf)
        m = jnp.maximum(jnp.max(logits, axis=-1, keepdims=True), sink)
        e = jnp.exp(logits - m)
        w = e / (jnp.sum(e, axis=-1, keepdims=True) + jnp.exp(sink - m))
        return jnp.einsum('bhgqk,bkhd->bqhgd', w, vn)

    o = lax.map(block_attn, (qb, kb, vb, mask))
    return o.transpose(1, 0, 2, 3, 4, 5).reshape(B, S, SW_HEADS, SW_DIM)

def mixer_ab(h, w_in, lb, hg_norm, w_out):
    B, S, _ = h.shape
    proj = h @ w_in
    qa, ka, va, qb, fb, ib, gb = jnp.split(proj, np.cumsum(AB_SPLITS)[:-1].tolist(), axis=-1)
    sb_shape = (B, S, SB_HEADS, SB_DIM)
    o_a = stick_breaking_attention(qa.reshape(sb_shape), ka.reshape(sb_shape), va.reshape(sb_shape))
    o_a = o_a.astype(h.dtype).reshape(B, S, SB_WIDTH)
    o_b = hgrn2(qb.reshape(B, S, HG_HEADS, HG_DK), fb.reshape(B, S, HG_HEADS, HG_DK), ib.reshape(B, S, HG_HEADS, HG_DV), lb)
    o_b = rmsnorm_2(o_b.astype(h.dtype), hg_norm) * jax.nn.silu(gb.reshape(B, S, HG_HEADS, HG_DV))
    o_b = o_b.reshape(B, S, HG_V)
    return jnp.concatenate([o_a, o_b], axis=-1) @ w_out

def mixer_c(h, w_in, q_norm, k_norm, sinks, rel_bias, w_out):
    B, S, _ = h.shape
    proj = h @ w_in
    q, k, v = jnp.split(proj, [SW_HEADS * SW_DIM, (SW_HEADS + SW_KV_HEADS) * SW_DIM], axis=-1)
    q = rmsnorm_2(q.reshape(B, S, SW_HEADS, SW_DIM), q_norm)
    k = rmsnorm_2(k.reshape(B, S, SW_KV_HEADS, SW_DIM), k_norm)
    v = v.reshape(B, S, SW_KV_HEADS, SW_DIM)
    o = sliding_window_attention(q, k, v, sinks, rel_bias).astype(h.dtype)
    return o.reshape(B, S, C_OUT) @ w_out

def conv_glu_ffn(h, w_up, conv_w, conv_b, w_down):
    u = h @ w_up
    u = lax.conv_general_dilated(u, conv_w[:, None, :], window_strides=(1,), padding=[(CONV_W - 1, 0)],
                                 dimension_numbers=('NWC', 'WIO', 'NWC'), feature_group_count=2 * D_FF) + conv_b
    gate, up = jnp.split(u, 2, axis=-1)
    return (jax.nn.silu(gate) * up) @ w_down

def second_inputs(seed: int = 0) -> dict:
    key = jax.random.key(seed)
    ks = jax.random.split(key, 21)

    def nrm(k, shape):
        return jax.random.normal(k, shape, jnp.float32)

    def w(k, shape, fan_in):
        return nrm(k, shape) * fan_in ** -0.5

    def gain(k, shape):
        return 1.0 + 0.02 * nrm(k, shape)

    F2 = 2 * D_FF
    return {
        'x': nrm(ks[0], (BATCH, SEQ, D_MODEL)),
        'p': nrm(ks[1], (DEPTH_2, BATCH, SEQ, PLE_DIM)),
        'mix_norm': gain(ks[2], (DEPTH_2, D_MODEL)),
        'ab_w_in': w(ks[3], (N_EVEN, D_MODEL, AB_IN), D_MODEL),
        'hg_lb_logits': 0.5 * nrm(ks[4], (N_EVEN, HG_QK)),
        'hg_out_norm': gain(ks[5], (N_EVEN, HG_DV)),
        'ab_w_out': w(ks[6], (N_EVEN, AB_OUT, D_MODEL), AB_OUT),
        'c_w_in': w(ks[7], (N_ODD, D_MODEL, C_IN), D_MODEL),
        'q_norm': gain(ks[8], (N_ODD, SW_DIM)),
        'k_norm': gain(ks[9], (N_ODD, SW_DIM)),
        'sinks': 0.5 * nrm(ks[10], (N_ODD, SW_HEADS)),
        'rel_bias': 0.5 * nrm(ks[11], (N_BUCKETS, SW_HEADS)),
        'c_w_out': w(ks[12], (N_ODD, C_OUT, D_MODEL), C_OUT),
        'ffn_norm': gain(ks[13], (DEPTH_2, D_MODEL)),
        'ffn_up': w(ks[14], (DEPTH_2, D_MODEL, F2), D_MODEL),
        'ffn_conv': w(ks[15], (DEPTH_2, CONV_W, F2), CONV_W),
        'ffn_conv_b': 0.02 * nrm(ks[16], (DEPTH_2, F2)),
        'ffn_down': w(ks[17], (DEPTH_2, D_FF, D_MODEL), D_FF),
        'ple_norm': gain(ks[18], (DEPTH_2, D_MODEL)),
        'ple_gate': w(ks[19], (DEPTH_2, D_MODEL, D_MODEL), D_MODEL),
        'ple_proj': w(ks[20], (DEPTH_2, PLE_DIM, D_MODEL), PLE_DIM),
    }

def second_block(x, p, mix_norm, ab_w_in, hg_lb_logits, hg_out_norm, ab_w_out, c_w_in, q_norm, k_norm,
              sinks, rel_bias, c_w_out, ffn_norm, ffn_up, ffn_conv, ffn_conv_b, ffn_down,
              ple_norm, ple_gate, ple_proj):
    lb_cum = jnp.cumsum(jax.nn.softmax(hg_lb_logits.astype(jnp.float32), axis=0), axis=0)
    lower_bounds = lb_cum - lb_cum[0]
    h = x
    for i in range(DEPTH_2):
        j = i // 2
        hn = rmsnorm_2(h, mix_norm[i])
        if i % 2 == 0:
            h = h + mixer_ab(hn, ab_w_in[j], lower_bounds[j], hg_out_norm[j], ab_w_out[j])
        else:
            h = h + mixer_c(hn, c_w_in[j], q_norm[j], k_norm[j], sinks[j], rel_bias, c_w_out[j])
        h = h + conv_glu_ffn(rmsnorm_2(h, ffn_norm[i]), ffn_up[i], ffn_conv[i], ffn_conv_b[i], ffn_down[i])
        gate = jax.nn.sigmoid(rmsnorm_2(h, ple_norm[i]) @ ple_gate[i])
        h = h + gate * (p[i] @ ple_proj[i])
    return h


def setup_inputs(seed=0):
    out = dict(first_inputs(seed))
    for name, value in second_inputs(seed + 1).items():
        if name != "x":
            out[name + "_2"] = value
    return out


def reference(
    x, norm1_w, w_in, gla_w_alpha, gla_b_alpha, gla_out_norm_w, moba_q_norm_w, moba_k_norm_w,
    mix_scale, w_out, norm2_w, peer_w_query, peer_subkeys, peer_u, peer_v, p_2, mix_norm_2,
    ab_w_in_2, hg_lb_logits_2, hg_out_norm_2, ab_w_out_2, c_w_in_2, q_norm_2, k_norm_2, sinks_2,
    rel_bias_2, c_w_out_2, ffn_norm_2, ffn_up_2, ffn_conv_2, ffn_conv_b_2, ffn_down_2,
    ple_norm_2, ple_gate_2, ple_proj_2,
):
    x = first_block(
        x, norm1_w, w_in, gla_w_alpha, gla_b_alpha, gla_out_norm_w, moba_q_norm_w,
        moba_k_norm_w, mix_scale, w_out, norm2_w, peer_w_query, peer_subkeys, peer_u, peer_v,
    )
    return second_block(
        x, p_2, mix_norm_2, ab_w_in_2, hg_lb_logits_2, hg_out_norm_2, ab_w_out_2, c_w_in_2,
        q_norm_2, k_norm_2, sinks_2, rel_bias_2, c_w_out_2, ffn_norm_2, ffn_up_2, ffn_conv_2,
        ffn_conv_b_2, ffn_down_2, ple_norm_2, ple_gate_2, ple_proj_2,
    )


_drawn_inputs = setup_inputs


def setup_inputs(seed=0):
    import zlib

    import numpy as np

    out = dict(_drawn_inputs(seed))
    spreads = {}
    factors = {'gla_b_alpha': 2.838,
     'gla_out_norm_w': 4.944,
     'moba_q_norm_w': 8.0,
     'moba_k_norm_w': 8.0,
     'mix_scale': 5.554,
     'norm2_w': 25.589,
     'mix_norm_2': 3.925,
     'hg_out_norm_2': 7.07,
     'q_norm_2': 8.0,
     'k_norm_2': 8.0,
     'sinks_2': 64.0,
     'ffn_norm_2': 3.456,
     'ffn_conv_b_2': 3.612,
     'ple_norm_2': 64.0,
     'rel_bias_2': 4.992}
    for name, (base, spread) in spreads.items():
        noise = np.random.default_rng([zlib.crc32(name.encode()), seed]).standard_normal(out[name].shape)
        drawn = base * np.exp(spread * noise) if base else spread * noise
        out[name] = __import__('jax').numpy.asarray(drawn.astype(out[name].dtype))
    for name, factor in factors.items():
        out[name] = (out[name] * factor).astype(out[name].dtype)
    return out
```

```python
from contextlib import ExitStack

import numpy as np

import concourse.bass as bass
from concourse import mybir

F32 = mybir.dt.float32
U32 = mybir.dt.uint32
ALU = mybir.AluOpType
ACT = mybir.ActivationFunctionType
AX = mybir.AxisListType.X

P = 128
D = 1024
S = 256
TT = S // P
KC = D // P
EPS = 1e-6
NEG = -1e30
GH, GDK, GDV, GRANK, CH = 4, 64, 128, 16, 64
MH, HD = 8, 64
PH, NKEYS, TOPK = 8, 128, 16
UNITS = TT * PH
SWH, SWKV, WIN, NBUCK = 16, 4, 128, 32
DFF = 2816
FT = DFF // P
PLE = 256
LEVELS = [1, 2, 4, 8, 16, 32]
BANK = 512

PLAN = [("vecs", 1), ("conv", 1), ("relb", 1), ("norm0", 4), ("win", 12), ("gr", 1),
        ("alpha", 1), ("gla_cum", 2), ("gla_dec", 1), ("gla_T", 3), ("gla_A", 2), ("gla_U", 3), ("gla_O", 2),
        ("mb_T", 6), ("mb_L0", 2), ("mb_P0", 2), ("mb_O0", 1), ("mb_L1", 4), ("mb_P1", 4), ("mb_O1", 1),
        ("mix0", 4), ("wout", 4), ("norm1", 4), ("subk", 4), ("query", 8), ("score", 8), ("peer", 4),
        ("norm2", 4), ("ab", 14), ("sb_T", 6), ("sb_Z", 6), ("sb_C", 6), ("sb_O", 2),
        ("hg_B", 2), ("hg_suf", 2), ("hg_T", 4), ("hg_D", 2), ("hg_L", 2 * len(LEVELS)), ("hg_U", 3), ("hg_O", 2),
        ("mix1", 4), ("about", 4), ("norm3", 4), ("up0", FT), ("down0", 4), ("norm4", 4), ("pT0", 1), ("gate0", 4),
        ("proj0", 4),
        ("norm5", 4), ("c", 6), ("sw_T", 8)]
for _u in range(4):
    _n = 2 if _u < 2 else 4
    PLAN += [(f"sw_L{_u}", _n), (f"sw_P{_u}", _n), (f"sw_O{_u}", 1)]
PLAN += [("mix2", 4), ("cout", 4), ("norm6", 4), ("up1", FT), ("down1", 4), ("norm7", 4), ("pT1", 1), ("gate1", 4),
         ("proj1", 4)]
J, N = {}, {}
_at = 0
for _name, _n in PLAN:
    J[_name], N[_name] = _at, _n
    _at += _n

END = {k: J[k] + N[k] for k in J}


def shape_constants():
    i = np.arange(P)
    s, t = i[:, None], i[None, :]
    same = (s // CH) == (t // CH)
    cols, at = [], {}

    def put(name, a):
        at[name] = (sum(c.shape[1] for c in cols), a.shape[1])
        cols.append(a.astype(np.float32))

    put("ident", np.eye(P))
    put("cum", same & (s <= t))
    put("suf", same & (s > t))
    put("incl", s >= t)
    put("ones", np.ones((P, P)))
    put("before", s < t)
    put("before_add", np.where(s < t, 0.0, NEG))
    put("causal_add", np.concatenate([np.zeros((P, P)), np.where(t <= s, 0.0, NEG)], 1))
    half = HD // 2
    inv = (np.float32(10000.0) ** (-np.arange(half, dtype=np.float32) / np.float32(half))).astype(np.float32)
    pos = np.arange(S, dtype=np.float32).reshape(TT, P)
    ang = pos[:, :, None] * inv[None, None, :]
    put("cos", np.cos(ang).transpose(1, 0, 2).reshape(P, -1))
    put("sin", np.sin(ang).transpose(1, 0, 2).reshape(P, -1))
    put("head_rows", np.stack([(i // GDK) == (h % 2) for h in range(GH)], 1))
    put("chunk_rows", np.stack([(i // CH) == c for c in range(2)], 1))
    put("iota", np.tile(np.arange(TOPK), (P, 1)))
    small = np.concatenate(cols, 1)
    levels = []
    for half_block in LEVELS:
        b = 2 * half_block
        levels.append((s // b == t // b) & (s % b < half_block) & (t % b >= half_block))
    levels = np.concatenate(levels, 1).astype(np.float32)
    u = np.arange(3 * P)
    dist = 2 * WIN - 1 - u
    band = (dist >= 0) & (dist < WIN)
    exact = NBUCK // 2
    large = exact + (np.log(np.maximum(dist, exact) / exact) / np.log(WIN / exact) * (NBUCK - exact)).astype(np.int32)
    bucket = np.where(dist < exact, np.maximum(dist, 0), np.minimum(large, NBUCK - 1))
    onehot = ((np.arange(NBUCK)[:, None] == bucket[None, :]) & band[None, :]).astype(np.float32)
    outside = np.tile(np.where(band, 0.0, NEG), (SWH, 1)).astype(np.float32)
    return small, at, levels, onehot, outside


def build(nc, a, out, at):
    ctx = ExitStack()
    with ctx:
        sems = {}

        def sem(name):
            if name not in sems:
                sems[name] = ctx.enter_context(nc.semaphore(name))
            return sems[name]

        def sb(name, shape, dt=F32):
            return ctx.enter_context(nc.sbuf_tensor(name, shape, dt))

        SLOT = 4096
        W = sb("weights", [P, 7 * SLOT])
        X = sb("x_res", [P, TT, D])
        XN = sb("x_norm", [P, TT, D])
        XNT = sb("x_normT", [P, KC, S])
        PROJ = sb("proj", [P, 7168])
        A = sb("work_a", [P, 4096])
        B = sb("work_b", [P, 4096])
        C = sb("consts", [P, sum(n for _, n in at.values())])
        VEC = sb("vec_cols", [P, 72])
        CONV = sb("conv_cols", [P, 2, 4 * 2 * FT])
        GAIN = sb("gain_rows", [P, 2 * GDV + 4 * HD])
        ALB = sb("alpha_bias", [P, GH * GDK])
        SINK = sb("sink_rows", [P, SWH])
        SS = sb("stats", [P, 96])
        SCR = W[:, 6 * SLOT:7 * SLOT]
        PS = ctx.enter_context(nc.psum_tensor("ps", [P, 8, BANK], F32))

        def const(name):
            o, n = at[name]
            return C[:, o:o + n]

        ident, cum, suf, incl, ones = (const(n) for n in ("ident", "cum", "suf", "incl", "ones"))
        causal_add = const("causal_add")
        zeros = causal_add[:, 0:P]
        slot = [W[:, n * SLOT:(n + 1) * SLOT] for n in range(6)]
        wk = [s.rearrange("p (c n) -> p c n", c=KC) for s in slot]
        NORM_COL = {0: 0, 1: None, 2: 8, 3: 24, 4: 40, 5: 16, 6: 32, 7: 48}
        MIX_COL = {0: 56, 1: None, 2: None}
        LB_GAIN, HG_GAIN = GAIN[:, 0:GDV], GAIN[:, GDV:2 * GDV]
        QK_GAIN = [GAIN[:, 2 * GDV + n * HD:2 * GDV + (n + 1) * HD] for n in range(4)]

        proj_in = PROJ[:, 0:6144].rearrange("p (t n) -> p t n", t=TT)
        proj_ab = PROJ[:, 0:7168].rearrange("p (t n) -> p t n", t=TT)
        proj_c = PROJ[:, 0:3072].rearrange("p (t n) -> p t n", t=TT)
        BIAS = PROJ[:, 3072:7168].rearrange("p (h s) -> p h s", h=SWH)
        HT = PROJ[:, 0:FT * S].rearrange("p (c t) -> p c t", c=FT)
        flatT = XNT[:, :, :].rearrange("p c t -> p (c t)")
        KZ = flatT.rearrange("p (t v n) -> p t v n", t=TT, v=8)
        KZT = B[:, 0:2048].rearrange("p (v t) -> p v t", v=8)
        QT = B[:, 2048:4096].rearrange("p (v t) -> p v t", v=8)
        PB = A[:, 0:2048]
        PT = A[:, 2048:4096].rearrange("p (b t) -> p b t", t=P)
        ST = SCR[:, 0:1536].rearrange("p (c h v) -> p c h v", c=3, h=4)
        KSC = SCR[:, 1536:3072].rearrange("p (c n) -> p c n", c=3)
        LEV = SCR[:, 3328:4096].rearrange("p (l t) -> p l t", l=6)
        DEC = SS[:, 40:56]
        UTW = B[:, 0:16]
        W_GR = B[:, 3072:3072 + KC * GRANK].rearrange("p (c n) -> p c n", c=KC)
        W_ALPHA = B[0:GRANK, 3328:3584]
        GRT = B[0:GRANK, 3584:3840]
        gG, gE, gB_, gS = (A[:, n * 512:(n + 1) * 512] for n in range(4))
        gKZ = flatT[:, 0:1024].rearrange("p (t h n) -> p t h n", t=TT, h=4)
        gKST = flatT[:, 1024:1536].rearrange("p (t n) -> p t n", t=TT)
        gKZT = B[:, 0:1024].rearrange("p (h t) -> p h t", h=4)
        gQT = B[:, 1024:1536].rearrange("p (j t) -> p j t", j=2)
        AT = B[:, 2048:3072].rearrange("p (t h n) -> p t h n", t=TT, h=4)
        gDECR = A[:, 2560:2568]
        OUTN = A[:, 0:1024].rearrange("p (t n) -> p t n", t=TT)
        SQ = A[:, 1024:2048].rearrange("p (t n) -> p t n", t=TT)
        OH = B[0:NBUCK, 0:384]
        RB = B[0:NBUCK, 384:400]
        OUTSIDE = B[0:SWH, 400:784]
        BROW = B[0:SWH, 784:1168]
        VROW = B[0:72, 1200:1328]
        CROW = [B[0:2 * 2 * FT, 1328 + P * n:1328 + P * (n + 1)] for n in range(4)]
        qT = A[:, :].rearrange("p (u t) -> p u t", u=16)
        SKN = B[:, 2048:4096].rearrange("p (u n) -> p u n", u=16)
        SKT = B[:, 0:2048].rearrange("p (u n) -> p u n", u=16)
        SCORE = PROJ[:, 0:4096]
        N2W = PROJ[:, 4096:5120]
        DIAG = PROJ[:, 5120:6144].rearrange("p (q k n) -> p q k n", q=2, k=4)
        R = PROJ[:, 6144:7168]
        r_s = R[:, 0:256].rearrange("p (q n) -> p q n", q=2)
        r_w = R[:, 256:512]
        r_cand = R[:, 512:768]
        r_sv = R[:, 768:800].rearrange("p (q n) -> p q n", q=2)
        r_top = R[:, 800:816]
        r_sum = R[:, 816:817]
        r_rs = R[:, 817:818]
        r_e = R[:, 820:836]
        r_gate = R[:, 836:868].rearrange("p (q n) -> p q n", q=2)
        r_dot = R[:, 868:876].rearrange("p (q n) -> p q n", q=2)
        r_act = R[:, 876:884].rearrange("p (q n) -> p q n", q=2)
        r_wt = R[:, 884:892].rearrange("p (q n) -> p q n", q=2)
        r_i = R[:, 892:924].rearrange("p (q n) -> p q n", q=2)
        RI = sb("route_idx", [P, 96], U32)
        r_si = RI[:, 0:32].rearrange("p (q n) -> p q n", q=2)
        r_pos = RI[:, 32:48]
        r_hi, r_lo = RI[:, 48:56], RI[:, 56:64]
        r_ab = sb("route_ab", [P, 32], U32)
        r_idx = RI[:, 64:96].rearrange("p (q n) -> p q n", q=2)
        NU, NV = 8, 16
        ubuf = [W[:, n * D:(n + 1) * D] for n in range(NU)]
        vbuf = [W[:, (NU + n) * D:(NU + n + 1) * D] for n in range(NV)]
        Z0 = A[:, 0:2048].rearrange("p (h t) -> p h t", h=8)
        Z1 = A[:, 2048:3072].rearrange("p (h t) -> p h t", h=8)
        L0 = B[:, 0:2048].rearrange("p (h t) -> p h t", h=8)
        L1 = B[:, 2048:3072].rearrange("p (h t) -> p h t", h=8)
        hBT, hQT, hKT, hE0 = (A[:, n * 1024:(n + 1) * 1024] for n in range(4))
        hE1, hT0 = B[:, 0:1024], B[:, 1024:2048]
        hKK = B[:, 3072:4096].rearrange("p (t n) -> p t n", t=TT)
        hKST = XNT[:, 0:4, :].rearrange("p c t -> p (c t)").rearrange("p (t n) -> p t n", t=TT)
        hSF = XNT[:, 4:8, :].rearrange("p c t -> p (c t)").rearrange("p (t n) -> p t n", t=TT)
        UP = [SCR[:, n * 2048:(n + 1) * 2048].rearrange("p (c g n) -> p c g n", c=KC, g=2) for n in range(2)]
        WD = W[:, 0:FT * D].rearrange("p (c n) -> p c n", c=FT)
        CT = A[:, 0:1024].rearrange("p (q n) -> p q n", q=2)
        GATE = A[:, 2048:4096].rearrange("p (t n) -> p t n", t=TT)
        PIN = B[:, 0:1024].rearrange("p (l t n) -> p l t n", l=2, t=TT)
        PINT = B[:, 1024:1536].rearrange("p (c t) -> p c t", c=2)
        PTMP = B[:, 2048:2560]

        PER = 3 * P - 1
        bias_scratch = nc.dram_tensor("bias_scratch", (SWH, P * PER), F32, kind="Internal").ap()

        pe_done, evac_done = sem("pe_done"), sem("evac_done")
        w_loaded = [sem(f"w_loaded{n}") for n in range(6)]
        up_loaded = [sem(f"up_loaded{n}") for n in range(2)]
        u_loaded = [sem(f"u_loaded{n}") for n in range(NU)]
        v_loaded = [sem(f"v_loaded{n}") for n in range(NV)]

        def cols512(m, c0, n=512):
            return m[:, c0:c0 + n].rearrange("(c p) n -> p c n", p=P)

        w_in, ab_in, c_in = a["w_in"][0], a["ab_w_in_2"][0], a["c_w_in_2"][0]
        ple_gate, ple_proj = a["ple_gate_2"], a["ple_proj_2"]
        up_w, down_w = a["ffn_up_2"], a["ffn_down_2"]
        in_cols = [0, 512, 1024, 1552, 2064, 2576]
        CHUNKS = []
        CHUNKS += [("win", n, n, cols512(w_in, c)) for n, c in enumerate(in_cols)]
        CHUNKS += [("wout", n, n, cols512(a["w_out"][0], 512 * n)) for n in range(2)]
        CHUNKS += [("query", n, 2 + n, cols512(a["peer_w_query"][0], 512 * n)) for n in range(4)]
        CHUNKS += [("ab", n, n % 6, cols512(ab_in, 512 * n)) for n in range(7)]
        CHUNKS += [("about", n, 1 + n, cols512(a["ab_w_out_2"][0], 512 * n)) for n in range(2)]
        CHUNKS += [("gate0", n, n, cols512(ple_gate[0], 512 * n)) for n in range(2)]
        CHUNKS += [("proj0", 0, 2, ple_proj[0].rearrange("(c p) n -> p c n", p=P))]
        CHUNKS += [("c", n, 3 + n, cols512(c_in, 512 * n)) for n in range(3)]
        CHUNKS += [("cout", n, n, cols512(a["c_w_out_2"][0], 512 * n)) for n in range(2)]
        CHUNKS += [("gate1", n, n, cols512(ple_gate[1], 512 * n)) for n in range(2)]
        CHUNKS += [("proj1", 0, 2, ple_proj[1].rearrange("(c p) n -> p c n", p=P))]
        LOAD_NO, SLOT_OF = {}, {}
        _cnt = [0] * 6
        for name, n, s, _ in CHUNKS:
            _cnt[s] += 1
            LOAD_NO[name, n], SLOT_OF[name, n] = 16 * _cnt[s], s

        block = ctx.enter_context(nc.Block())

        @block.sync
        def _(sp):
            def chunk(name, n, after=None):
                if after is not None:
                    sp.wait_ge(pe_done, after)
                s = SLOT_OF[name, n]
                src = [c for c in CHUNKS if c[0] == name and c[1] == n][0][3]
                dst = slot[s][:, 0:src.shape[1] * src.shape[2]].rearrange("p (c n) -> p c n", c=src.shape[1])
                sp.dma_start(dst, src).then_inc(w_loaded[s], 16)

            sp.dma_start(X[:, :, :], a["x"][0].rearrange("(t p) d -> p t d", p=P)).then_inc(sem("x_loaded"), 16)
            sp.dma_start(C[:, :], a["c_small"]).then_inc(sem("const_loaded"), 16)
            rows = [("norm1_w", 8), ("mix_norm_2", 16), ("ffn_norm_2", 16), ("ple_norm_2", 16), ("mix_scale", 8)]
            r = 0
            for name, n in rows:
                sp.dma_start(VROW[r:r + n, :], a[name].rearrange("l (c p) -> (l c) p", p=P)).then_inc(sem("vec_loaded"), 16)
                r += n
            chunk("win", 0)
            for l in range(2):
                taps = a["ffn_conv_2"][l].rearrange("k (c p) -> (k c) p", p=P)
                sp.dma_start(CROW[2 * l][:, :], taps[0:4 * FT, :]).then_inc(sem("conv_loaded"), 16)
                sp.dma_start(CROW[2 * l + 1][0:2 * FT, :], taps[4 * FT:6 * FT, :]).then_inc(sem("conv_loaded"), 16)
                sp.dma_start(CROW[2 * l + 1][2 * FT:4 * FT, :],
                             a["ffn_conv_b_2"][l:l + 1, :].rearrange("k (c p) -> (k c) p", p=P)).then_inc(sem("conv_loaded"), 16)
            sp.dma_start(OH, a["c_onehot"]).then_inc(sem("rel_loaded"), 16)
            sp.dma_start(RB, a["rel_bias_2"]).then_inc(sem("rel_loaded"), 16)
            sp.dma_start(OUTSIDE, a["c_outside"]).then_inc(sem("rel_loaded"), 16)
            chunk("win", 1)
            sp.dma_start(W_GR, cols512(w_in, 1536, GRANK)).then_inc(sem("gr_loaded"), 16)
            sp.dma_start(W_ALPHA, a["gla_w_alpha"][0]).then_inc(sem("gr_loaded"), 16)
            for dst, src in ((LB_GAIN, a["gla_out_norm_w"]), (HG_GAIN, a["hg_out_norm_2"]), (QK_GAIN[0], a["moba_q_norm_w"]),
                             (QK_GAIN[1], a["moba_k_norm_w"]), (QK_GAIN[2], a["q_norm_2"]), (QK_GAIN[3], a["k_norm_2"]),
                             (ALB[:, :], a["gla_b_alpha"]), (SINK[:, :], a["sinks_2"])):
                sp.dma_start(dst, src[0].partition_broadcast(P)).then_inc(sem("gain_loaded"), 16)
            sp.dma_start(SCR[:, 3328:4096], a["c_levels"]).then_inc(sem("levels_loaded"), 16)
            for n in range(2, 6):
                chunk("win", n)
            sp.wait_ge(sem("bias_row"), 1)
            sp.dma_start(bias_scratch.rearrange("h (t u) -> h t u", u=PER),
                         BROW[:, 0:PER].unsqueeze(1).broadcast_to([SWH, P, PER])).then_inc(sem("bias_written"), 16)
            for n in range(2):
                chunk("wout", n, after=J["win"] + 2 * (n + 1))
            for n in range(4):
                chunk("query", n, after=J["win"] + 2 * (n + 3))
            sp.wait_ge(evac_done, END["mb_O1"])
            sp.dma_start(N2W, a["norm2_w"][0].partition_broadcast(P)).then_inc(sem("n2w_loaded"), 16)
            sp.dma_start(SKN, a["peer_subkeys"][0].rearrange("h q k d -> k (h q) d")).then_inc(sem("subkeys_loaded"), 16)
            sp.wait_ge(sem("dots_done"), 4 * UNITS)
            for n in range(6):
                chunk("ab", n, after=END["peer"])
            chunk("ab", 6, after=J["ab"] + 2)
            for n in range(2):
                chunk("about", n, after=J["ab"] + 2 * (n + 2))

            def ffn_loads(l, ready):
                def up_pair(i, first=False):
                    for q in range(2):
                        if not first:
                            sp.wait_ge(pe_done, i * 2 + (J[f"up{l}"] + q - 1))
                        src = up_w[l].rearrange("(c p) (g n) -> p c g n", p=P, g=2)
                        for g in range(2):
                            sp.dma_start(UP[q][:, :, g, :], src[:, :, g, bass.ds(i * (2 * P) + q * P, P)]).then_inc(up_loaded[q], 16)

                def down_pair(i):
                    sp.dma_start(W[:, bass.ds(i * 2048, 2048)].rearrange("p (c n) -> p c n", c=2),
                                 down_w[l, bass.ds(i * (2 * P), 2 * P), :].rearrange("(c p) n -> p c n", p=P)
                                 ).then_inc(sem("down_loaded"), 16)

                sp.wait_ge(evac_done, ready)
                up_pair(0, first=True)
                sp.wait_ge(pe_done, END["about" if l == 0 else "cout"])
                down_pair(0)
                with sp.Fori(1, FT // 2) as i:
                    up_pair(i)
                    down_pair(i)

            def ple_loads(l):
                for n in range(2):
                    sp.wait_ge(sem("down_rows"), 3 * l + n + 1)
                    chunk(f"gate{l}", n)
                sp.wait_ge(sem("down_rows"), 3 * l + 3)
                chunk(f"proj{l}", 0)

            ffn_loads(0, END["hg_O"])
            sp.dma_start(PIN[:, 0], a["p_2"][0, 0].rearrange("(t p) n -> p t n", p=P)).then_inc(sem("p_loaded"), 16)
            ple_loads(0)
            for n in range(3):
                chunk("c", n, after=END["down0"])
            sp.wait_ge(sem("bias_written"), 16)
            sp.dma_start(BIAS, bass.AP(bias_scratch.tensor, P - 1, [[PER - 1, P], [P * PER, SWH], [1, 2 * P]])
                         ).then_inc(sem("bias_loaded"), 16)
            for n in range(2):
                chunk("cout", n, after=J["gate0"] + 2 * (n + 1))
            ffn_loads(1, END["up0"])
            sp.dma_start(PIN[:, 1], a["p_2"][1, 0].rearrange("(t p) n -> p t n", p=P)).then_inc(sem("p_loaded"), 16)
            ple_loads(1)
            for t in range(TT):
                sp.wait_ge(sem("x_final"), t + 1)
                sp.dma_start(out[0, t * P:(t + 1) * P, :], X[:, t, :]).then_inc(sem("out_written"), 16)
            sp.wait_ge(sem("out_written"), 16 * TT)

        @block.gpsimd
        def _(pool):
            pool.wait_ge(pe_done, END["query"])

            def unit(u, q, first=False):
                def hold(s, value):
                    pool.wait_ge(sem(s), value)
                    if not isinstance(value, int):
                        pool.sem_inc(sem("gather_holds"))

                hold("idx_ready", u + 1)
                for b in range(4):
                    if not (first and b < 2):
                        hold("dots_done", u * 4 + (b - 1))
                    for k in range(4):
                        n = (4 * b + k) % NU
                        nc.gpsimd.indirect_dma_start(
                            out=ubuf[n], out_offset=None, in_=a["peer_u"][0],
                            in_offset=bass.IndirectOffsetOnAxis(ap=r_idx[:, q, 4 * b + k:4 * b + k + 1], axis=0)
                        ).then_inc(u_loaded[n], 16)
                    if not first:
                        hold("rows_summed", u * 4 + (b - 3))
                    for k in range(4):
                        n = 4 * b + k
                        nc.gpsimd.indirect_dma_start(
                            out=vbuf[n], out_offset=None, in_=a["peer_v"][0],
                            in_offset=bass.IndirectOffsetOnAxis(ap=r_idx[:, q, n:n + 1], axis=0)
                        ).then_inc(v_loaded[n], 16)

            unit(0, 0, first=True)
            unit(1, 1)
            with pool.Fori(1, UNITS // 2) as i:
                unit(i * 2, 0)
                unit(i * 2 + 1, 1)

            for l in range(2):
                with pool.Fori(0, FT // 2) as i:
                    for q in range(2):
                        pool.wait_ge(sem("silu_done"), i * 2 + (FT * l + q + 1))
                        nc.gpsimd.tensor_tensor(PROJ[:, bass.ds(i * (2 * S) + q * S, S)], CT[:, q, 0:S], CT[:, q, S:2 * S],
                                                ALU.mult).then_inc(sem("hidden_ready"), 1)

        @block.scalar
        def _(act):
            own = [0]

            def link(ins):
                own[0] += 1
                ins.then_inc(sem("act_chain"), 1)
                act.wait_ge(sem("act_chain"), own[0])

            root_no, rstd = [0], sem("root_done")

            def root(dst, src, n):
                root_no[0] += 1
                act.wait_ge(sem("sumsq_ready"), root_no[0])
                nc.scalar.activation(dst, src, ACT.Sqrt, bias=eps_col, scale=1.0 / n).then_inc(rstd, 1)

            eps_col = SS[:, 95:96]
            act.wait_ge(sem("eps_ready"), 1)
            root(SS[:, 2:4], SS[:, 0:2], D)

            act.wait_ge(sem("g_abs"), 1)
            link(nc.scalar.activation(gE, gE, ACT.Exp, scale=-1.0))
            nc.scalar.activation(gE, gE, ACT.Ln, bias=1.0).then_inc(sem("g_log"), 1)
            act.wait_ge(sem("g_cum"), 1)
            nc.scalar.activation(gE, gB_, ACT.Exp).then_inc(sem("g_exp"), 1)
            nc.scalar.activation(gB_, gB_, ACT.Exp, scale=-1.0).then_inc(sem("g_exp"), 1)
            nc.scalar.activation(gS, gS, ACT.Exp).then_inc(sem("g_exp"), 1)
            act.wait_ge(sem("g_cum"), 2)
            nc.scalar.activation(DEC[:, 0:8], gDECR, ACT.Exp).then_inc(sem("g_exp"), 1)
            act.wait_ge(evac_done, END["win"])
            nc.scalar.activation(proj_in[:, :, 1024:1536], proj_in[:, :, 1024:1536], ACT.Silu).then_inc(sem("silu_gate"), 1)
            root(SS[:, 16:24], SS[:, 8:16], GDV)
            root(SS[:, 56:88], SS[:, 8:40], HD)

            att_no = [0]

            def exp_unit(cols, sink=False):
                att_no[0] += 1
                act.wait_ge(sem("att_sub"), att_no[0])
                nc.scalar.activation(PB[:, 0:cols], PB[:, 0:cols], ACT.Exp).then_inc(sem("att_exp"), 1)
                if sink:
                    nc.scalar.activation(SS[:, 16:24], SS[:, 16:24], ACT.Exp).then_inc(sem("sink_exp"), 1)

            exp_unit(1024)
            exp_unit(2048)
            root(SS[:, 2:4], SS[:, 0:2], D)

            def gate_exp(u):
                act.wait_ge(sem("top_ready"), u + 1)
                nc.scalar.activation(r_e, r_e, ACT.Exp).then_inc(sem("gate_exp"), 1)

            def gelu(u, b):
                act.wait_ge(sem("dots_done"), u * 4 + (b + 1))
                nc.scalar.activation(r_act[:, b % 2], r_dot[:, b % 2], ACT.Gelu).then_inc(sem("gelu_done"), 1)

            def diag(u, b, wait=True):
                act.wait_ge(sem("weights_ready"), u * 4 + (b + 1))
                if wait:
                    act.wait_ge(sem("rows_summed"), u * 4 + (b - 1))
                for k in range(4):
                    ins = nc.scalar.activation(DIAG[:, b % 2, k, :], ident, ACT.Copy, scale=r_wt[:, b % 2, k:k + 1])
                ins.then_inc(sem("diag_ready"), 1)

            def act_unit(u, first=False, last=False):
                for b in range(4):
                    gelu(u, b)
                    if b > 0:
                        diag(u, b - 1, wait=not (first and b <= 2))
                    elif not first:
                        diag(u - 1, 3)
                    if b == 1 and not last:
                        gate_exp(u + 1)

            gate_exp(0)
            act_unit(0, first=True)
            act_unit(1)
            with act.Fori(1, UNITS // 2 - 1) as i:
                act_unit(i * 2)
                act_unit(i * 2 + 1)
            act_unit(UNITS - 2)
            act_unit(UNITS - 1, last=True)
            diag(UNITS - 1, 3)

            root(SS[:, 2:4], SS[:, 0:2], D)
            act.wait_ge(sem("sb_abs"), 1)
            for t in (L0, L1):
                link(nc.scalar.activation(t, t, ACT.Exp, scale=-1.0))
            nc.scalar.activation(L0, L0, ACT.Ln, bias=1.0).then_inc(sem("sb_log"), 1)
            nc.scalar.activation(L1, L1, ACT.Ln, bias=1.0).then_inc(sem("sb_log"), 1)
            act.wait_ge(sem("sb_arg"), 1)
            nc.scalar.activation(Z0, Z0, ACT.Exp).then_inc(sem("sb_exp"), 1)
            nc.scalar.activation(Z1, Z1, ACT.Exp).then_inc(sem("sb_exp"), 1)
            hq, hf, hg = proj_ab[:, :, 1536:2048], proj_ab[:, :, 2048:2560], proj_ab[:, :, 3072:3584]
            act.wait_ge(sem("h_abs"), 1)
            link(nc.scalar.activation(hSF, hSF, ACT.Exp, scale=-1.0))
            nc.scalar.activation(hSF, hSF, ACT.Ln, bias=1.0).then_inc(sem("h_log"), 1)
            nc.scalar.activation(hKK, hf, ACT.Sigmoid, scale=-1.0).then_inc(sem("h_sig"), 1)
            nc.scalar.activation(hq, hq, ACT.Silu).then_inc(sem("h_silu"), 1)
            nc.scalar.activation(hg, hg, ACT.Silu).then_inc(sem("h_silu"), 1)
            act.wait_ge(sem("h_sufs"), 1)
            nc.scalar.activation(hSF, hSF, ACT.Exp).then_inc(sem("h_sufexp"), 1)
            for n, L in enumerate(LEVELS):
                act.wait_ge(sem("h_rel"), n + 1)
                e = (hE0 if n % 2 == 0 else hE1).rearrange("p (b i) -> p b i", i=2 * L)
                nc.scalar.activation(e[:, :, L:2 * L], e[:, :, L:2 * L], ACT.Exp).then_inc(sem("h_relexp"), 1)
                nc.scalar.activation(e[:, :, 0:L], e[:, :, 0:L], ACT.Exp, scale=-1.0).then_inc(sem("h_relexp"), 1)
            nc.scalar.activation(hT0, hBT, ACT.Exp).then_inc(sem("h_bexp"), 1)
            root(SS[:, 16:24], SS[:, 8:16], GDV)

            def act_ffn(l):
                j0 = J[f"up{l}"]
                with act.Fori(0, FT // 2) as i:
                    for q in range(2):
                        act.wait_ge(pe_done, i * 2 + (j0 + q + 1))
                        for g in range(2):
                            ins = nc.scalar.activation(CT2(q, g, S), PS[:, (j0 + q) % 8, g * S:(g + 1) * S], ACT.Identity,
                                                       bias=CONV[:, l, bass.ds(i * 2 + (3 * 2 * FT + g * FT + q), 1)],
                                                       scale=CONV[:, l, bass.ds(i * 2 + (2 * 2 * FT + g * FT + q), 1)])
                        ins.then_inc(sem("tap2_done"), 1)
                    for q in range(2):
                        act.wait_ge(evac_done, i * 2 + (j0 + q + 1))
                        nc.scalar.activation(CT[:, q, 0:S], CT[:, q, 0:S], ACT.Silu).then_inc(sem("silu_done"), 1)
                    act.wait_ge(sem("hidden_ready"), i * 2 + (FT * l + 2))

            def CT2(q, g, n):
                return CT[:, q, g * S:g * S + n]

            def act_ple(l):
                root(SS[:, 2:4], SS[:, 0:2], D)
                act.wait_ge(evac_done, END[f"gate{l}"])
                nc.scalar.activation(GATE, GATE, ACT.Sigmoid).then_inc(sem("ple_sigmoid"), 1)

            root(SS[:, 2:4], SS[:, 0:2], D)
            act_ffn(0)
            act_ple(0)
            root(SS[:, 2:4], SS[:, 0:2], D)
            root(SS[:, 40:80], SS[:, 0:40], HD)
            for u in range(4):
                exp_unit(1024 if u < 2 else 2048, sink=True)
            root(SS[:, 2:4], SS[:, 0:2], D)
            act_ffn(1)
            act_ple(1)

        @block.vector
        def _(v):
            own, counts = [0], {}

            def step(ins, s=None, wait=True):
                s = s or "dve_chain"
                counts[s] = counts.get(s, 0) + 1
                ins.then_inc(sem(s), 1)
                if wait:
                    v.wait_ge(sem(s), counts[s])

            def bank(j):
                v.wait_ge(pe_done, j + 1)
                return PS[:, j % 8, :]

            def freed(ins, j, wait=False):
                ins.then_inc(evac_done, 1)
                if wait:
                    v.wait_ge(evac_done, j + 1)

            def bc(ap, n, axis=2):
                x = ap.unsqueeze(axis)
                shape = list(x.shape)
                shape[axis] = n
                return x.broadcast_to(shape)

            norm_no = [0]

            def reciprocal_root(dst, src):
                norm_no[0] += 1
                v.wait_ge(sem("root_done"), norm_no[0])
                step(nc.vector.reciprocal(dst, src))

            def transposed(j, n, dst, col=None):
                for m in range(n):
                    src = bank(j + m)[:, :].rearrange("p (c t) -> p c t", c=2)
                    d = dst[:, 2 * m:2 * m + 2, :]
                    if col is None:
                        freed(nc.vector.tensor_copy(d, src), j + m)
                    else:
                        freed(nc.vector.tensor_tensor(d, src, bc(VEC[:, col + 2 * m:col + 2 * m + 2], S), ALU.mult), j + m)
                v.wait_ge(evac_done, j + n)

            def norm(k, gain=None):
                for t in range(TT):
                    step(nc.vector.tensor_tensor_reduce(out=XN[:, t], in0=X[:, t], in1=X[:, t], scale=1.0, scalar=0.0,
                                                        op0=ALU.mult, op1=ALU.add, accum_out=SS[:, t:t + 1]),
                         "sumsq_ready" if t == TT - 1 else None)
                reciprocal_root(SS[:, 2:4], SS[:, 2:4])
                for t in range(TT):
                    if gain is None:
                        step(nc.vector.tensor_scalar(XN[:, t], X[:, t], SS[:, 2 + t:3 + t], None, ALU.mult), "xn_ready", False)
                    else:
                        step(nc.vector.scalar_tensor_tensor(out=XN[:, t], in0=X[:, t], scalar=SS[:, 2 + t:3 + t], in1=gain,
                                                            op0=ALU.mult, op1=ALU.mult), "xn_ready", False)
                transposed(J[f"norm{k}"], 4, XNT, NORM_COL[k])

            def evac_cols(j, n, dst, w=BANK):
                for m in range(n):
                    for t in range(TT):
                        freed(nc.vector.tensor_copy(dst[:, t, m * w:(m + 1) * w], bank(j + 2 * m + t)), j + 2 * m + t)
                v.wait_ge(evac_done, j + 2 * n)

            def add_residual(j, n):
                for m in range(n):
                    for t in range(TT):
                        d = X[:, t, m * BANK:(m + 1) * BANK]
                        freed(nc.vector.tensor_tensor(d, bank(j + 2 * m + t), d, ALU.add), j + 2 * m + t)
                v.wait_ge(evac_done, j + 2 * n)

            step(nc.vector.memset(SS[:, 95:96], EPS), "eps_ready")
            v.wait_ge(sem("const_loaded"), 16)
            freed(nc.vector.tensor_copy(VEC[:, 0:64], bank(J["vecs"])[:, 0:64]), J["vecs"])
            freed(nc.vector.tensor_copy(CONV[:, :, :], bank(J["conv"])[:, 0:8 * 2 * FT].rearrange("p (l n) -> p l n", l=2)),
                  J["conv"])
            v.wait_ge(sem("rel_loaded"), 48)
            freed(nc.vector.tensor_tensor(BROW, bank(J["relb"])[0:SWH, 0:384], OUTSIDE, ALU.add), J["relb"], wait=True)
            step(nc.vector.tensor_copy(SS[0:1, 6:7], SS[0:1, 95:96]), "bias_row")
            v.wait_ge(sem("x_loaded"), 16)
            norm(0)
            evac_cols(J["win"], 6, proj_in)

            freed(nc.vector.tensor_copy(GRT, bank(J["gr"])[0:GRANK, 0:S]), J["gr"], wait=True)
            v.wait_ge(sem("gain_loaded"), 16 * 8)
            g2 = gG.rearrange("p (t n) -> p t n", t=TT)
            freed(nc.vector.tensor_tensor(g2, bank(J["alpha"]).rearrange("p (t n) -> p t n", t=TT),
                                          bc(ALB[:, :], TT, 1), ALU.add), J["alpha"], wait=True)
            step(nc.vector.scalar_tensor_tensor(out=gE, in0=gG, scalar=-1.0, in1=gG, op0=ALU.mult, op1=ALU.max), "g_abs")
            v.wait_ge(sem("g_log"), 1)
            step(nc.vector.scalar_tensor_tensor(out=gG, in0=gG, scalar=0.0, in1=gE, op0=ALU.min, op1=ALU.subtract))
            step(nc.vector.tensor_scalar(gG, gG, 1.0 / 16.0, None, ALU.mult), "g_ready")
            freed(nc.vector.tensor_copy(gB_, bank(J["gla_cum"])), J["gla_cum"], wait=True)
            freed(nc.vector.tensor_copy(gS, bank(J["gla_cum"] + 1)), J["gla_cum"] + 1, wait=True)
            step(nc.vector.memset(gKZ, 0.0), "g_cum")
            freed(nc.vector.tensor_copy(gDECR, bank(J["gla_dec"])[:, 0:8]), J["gla_dec"], wait=True)
            step(nc.vector.memset(SS[:, 6:7], 0.0), "g_cum")
            q_, k_ = proj_in[:, :, 0:256], proj_in[:, :, 256:512]
            v.wait_ge(sem("g_exp"), 3)
            e3, n3, s3 = (x.rearrange("p (t n) -> p t n", t=TT) for x in (gE, gB_, gS))
            step(nc.vector.scalar_tensor_tensor(out=q_, in0=q_, scalar=GDK ** -0.5, in1=e3, op0=ALU.mult, op1=ALU.mult), "g_qk")
            for par in range(2):
                kk = k_.rearrange("p t (j h n) -> p t j h n", j=2, h=2)[:, :, :, par, :]
                nn = n3.rearrange("p t (j h n) -> p t j h n", j=2, h=2)[:, :, :, par, :]
                dst = gKZ.rearrange("p t (j h) n -> p t j h n", j=2)[:, :, :, par, par * GDK:(par + 1) * GDK]
                step(nc.vector.tensor_tensor(dst, kk, nn, ALU.mult), "g_qk")
            step(nc.vector.tensor_tensor(gKST, k_, s3, ALU.mult))
            v.wait_ge(sem("bias_written"), 16)
            transposed(J["gla_T"], 2, gKZT)
            transposed(J["gla_T"] + 2, 1, gQT)
            for t in range(TT):
                j = J["gla_A"] + t
                freed(nc.vector.tensor_tensor(AT[:, t], bank(j).rearrange("p (h n) -> p h n", h=4), bc(cum, 4, 1), ALU.mult), j, True)

            def recurrence(kst, width, dec4, first_job, rows):
                for c in range(3):
                    step(nc.vector.tensor_scalar(KSC[:, c, 0:width], kst[:, c // 2], const("chunk_rows")[:, c % 2:c % 2 + 1], None,
                                                 ALU.mult), "kst_ready", wait=False)
                for c in range(3):
                    j = first_job + c
                    u = bank(j).rearrange("p (h n) -> p h n", h=4)
                    if rows:
                        freed(nc.vector.tensor_tensor(ST[:, c], u, bc(const("head_rows"), GDV), ALU.mult), j, True)
                    else:
                        freed(nc.vector.tensor_copy(ST[:, c], u), j, True)
                    if c:
                        tmp = KTMP
                        step(nc.vector.tensor_tensor(tmp, ST[:, c - 1], dec4(c), ALU.mult))
                        step(nc.vector.tensor_tensor(ST[:, c], ST[:, c], tmp, ALU.add))
                step(nc.vector.memset(SS[:, 6:7], 0.0), "state_ready")

            def head_norm(first_job, gain, gates, dst):
                for t in range(TT):
                    freed(nc.vector.tensor_copy(OUTN[:, t], bank(first_job + t)), first_job + t)
                v.wait_ge(evac_done, first_job + TT)
                step(nc.vector.tensor_tensor(SQ, OUTN, OUTN, ALU.mult))
                o4, q4 = (x.rearrange("p t (h n) -> p (t h) n", n=GDV) for x in (OUTN, SQ))
                step(nc.vector.tensor_reduce(SS[:, 8:16], q4, AX, ALU.add), "sumsq_ready")
                reciprocal_root(SS[:, 16:24], SS[:, 16:24])
                step(nc.vector.tensor_tensor(o4, o4, bc(SS[:, 16:24], GDV), ALU.mult))
                step(nc.vector.tensor_tensor(o4, o4, bc(gain, 8, 1), ALU.mult))
                step(nc.vector.tensor_tensor(dst, OUTN, gates, ALU.mult))

            v.wait_ge(sem("g_exp"), 4)
            KTMP = A[:, 3072:3584].rearrange("p (h n) -> p h n", h=4)
            gdec = DEC[:, 0:8].rearrange("p (j c) -> p j c", j=2)

            def gla_dec4(c):
                x = gdec[:, :, c].unsqueeze(2).unsqueeze(3).broadcast_to([P, 2, 2, GDV])
                return x.rearrange("p j h n -> p (j h) n") if False else x
            st_tmp = KTMP.rearrange("p (j h) n -> p j h n", j=2)

            def recurrence_gla():
                for c in range(3):
                    step(nc.vector.tensor_scalar(KSC[:, c, 0:256], gKST[:, c // 2], const("chunk_rows")[:, c % 2:c % 2 + 1], None,
                                                 ALU.mult), "kst_ready", wait=False)
                for c in range(3):
                    j = J["gla_U"] + c
                    u = bank(j).rearrange("p (h n) -> p h n", h=4)
                    freed(nc.vector.tensor_tensor(ST[:, c], u, bc(const("head_rows"), GDV), ALU.mult), j, True)
                    if c:
                        for pair in range(2):
                            step(nc.vector.scalar_tensor_tensor(
                                out=ST[:, c, 2 * pair:2 * pair + 2], in0=ST[:, c - 1, 2 * pair:2 * pair + 2],
                                scalar=gdec[:, pair, c:c + 1], in1=ST[:, c, 2 * pair:2 * pair + 2],
                                op0=ALU.mult, op1=ALU.add))
                step(nc.vector.memset(SS[:, 6:7], 0.0), "state_ready")

            recurrence_gla()
            v.wait_ge(sem("silu_gate"), 1)
            head_norm(J["gla_O"], LB_GAIN, proj_in[:, :, 1024:1536], XN[:, :, 0:512])

            def head_rms(view, n, ss, rs):
                sq = PSQ(n)
                step(nc.vector.tensor_tensor(sq, view, view, ALU.mult))
                for t in range(TT):
                    step(nc.vector.tensor_reduce(ss[:, t * n:(t + 1) * n], sq[:, t], AX, ALU.add),
                         "sumsq_ready" if t == TT - 1 else None)
                reciprocal_root(rs, rs)

            def PSQ(n):
                return A[:, 0:TT * n * HD].rearrange("p (t h n) -> p t h n", t=TT, n=HD)

            def softmax_unit(j0, tag, t, heads, add, dst, sink=None):
                nk = 1 if t == 0 else 2
                cols = nk * P
                per = BANK // cols
                for m in range(8 // per):
                    j = j0["L"] + m
                    src = bank(j).rearrange("p (h s) -> p h s", h=per)
                    d = PB[:, m * BANK:(m + 1) * BANK].rearrange("p (h s) -> p h s", h=per)
                    freed(nc.vector.scalar_tensor_tensor(out=d, in0=src, scalar=HD ** -0.5, in1=add(m * per, per, cols),
                                                         op0=ALU.mult, op1=ALU.add), j, True)
                view = PB[:, 0:8 * cols].rearrange("p (h s) -> p h s", h=8)
                mx, den = SS[:, 24:32], SS[:, 32:40]
                step(nc.vector.tensor_reduce(mx, view, AX, ALU.max))
                if sink is not None:
                    step(nc.vector.tensor_tensor(mx, mx, sink, ALU.max))
                    step(nc.vector.tensor_tensor(SS[:, 16:24], sink, mx, ALU.subtract))
                step(nc.vector.tensor_tensor(view, view, bc(mx, cols), ALU.subtract), "att_sub")
                v.wait_ge(sem("att_exp"), counts["att_sub"])
                step(nc.vector.tensor_reduce(den, view, AX, ALU.add))
                if sink is not None:
                    v.wait_ge(sem("sink_exp"), counts["att_sub"] - 2)
                    step(nc.vector.tensor_tensor(den, den, SS[:, 16:24], ALU.add))
                step(nc.vector.reciprocal(den, den))
                for m in range(2 * nk):
                    j = j0["P"] + m
                    freed(nc.vector.tensor_copy(PT[:, 4 * m:4 * m + 4, :], bank(j).rearrange("p (b t) -> p b t", b=4)), j)
                v.wait_ge(evac_done, j0["P"] + 2 * nk)
                src = bank(j0["O"]).rearrange("p (h n) -> p h n", h=8)
                freed(nc.vector.tensor_tensor(dst.rearrange("p (h n) -> p h n", h=8), src, bc(den, HD), ALU.mult), j0["O"], True)

            def copy_keys(view, heads):
                for par in range(2):
                    src = view.rearrange("p t (j h) n -> p t j h n", h=2)[:, :, :, par, :]
                    dst = KZ.rearrange("p t (j h) n -> p t j h n", h=2)[:, :, :, par, par * HD:(par + 1) * HD]
                    step(nc.vector.tensor_copy(dst, src), "keys_ready")

            qk = proj_in[:, :, 1536:2560].rearrange("p t (h n) -> p t h n", n=HD)
            head_rms(qk, 16, SS[:, 8:40], SS[:, 56:88])
            for t in range(TT):
                step(nc.vector.tensor_tensor(qk[:, t], qk[:, t], bc(SS[:, 56 + 16 * t:72 + 16 * t], HD), ALU.mult))
                for n in range(2):
                    hs = qk[:, t, 8 * n:8 * n + 8]
                    step(nc.vector.tensor_tensor(hs, hs, bc(QK_GAIN[n], 8, 1), ALU.mult))
            half = HD // 2
            for t in range(TT):
                x1, x2 = qk[:, t, :, 0:half], qk[:, t, :, half:HD]
                cos = bc(const("cos")[:, t * half:(t + 1) * half], 16, 1)
                sin = bc(const("sin")[:, t * half:(t + 1) * half], 16, 1)
                tmp = [A[:, n * 512:(n + 1) * 512].rearrange("p (h n) -> p h n", h=16) for n in range(4)]
                step(nc.vector.tensor_tensor(tmp[0], x1, cos, ALU.mult), wait=False)
                step(nc.vector.tensor_tensor(tmp[1], x2, sin, ALU.mult), wait=False)
                step(nc.vector.tensor_tensor(tmp[2], x2, cos, ALU.mult), wait=False)
                step(nc.vector.tensor_tensor(tmp[3], x1, sin, ALU.mult))
                step(nc.vector.tensor_tensor(x1, tmp[0], tmp[1], ALU.subtract), wait=False)
                step(nc.vector.tensor_tensor(x2, tmp[2], tmp[3], ALU.add))
            step(nc.vector.memset(flatT, 0.0))
            copy_keys(qk[:, :, 8:16], 8)
            transposed(J["mb_T"], 2, QT)
            transposed(J["mb_T"] + 2, 4, KZT)

            def causal(h0, n, cols):
                return bc(causal_add[:, 2 * P - cols:2 * P], n, 1)

            for t in range(TT):
                softmax_unit({k: J[f"mb_{k}{t}"] for k in "LPO"}, "mb", t, 8, causal, XN[:, t, 512:1024])

            step(nc.vector.memset(SS[:, 6:7], 0.0), "mixed")
            transposed(J["mix0"], 4, XNT, MIX_COL[0])
            add_residual(J["wout"], 2)

            v.wait_ge(sem("n2w_loaded"), 16)
            norm(1, gain=N2W)
            for m in range(4):
                j = J["subk"] + m
                freed(nc.vector.tensor_copy(SKT[:, 4 * m:4 * m + 4, :], bank(j).rearrange("p (b t) -> p b t", b=4)), j)
            transposed(J["query"], 8, qT)
            for m in range(8):
                j = J["score"] + m
                freed(nc.vector.tensor_copy(SCORE[:, m * BANK:(m + 1) * BANK], bank(j)), j, wait=(m == 7))

            def routed(u, q):
                n = [0]
                v.sem_clear(sem("route_step"))

                def then(ins):
                    n[0] += 1
                    ins.then_inc(sem("route_step"), 1)
                    v.wait_ge(sem("route_step"), n[0])

                def top16(vals, best, index, width):
                    then(nc.vector.max(best[:, 0:8], vals))
                    then(nc.vector.max_index(index[:, 0:8], best[:, 0:8], vals))
                    then(nc.vector.match_replace(r_w[:, 0:width], best[:, 0:8], vals, NEG))
                    then(nc.vector.max(best[:, 8:16], r_w[:, 0:width]))
                    then(nc.vector.max_index(index[:, 8:16], best[:, 8:16], r_w[:, 0:width]))

                then(nc.vector.tensor_copy(R[:, 0:256], PROJ[:, bass.ds(u * 256, 256)]))
                for p_ in range(2):
                    top16(r_s[:, p_], r_sv[:, p_], r_si[:, p_], NKEYS)
                cand = r_cand.rearrange("p (i j) -> p i j", i=TOPK)
                then(nc.vector.tensor_tensor(cand, bc(r_sv[:, 0], TOPK), bc(r_sv[:, 1], TOPK, 1), ALU.add))
                top16(r_cand, r_top, r_pos, TOPK * TOPK)
                then(nc.vector.tensor_scalar(r_ab[:, 0:16], r_pos, 4, None, ALU.logical_shift_right))
                then(nc.vector.tensor_scalar(r_ab[:, 16:32], r_pos, 15, None, ALU.bitwise_and))
                hot = r_w[:, 0:256].rearrange("p (k j) -> p k j", k=TOPK)
                for p_ in range(2):
                    then(nc.vector.tensor_tensor(hot, bc(r_ab[:, 16 * p_:16 * p_ + 16], TOPK), bc(const("iota"), TOPK, 1),
                                                 ALU.is_equal))
                    then(nc.vector.tensor_tensor(hot, hot, bc(r_si[:, p_], TOPK, 1), ALU.mult))
                    then(nc.vector.tensor_reduce(r_i[:, p_], hot, AX, ALU.add))
                then(nc.vector.tensor_scalar(r_e, r_top, r_top[:, 0:1], None, ALU.subtract))
                nc.vector.scalar_tensor_tensor(out=r_idx[:, q], in0=r_i[:, 0], scalar=float(NKEYS), in1=r_i[:, 1],
                                               op0=ALU.mult, op1=ALU.add).then_inc(sem("idx_ready"), 1)
                then(nc.vector.memset(SS[:, 6:7], 0.0))
                nc.vector.memset(SS[:, 7:8], 0.0).then_inc(sem("top_ready"), 1)
                v.wait_ge(sem("gate_exp"), u + 1)
                then(nc.vector.tensor_reduce(r_sum, r_e, AX, ALU.add))
                then(nc.vector.reciprocal(r_rs, r_sum))
                then(nc.vector.tensor_scalar(r_gate[:, q], r_e, r_rs, None, ALU.mult))

            def dots(u, q, t, b):
                for k in range(4):
                    n = (4 * b + k) % NU
                    v.wait_ge(u_loaded[n], u * 32 + 16 * (1 + b // 2))
                    ins = nc.vector.tensor_tensor_reduce(out=ubuf[n], in0=ubuf[n], in1=XN[:, t], scale=1.0, scalar=0.0,
                                                         op0=ALU.mult, op1=ALU.add, accum_out=r_dot[:, b % 2, k:k + 1])
                ins.then_inc(sem("dots_done"), 1)

            def weights(u, q, b):
                v.wait_ge(sem("gelu_done"), u * 4 + (b + 1))
                nc.vector.tensor_tensor(r_wt[:, b % 2], r_act[:, b % 2], r_gate[:, q, 4 * b:4 * b + 4],
                                        ALU.mult).then_inc(sem("weights_ready"), 1)

            def vec_unit(u, q, t, first=False, last=False):
                for b in range(4):
                    if not (first and b < 2):
                        v.wait_ge(sem("gelu_done"), u * 4 + (b - 1))
                    dots(u, q, t, b)
                    if not (first and b < 3):
                        v.wait_ge(sem("diag_ready"), u * 4 + (b - 2))
                    if b > 0:
                        weights(u, q, b - 1)
                    elif not first:
                        weights(u - 1, 1 - q, 3)
                    if b == 1 and not last:
                        routed(u + 1, 1 - q)

            routed(0, 0)
            vec_unit(0, 0, 0, first=True)
            vec_unit(1, 1, 0)
            with v.Fori(1, PH // 2) as i:
                vec_unit(i * 2, 0, 0)
                vec_unit(i * 2 + 1, 1, 0)
            with v.Fori(PH // 2, UNITS // 2 - 1) as i:
                vec_unit(i * 2, 0, 1)
                vec_unit(i * 2 + 1, 1, 1)
            vec_unit(UNITS - 2, 0, 1)
            vec_unit(UNITS - 1, 1, 1, last=True)
            v.wait_ge(sem("diag_ready"), 4 * UNITS - 2)
            weights(UNITS - 1, 1, 3)
            v.wait_ge(sem("dots_done"), 4 * UNITS)
            for t in range(TT):
                for m in range(2):
                    j = J["peer"] + 2 * t + m
                    d = X[:, t, m * BANK:(m + 1) * BANK]
                    freed(nc.vector.tensor_tensor(d, bank(j), d, ALU.add), j)
            v.wait_ge(evac_done, END["peer"])

            norm(2)
            evac_cols(J["ab"], 7, proj_ab)
            step(nc.vector.memset(flatT, 0.0))
            copy_keys(proj_ab[:, :, 512:1024].rearrange("p t (h n) -> p t h n", n=HD), 8)
            transposed(J["sb_T"], 2, QT)
            transposed(J["sb_T"] + 2, 4, KZT)
            for m in range(4):
                j = J["sb_Z"] + m
                freed(nc.vector.tensor_scalar(A[:, m * BANK:(m + 1) * BANK], bank(j), HD ** -0.5, None, ALU.mult), j)
            for m in range(2):
                j = J["sb_Z"] + 4 + m
                freed(nc.vector.tensor_scalar(A[:, 2048 + m * BANK:2048 + (m + 1) * BANK], bank(j), HD ** -0.5, None, ALU.mult), j, True)
            step(nc.vector.scalar_tensor_tensor(out=L0, in0=Z0, scalar=-1.0, in1=Z0, op0=ALU.mult, op1=ALU.max))
            step(nc.vector.scalar_tensor_tensor(out=L1, in0=Z1, scalar=-1.0, in1=Z1, op0=ALU.mult, op1=ALU.max), "sb_abs")
            v.wait_ge(sem("sb_log"), 2)
            for z, l in ((Z0, L0), (Z1, L1)):
                step(nc.vector.scalar_tensor_tensor(out=l, in0=z, scalar=0.0, in1=l, op0=ALU.max, op1=ALU.add))
            for l in (L0[:, :, 0:P], L1):
                step(nc.vector.tensor_tensor(l, l, bc(const("before"), 8, 1), ALU.mult), "sb_plus")
            for m in range(6):
                j = J["sb_C"] + m
                d = A[:, m * BANK:(m + 1) * BANK]
                freed(nc.vector.tensor_tensor(d, d, bank(j), ALU.subtract), j, True)
            for z in (Z0[:, :, 0:P], Z1):
                step(nc.vector.tensor_tensor(z, z, bc(const("before_add"), 8, 1), ALU.add))
            step(nc.vector.memset(SS[:, 6:7], 0.0), "sb_arg")
            for t in range(TT):
                j = J["sb_O"] + t
                freed(nc.vector.tensor_copy(XN[:, t, 0:512], bank(j)), j, True)

            hq, hf, hi, hg = (proj_ab[:, :, 1536 + 512 * n:2048 + 512 * n] for n in range(4))
            step(nc.vector.scalar_tensor_tensor(out=hSF, in0=hf, scalar=-1.0, in1=hf, op0=ALU.mult, op1=ALU.max), "h_abs")
            v.wait_ge(sem("h_log"), 1)
            v.wait_ge(sem("h_sig"), 1)
            step(nc.vector.scalar_tensor_tensor(out=hf, in0=hf, scalar=0.0, in1=hSF, op0=ALU.min, op1=ALU.subtract), "h_logf")
            transposed(J["hg_B"], 2, hBT.rearrange("p (h t) -> p h t", h=4))
            for t in range(TT):
                j = J["hg_suf"] + t
                freed(nc.vector.tensor_copy(hSF[:, t], bank(j)), j, True)
            step(nc.vector.memset(SS[:, 6:7], 0.0), "h_sufs")
            transposed(J["hg_T"], 2, hQT.rearrange("p (h t) -> p h t", h=4))
            transposed(J["hg_T"] + 2, 2, hKT.rearrange("p (h t) -> p h t", h=4))
            for t in range(TT):
                j = J["hg_D"] + t
                freed(nc.vector.tensor_tensor(AT[:, t], bank(j).rearrange("p (h n) -> p h n", h=4), bc(ident, 4, 1), ALU.mult), j, True)
            v.wait_ge(sem("h_sufexp"), 1)
            step(nc.vector.tensor_tensor(hKST, hKK, hSF, ALU.mult))
            for n, L in enumerate(LEVELS):
                e = hE0 if n % 2 == 0 else hE1
                bt, ev, qv, kv = (x.rearrange("p (b i) -> p b i", i=2 * L) for x in (hBT, e, hQT, hKT))
                nb = 4 * S // (2 * L)
                ref = bt[:, :, L - 1:L].broadcast_to([P, nb, 2 * L])
                step(nc.vector.tensor_tensor(ev, bt, ref, ALU.subtract), "h_rel")
                v.wait_ge(sem("h_relexp"), 2 * n + 2)
                step(nc.vector.tensor_tensor(ev[:, :, L:2 * L], ev[:, :, L:2 * L], qv[:, :, L:2 * L], ALU.mult), "h_lev")
                step(nc.vector.tensor_tensor(ev[:, :, 0:L], ev[:, :, 0:L], kv[:, :, 0:L], ALU.mult), "h_lev")
                for t in range(TT):
                    j = J["hg_L"] + 2 * n + t
                    tmp = B[:, 3072:3584].rearrange("p (h n) -> p h n", h=4)
                    freed(nc.vector.tensor_tensor(tmp, bank(j).rearrange("p (h n) -> p h n", h=4),
                                                  bc(LEV[:, n], 4, 1), ALU.mult), j, True)
                    step(nc.vector.tensor_tensor(AT[:, t], AT[:, t], tmp, ALU.add))
            v.wait_ge(sem("h_bexp"), 1)
            step(nc.vector.tensor_tensor(hQT, hQT, hT0, ALU.mult), "h_qb")
            hdec = hT0.rearrange("p (h c i) -> p h c i", h=4, c=4)
            for c in range(3):
                step(nc.vector.tensor_scalar(KSC[:, c], hKST[:, c // 2], const("chunk_rows")[:, c % 2:c % 2 + 1], None,
                                             ALU.mult), "kst_ready", wait=False)
            for c in range(3):
                j = J["hg_U"] + c
                freed(nc.vector.tensor_copy(ST[:, c], bank(j).rearrange("p (h n) -> p h n", h=4)), j, True)
                if c:
                    for h in range(4):
                        step(nc.vector.scalar_tensor_tensor(out=ST[:, c, h], in0=ST[:, c - 1, h],
                                                            scalar=hdec[:, h, c, CH - 1:CH], in1=ST[:, c, h],
                                                            op0=ALU.mult, op1=ALU.add), wait=(h == 3))
            step(nc.vector.memset(SS[:, 6:7], 0.0), "state_ready")
            v.wait_ge(sem("h_silu"), 2)
            head_norm(J["hg_O"], HG_GAIN, hg, XN[:, :, 512:1024])
            step(nc.vector.memset(SS[:, 6:7], 0.0), "mixed")
            transposed(J["mix1"], 4, XNT)
            add_residual(J["about"], 2)

            def vec_ffn(l, k):
                norm(k)
                j0 = J[f"up{l}"]
                with v.Fori(0, FT // 2) as i:
                    for q in range(2):
                        v.wait_ge(sem("tap2_done"), i * 2 + (FT * l + q + 1))
                        for tap in (1, 0):
                            n = 2 - tap
                            if tap == 0:
                                v.wait_ge(sem("tap1_done"), i * 2 + (FT * l + q + 1))
                            for g in range(2):
                                d = CT[:, q, g * S + n:(g + 1) * S]
                                ins = nc.vector.scalar_tensor_tensor(
                                    out=d, in0=PS[:, (j0 + q) % 8, g * S:(g + 1) * S - n],
                                    scalar=CONV[:, l, bass.ds(i * 2 + (tap * 2 * FT + g * FT + q), 1)], in1=d,
                                    op0=ALU.mult, op1=ALU.add)
                            ins.then_inc(sem("tap1_done") if tap else evac_done, 1)
                for t in range(TT):
                    for m in range(2):
                        j = J[f"down{l}"] + 2 * t + m
                        d = X[:, t, m * BANK:(m + 1) * BANK]
                        freed(nc.vector.tensor_tensor(d, bank(j), d, ALU.add), j)
                v.wait_ge(evac_done, END[f"down{l}"])

            def vec_ple(l, k):
                norm(k)
                transposed(J[f"pT{l}"], 1, PINT)
                evac_cols(J[f"gate{l}"], 2, GATE)
                v.wait_ge(sem("ple_sigmoid"), l + 1)
                for t in range(TT):
                    for m in range(2):
                        j = J[f"proj{l}"] + 2 * t + m
                        g = GATE[:, t, m * BANK:(m + 1) * BANK]
                        freed(nc.vector.tensor_tensor(g, bank(j), g, ALU.mult), j, True)
                        d = X[:, t, m * BANK:(m + 1) * BANK]
                        step(nc.vector.tensor_tensor(d, d, g, ALU.add), "x_final" if l == 1 and m == 1 else None)

            vec_ffn(0, 3)
            vec_ple(0, 4)

            norm(5)
            evac_cols(J["c"], 3, proj_c)
            qk = proj_c[:, :, 0:1280].rearrange("p t (h n) -> p t h n", n=HD)
            head_rms(qk, 20, SS[:, 0:40], SS[:, 40:80])
            for t in range(TT):
                step(nc.vector.tensor_tensor(qk[:, t], qk[:, t], bc(SS[:, 40 + 20 * t:60 + 20 * t], HD), ALU.mult))
                for n, (h0, h1) in enumerate(((0, 16), (16, 20))):
                    hs = qk[:, t, h0:h1]
                    step(nc.vector.tensor_tensor(hs, hs, bc(QK_GAIN[2 + n], h1 - h0, 1), ALU.mult))
            step(nc.vector.memset(flatT, 0.0))
            for par in range(2):
                dst = KZ.rearrange("p t (j h) n -> p t j h n", h=2)[:, :, :, par, par * HD:(par + 1) * HD]
                step(nc.vector.tensor_copy(dst, qk[:, :, 16:20]), "keys_ready")
            transposed(J["sw_T"], 4, QT)
            transposed(J["sw_T"] + 4, 4, KZT)
            v.wait_ge(sem("bias_loaded"), 16)
            for u in range(4):
                t, hg_ = u // 2, u % 2

                def biased(h0, n, cols, base=8 * hg_):
                    return BIAS[:, base + h0:base + h0 + n, 2 * P - cols:2 * P]

                softmax_unit({k: J[f"sw_{k}{u}"] for k in "LPO"}, "sw", t, 8, biased,
                             XN[:, t, hg_ * 512:(hg_ + 1) * 512], sink=SINK[:, 8 * hg_:8 * hg_ + 8])
            step(nc.vector.memset(SS[:, 6:7], 0.0), "mixed")
            transposed(J["mix2"], 4, XNT)
            add_residual(J["cout"], 2)
            vec_ffn(1, 6)
            vec_ple(1, 7)

        @block.tensor
        def _(pe):
            def bank(j):
                if j >= 8:
                    pe.wait_ge(evac_done, j - 7)
                return PS[:, j % 8, :]

            def transposes(j, blocks):
                b = bank(j)
                for n, src in enumerate(blocks):
                    ins = pe.transpose(b[:, n * P:(n + 1) * P], src, ident)
                ins.then_inc(pe_done, 1)

            def norm_T(j, src=None):
                s = src if src is not None else XN
                for m in range(4):
                    transposes(j + m, [s[:, t, (2 * m + c) * P:(2 * m + c + 1) * P] for c in range(2) for t in range(TT)])

            xn_no = [0]

            def norm(k):
                xn_no[0] += TT
                pe.wait_ge(sem("xn_ready"), xn_no[0])
                norm_T(J[f"norm{k}"])

            def loaded(name, n):
                pe.wait_ge(w_loaded[SLOT_OF[name, n]], LOAD_NO[name, n])

            def dense(name, chunks, ready):
                pe.wait_ge(evac_done, ready)
                for n in range(chunks):
                    loaded(name, n)
                    for t in range(TT):
                        b = bank(J[name] + 2 * n + t)
                        for c in range(KC):
                            ins = pe.matmul(b, XNT[:, c, t * P:(t + 1) * P], wk[SLOT_OF[name, n]][:, c, :],
                                            start=(c == 0), stop=(c == KC - 1))
                        ins.then_inc(pe_done, 1)

            pe.wait_ge(sem("const_loaded"), 16)
            pe.wait_ge(sem("vec_loaded"), 16 * 5)
            pe.transpose(PS[:, J["vecs"], 0:64], VROW[0:64, :], ident[0:64, 0:64]).then_inc(pe_done, 1)
            pe.wait_ge(sem("conv_loaded"), 16 * 6)
            for n in range(4):
                ins = pe.transpose(PS[:, J["conv"], n * 4 * FT:(n + 1) * 4 * FT], CROW[n][:, :], ident[0:4 * FT, 0:4 * FT])
            ins.then_inc(pe_done, 1)
            pe.wait_ge(sem("rel_loaded"), 48)
            pe.matmul(PS[0:SWH, J["relb"], 0:384], RB, OH, start=True, stop=True).then_inc(pe_done, 1)
            norm(0)
            dense("win", 6, END["norm0"])
            b = bank(J["gr"])
            pe.wait_ge(sem("gr_loaded"), 32)
            for c in range(KC):
                ins = pe.matmul(b[0:GRANK, 0:S], W_GR[:, c, :], XNT[:, c, :], start=(c == 0), stop=(c == KC - 1))
            ins.then_inc(pe_done, 1)

            pe.wait_ge(evac_done, END["gr"])
            b = bank(J["alpha"])
            for t in range(TT):
                ins = pe.matmul(b[:, t * 256:(t + 1) * 256], GRT[:, t * P:(t + 1) * P], W_ALPHA, start=True, stop=True)
            ins.then_inc(pe_done, 1)
            pe.wait_ge(sem("g_ready"), 1)
            for n, m in enumerate((cum, suf)):
                b = bank(J["gla_cum"] + n)
                for t in range(TT):
                    ins = pe.matmul(b[:, t * 256:(t + 1) * 256], m, gG[:, t * 256:(t + 1) * 256], start=True, stop=True)
                ins.then_inc(pe_done, 1)
            b = bank(J["gla_dec"])
            for pair in range(2):
                for t in range(TT):
                    ins = pe.matmul(b[:, pair * 4 + 2 * t:pair * 4 + 2 * t + 2], gG[:, t * 256 + pair * P:t * 256 + (pair + 1) * P],
                                    cum[:, CH - 1:P:CH], start=True, stop=True)
            ins.then_inc(pe_done, 1)
            pe.wait_ge(sem("g_qk"), 3)
            for m in range(2):
                transposes(J["gla_T"] + m, [gKZ[:, t, 2 * m + h, :] for h in range(2) for t in range(TT)])
            transposes(J["gla_T"] + 2, [proj_in[:, t, j * P:(j + 1) * P] for j in range(2) for t in range(TT)])
            pe.wait_ge(evac_done, END["gla_T"])
            for t in range(TT):
                b = bank(J["gla_A"] + t)
                for h in range(4):
                    ins = pe.matmul(b[:, h * P:(h + 1) * P], gKZT[:, h, t * P:(t + 1) * P], gQT[:, h // 2, t * P:(t + 1) * P],
                                    start=True, stop=True)
                ins.then_inc(pe_done, 1)

            def recurrence(ju, jo, count, kcols, values, queries):
                for c in range(3):
                    pe.wait_ge(sem("kst_ready"), 3 * count + c + 1)
                    b = bank(ju + c)
                    for h in range(4):
                        ins = pe.matmul(b[:, h * P:(h + 1) * P], kcols(c, h), values(c // 2, h), start=True, stop=True)
                    ins.then_inc(pe_done, 1)
                pe.wait_ge(sem("state_ready"), count + 1)
                for t in range(TT):
                    b = bank(jo + t)
                    for h in range(4):
                        o = b[:, h * P:(h + 1) * P]
                        pe.matmul(o, AT[:, t, h, :], values(t, h), start=True, stop=False, skip_group_check=True)
                        for par in range(2):
                            c = 2 * t + par
                            if c:
                                ins = pe.matmul(o[par * CH:(par + 1) * CH, :], queries(t, h, par), ST[:, c - 1, h, :],
                                                start=False, stop=True, skip_group_check=True)
                    ins.then_inc(pe_done, 1)

            recurrence(J["gla_U"], J["gla_O"], 0,
                       lambda c, h: KSC[:, c, (h // 2) * P:(h // 2 + 1) * P],
                       lambda t, h: proj_in[:, t, 512 + h * P:512 + (h + 1) * P],
                       lambda t, h, par: gQT[:, h // 2, t * P + par * CH:t * P + (par + 1) * CH])

            def qk_T(j, nq, qsrc, first_keys):
                pe.wait_ge(sem("keys_ready"), first_keys)
                for m in range(nq // 2):
                    transposes(j + m, [qsrc(t, 2 * m + c) for c in range(2) for t in range(TT)])
                for m in range(4):
                    transposes(j + nq // 2 + m, [KZ[:, t, 2 * m + c, :] for c in range(2) for t in range(TT)])
                pe.wait_ge(evac_done, j + nq // 2 + 4)

            def softmax_unit(j0, t, no, pair, variant, values):
                nk = 1 if t == 0 else 2
                cols = nk * P
                per = BANK // cols
                for m in range(8 // per):
                    b = bank(j0["L"] + m)
                    for h in range(per):
                        hh = m * per + h
                        ins = pe.matmul(b[:, h * cols:(h + 1) * cols], QT[:, pair(hh), t * P:(t + 1) * P],
                                        KZT[:, variant(hh), 0:cols], start=True, stop=True)
                    ins.then_inc(pe_done, 1)
                pe.wait_ge(sem("att_exp"), no)
                for m in range(2 * nk):
                    transposes(j0["P"] + m, [PB[:, (4 * m + n) * P:(4 * m + n + 1) * P] for n in range(4)])
                pe.wait_ge(evac_done, j0["P"] + 2 * nk)
                b = bank(j0["O"])
                for h in range(8):
                    for k in range(nk):
                        ins = pe.matmul(b[:, h * HD:(h + 1) * HD], PT[:, h * nk + k, :], values(k, h),
                                        start=(k == 0), stop=(k == nk - 1))
                ins.then_inc(pe_done, 1)

            qk_T(J["mb_T"], 4, lambda t, j: proj_in[:, t, 1536 + j * P:1536 + (j + 1) * P], 2)
            for t in range(TT):
                softmax_unit({k: J[f"mb_{k}{t}"] for k in "LPO"}, t, t + 1, lambda h: h // 2, lambda h: h,
                             lambda k, h: proj_in[:, k, 2560 + h * HD:2560 + (h + 1) * HD])
            pe.wait_ge(sem("mixed"), 1)
            norm_T(J["mix0"])
            dense("wout", 2, END["mix0"])

            norm(1)
            pe.wait_ge(sem("subkeys_loaded"), 16)
            for m in range(4):
                transposes(J["subk"] + m, [SKN[:, 4 * m + n, :] for n in range(4)])
            pe.wait_ge(evac_done, END["norm1"])
            for m in range(8):
                n = m // 2
                if m % 2 == 0:
                    loaded("query", n)
                b = bank(J["query"] + m)
                for q in range(2):
                    w0 = (m % 2) * 256 + q * P
                    for c in range(KC):
                        ins = pe.matmul(b[:, q * S:(q + 1) * S], wk[SLOT_OF["query", n]][:, c, w0:w0 + P], XNT[:, c, :],
                                        start=(c == 0), stop=(c == KC - 1))
                ins.then_inc(pe_done, 1)
            pe.wait_ge(evac_done, END["query"])
            for m in range(8):
                t, h0 = m // 4, (m % 4) * 2
                b = bank(J["score"] + m)
                for n in range(4):
                    u = 2 * h0 + n
                    ins = pe.matmul(b[:, n * P:(n + 1) * P], qT[:, u, t * P:(t + 1) * P], SKT[:, u, :], start=True, stop=True)
                ins.then_inc(pe_done, 1)

            def sum_rows(u, t):
                for b in range(4):
                    pe.wait_ge(sem("diag_ready"), u * 4 + (b + 1))
                    for k in range(4):
                        n = 4 * b + k
                        pe.wait_ge(v_loaded[n], u * 16 + 16)
                        for m in range(2):
                            ins = pe.matmul(PS[:, (J["peer"] + 2 * t + m) % 8, :], DIAG[:, b % 2, k, :],
                                            vbuf[n][:, m * BANK:(m + 1) * BANK], start=False, stop=False, skip_group_check=True)
                    ins.then_inc(sem("rows_summed"), 1)

            for t in range(TT):
                accs = [bank(J["peer"] + 2 * t + m) for m in range(2)]
                for acc in accs:
                    pe.matmul(acc, zeros, C[:, 0:BANK], start=True, stop=False, skip_group_check=True)
                with pe.Fori(t * PH // 2, (t + 1) * PH // 2) as i:
                    sum_rows(i * 2, t)
                    sum_rows(i * 2 + 1, t)
                for acc in accs:
                    pe.matmul(acc[:, 0:P], zeros, ident, start=False, stop=True, skip_group_check=True).then_inc(pe_done, 1)

            norm(2)
            dense("ab", 7, END["norm2"])
            qk_T(J["sb_T"], 4, lambda t, j: proj_ab[:, t, j * P:(j + 1) * P], 4)
            for m in range(4):
                b = bank(J["sb_Z"] + m)
                for n in range(2):
                    h = 2 * m + n
                    ins = pe.matmul(b[:, n * S:(n + 1) * S], KZT[:, h, 0:P], QT[:, h // 2, :], start=True, stop=True)
                ins.then_inc(pe_done, 1)
            for m in range(2):
                b = bank(J["sb_Z"] + 4 + m)
                for n in range(4):
                    h = 4 * m + n
                    ins = pe.matmul(b[:, n * P:(n + 1) * P], KZT[:, h, P:S], QT[:, h // 2, P:S], start=True, stop=True)
                ins.then_inc(pe_done, 1)
            pe.wait_ge(sem("sb_plus"), 2)
            for m in range(4):
                b = bank(J["sb_C"] + m)
                pe.matmul(b, incl, B[:, m * BANK:(m + 1) * BANK], start=True, stop=False, skip_group_check=True)
                pe.matmul(b.rearrange("p (h t) -> p h t", h=2)[:, :, P:S], ones, L1[:, 2 * m:2 * m + 2, :],
                          start=False, stop=True, skip_group_check=True).then_inc(pe_done, 1)
            for m in range(2):
                b = bank(J["sb_C"] + 4 + m)
                pe.matmul(b, incl, B[:, 2048 + m * BANK:2048 + (m + 1) * BANK], start=True, stop=True).then_inc(pe_done, 1)
            pe.wait_ge(sem("sb_exp"), 2)
            for t in range(TT):
                b = bank(J["sb_O"] + t)
                for h in range(8):
                    vals = lambda k: proj_ab[:, k, 1024 + h * HD:1024 + (h + 1) * HD]
                    ins = pe.matmul(b[:, h * HD:(h + 1) * HD], Z0[:, h, t * P:(t + 1) * P], vals(0), start=True, stop=(t == 0))
                    if t:
                        ins = pe.matmul(b[:, h * HD:(h + 1) * HD], Z1[:, h, :], vals(1), start=False, stop=True)
                ins.then_inc(pe_done, 1)

            pe.wait_ge(sem("h_logf"), 1)
            for m in range(2):
                b = bank(J["hg_B"] + m)
                for n in range(2):
                    for t in range(TT):
                        h = 2 * m + n
                        ins = pe.matmul(b[:, n * S + t * P:n * S + (t + 1) * P], proj_ab[:, t, 2048 + h * P:2048 + (h + 1) * P],
                                        cum, start=True, stop=True)
                ins.then_inc(pe_done, 1)
            for t in range(TT):
                pe.matmul(bank(J["hg_suf"] + t), suf, proj_ab[:, t, 2048:2560], start=True, stop=True).then_inc(pe_done, 1)
            pe.wait_ge(sem("h_silu"), 1)
            for m in range(2):
                transposes(J["hg_T"] + m, [proj_ab[:, t, 1536 + (2 * m + c) * P:1536 + (2 * m + c + 1) * P]
                                           for c in range(2) for t in range(TT)])
            for m in range(2):
                transposes(J["hg_T"] + 2 + m, [hKK[:, t, (2 * m + c) * P:(2 * m + c + 1) * P] for c in range(2) for t in range(TT)])
            pe.wait_ge(evac_done, END["hg_T"])
            for t in range(TT):
                b = bank(J["hg_D"] + t)
                for h in range(4):
                    o = h * S + t * P
                    ins = pe.matmul(b[:, h * P:(h + 1) * P], hKT[:, o:o + P], hQT[:, o:o + P], start=True, stop=True)
                ins.then_inc(pe_done, 1)
            for n in range(len(LEVELS)):
                pe.wait_ge(sem("h_lev"), 2 * n + 2)
                e = hE0 if n % 2 == 0 else hE1
                for t in range(TT):
                    b = bank(J["hg_L"] + 2 * n + t)
                    for h in range(4):
                        o = h * S + t * P
                        ins = pe.matmul(b[:, h * P:(h + 1) * P], e[:, o:o + P], e[:, o:o + P], start=True, stop=True)
                    ins.then_inc(pe_done, 1)
            pe.wait_ge(sem("h_qb"), 1)
            recurrence(J["hg_U"], J["hg_O"], 1,
                       lambda c, h: KSC[:, c, h * P:(h + 1) * P],
                       lambda t, h: proj_ab[:, t, 2560 + h * P:2560 + (h + 1) * P],
                       lambda t, h, par: hQT[:, h * S + t * P + par * CH:h * S + t * P + (par + 1) * CH])
            pe.wait_ge(sem("mixed"), 2)
            norm_T(J["mix1"])
            dense("about", 2, END["mix1"])

            def ffn(l, k):
                norm(k)
                pe.wait_ge(evac_done, END[f"norm{k}"])
                j0 = J[f"up{l}"]
                with pe.Fori(0, FT // 2) as i:
                    for q in range(2):
                        pe.wait_ge(up_loaded[q], i * 32 + (32 * (FT // 2) * l + 32))
                        pe.wait_ge(evac_done, i * 2 + (j0 + q - 1))
                        for g in range(2):
                            for c in range(KC):
                                ins = pe.matmul(PS[:, (j0 + q) % 8, g * S:(g + 1) * S], UP[q][:, c, g, :], XNT[:, c, :],
                                                start=(c == 0), stop=(c == KC - 1))
                        ins.then_inc(pe_done, 1)
                pe.wait_ge(evac_done, END[f"up{l}"])
                pe.wait_ge(sem("down_loaded"), 16 * (FT // 2) * (l + 1))
                pe.wait_ge(sem("hidden_ready"), FT * (l + 1))
                j1 = J[f"down{l}"]
                for c in range(FT):
                    for t in range(TT):
                        for m in range(2):
                            ins = pe.matmul(PS[:, (j1 + 2 * t + m) % 8, :], HT[:, c, t * P:(t + 1) * P],
                                            WD[:, c, m * BANK:(m + 1) * BANK], start=(c == 0), stop=(c == FT - 1))
                            if c == FT - 1:
                                ins.then_inc(pe_done, 1)
                    if c in (3, 7, 11):
                        ins.then_inc(sem("down_rows"), 1)

            def ple(l, k):
                norm(k)
                pe.wait_ge(sem("p_loaded"), 16 + 16 * l)
                transposes(J[f"pT{l}"], [PIN[:, l, t, c * P:(c + 1) * P] for c in range(2) for t in range(TT)])
                dense(f"gate{l}", 2, END[f"norm{k}"])
                loaded(f"proj{l}", 0)
                pe.wait_ge(evac_done, END[f"pT{l}"])
                wp = slot[SLOT_OF[f"proj{l}", 0]][:, 0:2 * D].rearrange("p (c n) -> p c n", c=2)
                for t in range(TT):
                    for m in range(2):
                        b = bank(J[f"proj{l}"] + 2 * t + m)
                        for c in range(2):
                            ins = pe.matmul(b, PINT[:, c, t * P:(t + 1) * P], wp[:, c, m * BANK:(m + 1) * BANK],
                                            start=(c == 0), stop=(c == 1))
                        ins.then_inc(pe_done, 1)

            ffn(0, 3)
            ple(0, 4)
            norm(5)
            dense("c", 3, END["norm5"])
            qk_T(J["sw_T"], 8, lambda t, j: proj_c[:, t, j * P:(j + 1) * P], 6)
            for u in range(4):
                t, g = u // 2, u % 2
                softmax_unit({k: J[f"sw_{k}{u}"] for k in "LPO"}, t, 3 + u,
                             lambda h, g=g: (8 * g + h) // 2, lambda h, g=g: ((8 * g + h) // 4) * 2 + h % 2,
                             lambda k, h, g=g: proj_c[:, k, 1280 + ((8 * g + h) // 4) * HD:1280 + ((8 * g + h) // 4 + 1) * HD])
            pe.wait_ge(sem("mixed"), 3)
            norm_T(J["mix2"])
            dense("cout", 2, END["mix2"])
            ffn(1, 6)
            ple(1, 7)


_INS = ['x', 'norm1_w', 'w_in', 'gla_w_alpha', 'gla_b_alpha', 'gla_out_norm_w', 'moba_q_norm_w', 'moba_k_norm_w',
        'mix_scale', 'w_out', 'norm2_w', 'peer_w_query', 'peer_subkeys', 'peer_u', 'peer_v', 'p_2', 'mix_norm_2',
        'ab_w_in_2', 'hg_out_norm_2', 'ab_w_out_2', 'c_w_in_2', 'q_norm_2', 'k_norm_2', 'sinks_2',
        'rel_bias_2', 'c_w_out_2', 'ffn_norm_2', 'ffn_up_2', 'ffn_conv_2', 'ffn_conv_b_2', 'ffn_down_2',
        'ple_norm_2', 'ple_gate_2', 'ple_proj_2']


def kernel(**inputs):
    import numpy as _np
    import concourse.bacc as _bacc
    from concourse.bass_utils import run_bass_kernel_spmd as _run

    nc = _bacc.Bacc("TRN2", target_bir_lowering=False, num_devices=1)
    small, at, levels, onehot, outside = shape_constants()
    arrays, aps = {}, {}
    given = [(n, _np.ascontiguousarray(inputs[n])) for n in _INS]
    given += [("c_small", small), ("c_levels", levels), ("c_onehot", onehot), ("c_outside", outside)]
    for name, arr in given:
        arrays[f"in_{name}"] = arr
        aps[name] = nc.dram_tensor(f"in_{name}", arr.shape, mybir.dt.from_np(arr.dtype), kind="ExternalInput").ap()
    out = nc.dram_tensor("out_0", (1, S, D), F32, kind="ExternalOutput").ap()
    build(nc, aps, out, at)
    r = _run(nc, [arrays], core_ids=[0])
    return r.results[0]["out_0"]
```

```python
from contextlib import ExitStack

import numpy as np

import concourse.bass as bass
from concourse import mybir

F32 = mybir.dt.float32
F32R = mybir.dt.float32r
U32 = mybir.dt.uint32
ALU = mybir.AluOpType
ACT = mybir.ActivationFunctionType
AX = mybir.AxisListType.X

P = 128
D = 1024
S = 256
TT = S // P
KC = D // P
EPS = 1e-6
NEG = -1e30
GH, GDK, GDV, GRANK, CH = 4, 64, 128, 16, 64
MH, HD = 8, 64
PH, NKEYS, TOPK = 8, 128, 16
UNITS = TT * PH
SWH, SWKV, WIN, NBUCK = 16, 4, 128, 32
DFF = 2816
FT = DFF // P
PLE = 256
LEVELS = [1, 2, 4, 8, 16, 32]
BANK = 512

PLAN = [("vecs", 1), ("norm0", 4), ("conv", 1), ("relb", 1), ("win", 12), ("gr", 1),
        ("alpha", 1), ("mb_T", 4), ("mb_L0", 2), ("gla_cum", 2), ("gla_dec", 1), ("mb_L1", 4), ("gla_T", 2),
        ("mb_P0", 2), ("mb_O0", 1), ("gla_A", 2), ("gla_U", 3), ("mb_P1", 4), ("mb_O1", 1), ("gla_O", 2),
        ("mix0", 4), ("wout", 4), ("subk", 4), ("norm1", 4), ("query", 3), ("score", 1), ("query_rest", 5), ("score_rest", 7),
        ("peer", 4),
        ("norm2", 4), ("ab", 14), ("sb_T", 4), ("sb_Z", 6), ("hg_B", 2), ("hg_suf", 2), ("hg_T", 4), ("hg_D", 2), ("sb_C", 6),
        ("hg_L0", 2), ("hg_L1", 2), ("sb_O", 2), ("hg_L2", 2), ("hg_L3", 2), ("hg_L4", 2), ("hg_U", 3), ("hg_L5", 2), ("hg_O", 2),
        ("mix1", 4), ("about", 4), ("norm3", 4), ("up0", FT), ("down0", 4), ("norm4", 4), ("pT0", 1), ("gate0", 4),
        ("proj0", 4),
        ("norm5", 4), ("c", 6), ("sw_T", 6)]
SW_UNITS = 4
PLAN += [("sw_L0", 2)]
for _u in range(SW_UNITS):
    PLAN += [(f"sw_L{_u + 1}", 2 if _u + 1 < 2 else 4)] if _u + 1 < SW_UNITS else []
    PLAN += [(f"sw_P{_u}", 2 if _u < 2 else 4), (f"sw_O{_u}", 1)]
PLAN += [("mix2", 4), ("cout", 4), ("norm6", 4), ("up1", FT), ("down1", 4), ("norm7", 4), ("pT1", 1), ("gate1", 4),
         ("proj1", 4)]
J, N = {}, {}
_at = 0
for _name, _n in PLAN:
    J[_name], N[_name] = _at, _n
    _at += _n

END = {k: J[k] + N[k] for k in J}


def query_job(m):
    return J["query"] + m if m < 3 else J["query_rest"] + m - 3


def score_job(m):
    return J["score"] if m == 0 else J["score_rest"] + m - 1


def shape_constants():
    i = np.arange(P)
    s, t = i[:, None], i[None, :]
    same = (s // CH) == (t // CH)
    cols, at = [], {}

    def put(name, a):
        at[name] = (sum(c.shape[1] for c in cols), a.shape[1])
        cols.append(a.astype(np.float32))

    put("ident", np.eye(P))
    put("cum", same & (s <= t))
    put("suf", same & (s > t))
    put("incl", s >= t)
    put("ones", np.ones((P, P)))
    put("before", s < t)
    put("before_add", np.where(s < t, 0.0, NEG))
    put("causal_add", np.concatenate([np.zeros((P, P)), np.where(t <= s, 0.0, NEG)], 1))
    half = HD // 2
    inv = (np.float32(10000.0) ** (-np.arange(half, dtype=np.float32) / np.float32(half))).astype(np.float32)
    pos = np.arange(S, dtype=np.float32).reshape(TT, P)
    ang = pos[:, :, None] * inv[None, None, :]
    put("cos", np.cos(ang).transpose(1, 0, 2).reshape(P, -1))
    put("sin", np.sin(ang).transpose(1, 0, 2).reshape(P, -1))
    put("head_rows", np.stack([(i // GDK) == (h % 2) for h in range(GH)], 1))
    put("chunk_rows", np.stack([(i // CH) == c for c in range(2)], 1))
    put("iota", np.tile(np.arange(TOPK), (P, 1)))
    small = np.concatenate(cols, 1)
    levels = []
    for half_block in LEVELS:
        b = 2 * half_block
        levels.append((s // b == t // b) & (s % b < half_block) & (t % b >= half_block))
    levels = np.concatenate(levels, 1).astype(np.float32)
    u = np.arange(3 * P)
    dist = 2 * WIN - 1 - u
    band = (dist >= 0) & (dist < WIN)
    exact = NBUCK // 2
    large = exact + (np.log(np.maximum(dist, exact) / exact) / np.log(WIN / exact) * (NBUCK - exact)).astype(np.int32)
    bucket = np.where(dist < exact, np.maximum(dist, 0), np.minimum(large, NBUCK - 1))
    onehot = ((np.arange(NBUCK)[:, None] == bucket[None, :]) & band[None, :]).astype(np.float32)
    outside = np.tile(np.where(band, 0.0, NEG), (SWH, 1)).astype(np.float32)
    return small, at, levels, onehot, outside


def build(nc, a, out, at):
    ctx = ExitStack()
    with ctx:
        sems = {}

        def sem(name):
            if name not in sems:
                sems[name] = ctx.enter_context(nc.semaphore(name))
            return sems[name]

        def sb(name, shape, dt=F32):
            return ctx.enter_context(nc.sbuf_tensor(name, shape, dt))

        SLOT, HALF = 4096, 2048
        O_RAW, O_HI, O_LO, O_SCR, O_XN, O_X, O_T, O_PROJ, O_A, O_B, O_END = np.cumsum(
            [0, 2 * SLOT, 2 * SLOT, 2 * SLOT, 4096, TT * D, TT * D, KC * S, 7168, 4096, 4096]).tolist()
        base = -(-nc.sbuf_base // 64) * 64
        sb("arena", [P, O_END])

        def place(name, shape, col, dt=F32):
            return nc.alloc_sbuf_tensor_at(name, shape, dt, offset=base + 4 * col)

        RAW = place("weights_raw", [P, 2 * SLOT], O_RAW)
        WHI = place("weights_hi", [P, 2 * SLOT], O_HI, F32R)
        WLO = place("weights_lo", [P, 2 * SLOT], O_LO, F32R)
        ROWS = place("expert_rows", [P, 6 * SLOT], O_RAW)
        SCR = place("scratch", [P, 4096], O_SCR)
        XN = place("x_norm", [P, TT, D], O_XN)
        X = place("x_res", [P, TT, D], O_X)
        T = place("work_t", [P, KC * S], O_T)
        XHI = place("x_normT_hi", [P, KC, S], O_T, F32R)
        XLO = place("x_normT_lo", [P, KC, S], O_B + 2048, F32R)
        PROJ = place("proj", [P, 7168], O_PROJ)
        HHI = place("hidden_hi", [P, FT, S], O_PROJ, F32R)
        HLO = place("hidden_lo", [P, FT, S], O_SCR, F32R)
        A = place("work_a", [P, 4096], O_A)
        B = place("work_b", [P, 4096], O_B)
        PHI = place("ple_hi", [P, 2, S], O_B + 1024, F32R)
        PLO = place("ple_lo", [P, 2, S], O_B + 1536, F32R)
        C = sb("consts", [P, sum(n for _, n in at.values())])
        VEC = sb("vec_cols", [P, 72])
        CONV = sb("conv_cols", [P, 2, 4 * 2 * FT])
        GAIN = sb("gain_rows", [P, 2 * GDV + 4 * HD])
        ALB = sb("alpha_bias", [P, GH * GDK])
        SINK = sb("sink_rows", [P, SWH])
        SS = sb("stats", [P, 104])
        PS = ctx.enter_context(nc.psum_tensor("ps", [P, 8, BANK], F32))

        def const(name):
            o, n = at[name]
            return C[:, o:o + n]

        ident, cum, suf, incl, ones = (const(n) for n in ("ident", "cum", "suf", "incl", "ones"))
        causal_add = const("causal_add")
        zeros = causal_add[:, 0:P]
        NORM_COL = {0: 0, 1: None, 2: 8, 3: 24, 4: 40, 5: 16, 6: 32, 7: 48}
        MIX_COL = {0: 56, 1: None, 2: None}
        LB_GAIN, HG_GAIN = GAIN[:, 0:GDV], GAIN[:, GDV:2 * GDV]
        QK_GAIN = [GAIN[:, 2 * GDV + n * HD:2 * GDV + (n + 1) * HD] for n in range(4)]

        proj_in = PROJ[:, 0:6144].rearrange("p (t n) -> p t n", t=TT)
        proj_ab = PROJ[:, 0:7168].rearrange("p (t n) -> p t n", t=TT)
        proj_c = PROJ[:, 0:3072].rearrange("p (t n) -> p t n", t=TT)
        BIAS = PROJ[:, 3072:7168].rearrange("p (h s) -> p h s", h=SWH)
        KDUP = T[:, 0:1024].rearrange("p (t h d n) -> p t h d n", t=TT, h=SWKV, d=2)
        KZT = B[:, 0:2048].rearrange("p (v t) -> p v t", v=8)
        QT = B[:, 2048:4096].rearrange("p (v t) -> p v t", v=8)
        PB = [A[:, 0:2048], SCR[:, 0:2048]]
        PT = A[:, 2048:4096].rearrange("p (b t) -> p b t", t=P)
        M0, M1, M2 = (ROWS[:, n * SLOT:(n + 1) * SLOT] for n in (1, 3, 5))
        ST = M1[:, 0:1536].rearrange("p (c h v) -> p c h v", c=3, h=4)
        KSC = M1[:, 1536:3072].rearrange("p (c n) -> p c n", c=3)
        LEV = SCR[:, 3328:4096].rearrange("p (l t) -> p l t", l=6)
        AT = M2[:, 0:1024].rearrange("p (t h n) -> p t h n", t=TT, h=4)
        OUTN = M2[:, 1024:2048].rearrange("p (t n) -> p t n", t=TT)
        SQ = M2[:, 2048:3072].rearrange("p (t n) -> p t n", t=TT)
        DEC = SS[:, 56:64]
        W_GR = SCR[:, 2048:2048 + KC * GRANK].rearrange("p (c n) -> p c n", c=KC)
        W_ALPHA = SCR[0:GRANK, 2176:2432]
        GRT = SCR[0:GRANK, 2432:2688]
        gG, gE, gB_, gS = (M0[:, n * 512:(n + 1) * 512] for n in range(4))
        gKST = T[:, 1024:1536].rearrange("p (t n) -> p t n", t=TT)
        gKN = T[:, 0:512].rearrange("p (t n) -> p t n", t=TT)
        gKZT = M0[:, 2048:3072].rearrange("p (h t) -> p h t", h=4)
        gQT = M2[:, 3072:3584].rearrange("p (j t) -> p j t", j=2)
        gDECR = M0[:, 3584:3592]
        OH = B[0:NBUCK, 0:384]
        RB = B[0:NBUCK, 384:400]
        OUTSIDE = B[0:SWH, 400:784]
        BROW = B[0:SWH, 784:1168]
        VROW = B[0:72, 1200:1328]
        CROW = [B[0:2 * 2 * FT, 1328 + P * n:1328 + P * (n + 1)] for n in range(4)]
        qT = A[:, :].rearrange("p (u t) -> p u t", u=16)
        SKN = SCR[:, 0:2048].rearrange("p (u n) -> p u n", u=16)
        SKT = B[:, 0:2048].rearrange("p (u n) -> p u n", u=16)
        SCORE = PROJ[:, 0:4096]
        N2W = PROJ[:, 4096:5120]
        DIAG = PROJ[:, 5120:6144].rearrange("p (q k n) -> p q k n", q=2, k=4)
        R = PROJ[:, 6144:7168]
        r_s = R[:, 0:256].rearrange("p (q n) -> p q n", q=2)
        r_w = R[:, 256:512]
        r_cand = R[:, 512:768]
        r_sv = R[:, 768:800].rearrange("p (q n) -> p q n", q=2)
        r_top = R[:, 800:816]
        r_sum = R[:, 816:817]
        r_rs = R[:, 817:818]
        r_e = R[:, 820:836]
        r_gate = R[:, 836:868].rearrange("p (q n) -> p q n", q=2)
        r_dot = R[:, 868:876].rearrange("p (q n) -> p q n", q=2)
        r_act = R[:, 876:884].rearrange("p (q n) -> p q n", q=2)
        r_wt = R[:, 884:892].rearrange("p (q n) -> p q n", q=2)
        r_i = R[:, 892:924].rearrange("p (q n) -> p q n", q=2)
        RI = sb("route_idx", [P, 96], U32)
        r_si = RI[:, 0:32].rearrange("p (q n) -> p q n", q=2)
        r_pos = RI[:, 32:48]
        r_hi, r_lo = RI[:, 48:56], RI[:, 56:64]
        r_ab = sb("route_ab", [P, 32], U32)
        r_idx = RI[:, 64:96].rearrange("p (q n) -> p q n", q=2)
        NU, NV = 8, 16
        ubuf = [ROWS[:, n * D:(n + 1) * D] for n in range(NU)]
        vbuf = [ROWS[:, (NU + n) * D:(NU + n + 1) * D] for n in range(NV)]
        Z0 = A[:, 0:2048].rearrange("p (h t) -> p h t", h=8)
        Z1 = A[:, 2048:3072].rearrange("p (h t) -> p h t", h=8)
        L0 = B[:, 0:2048].rearrange("p (h t) -> p h t", h=8)
        L1 = B[:, 2048:3072].rearrange("p (h t) -> p h t", h=8)
        hBT, hKT, hE0, hE1 = (M0[:, n * 1024:(n + 1) * 1024] for n in range(4))
        hQT = M1[:, 3072:4096]
        hQB = B[:, 3072:4096]
        hTMP = M2[:, 3072:4096].rearrange("p (t h n) -> p t h n", t=TT, h=4)
        hLN = SCR[:, 0:1024].rearrange("p (t n) -> p t n", t=TT)
        hT0 = SCR[:, 1024:2048]
        hKK = A[:, 3072:4096].rearrange("p (t n) -> p t n", t=TT)
        hKST = T[:, 0:1024].rearrange("p (t n) -> p t n", t=TT)
        hSF = T[:, 1024:2048].rearrange("p (t n) -> p t n", t=TT)
        CT = A[:, 0:2048].rearrange("p (q n) -> p q n", q=4)
        GATE = A[:, 2048:4096].rearrange("p (t n) -> p t n", t=TT)
        PIN = B[:, 0:1024].rearrange("p (l t n) -> p l t n", l=2, t=TT)

        PER = 3 * P - 1
        bias_scratch = nc.dram_tensor("bias_scratch", (SWH, P * PER), F32, kind="Internal").ap()

        pe_done, evac_done = sem("pe_done"), sem("evac_done")
        raw_loaded = [sem(f"raw_loaded{h}") for h in range(4)]
        hi_ready = [sem(f"hi_ready{h}") for h in range(4)]
        lo_ready = [sem(f"lo_ready{h}") for h in range(4)]
        u_loaded = [sem(f"u_loaded{n}") for n in range(NU)]
        v_loaded = [sem(f"v_loaded{n}") for n in range(NV)]

        def cols512(m, c0, n=512):
            return m[:, c0:c0 + n].rearrange("(c p) n -> p c n", p=P)

        w_in, ab_in, c_in = a["w_in"][0], a["ab_w_in_2"][0], a["c_w_in_2"][0]
        up_w, down_w = a["ffn_up_2"], a["ffn_down_2"]
        FP = FT // 2
        in_cols = [0, 512, 1024, 1552, 2064, 2576]
        PIECES = [("win", n, (2 * (n % 2), 4), cols512(w_in, c)) for n, c in enumerate(in_cols)]
        PIECES += [("wout", n, (2 * (n % 2), 4), cols512(a["w_out"][0], 512 * n)) for n in range(2)]
        PIECES += [("query", n, (2 * (n % 2), 4), cols512(a["peer_w_query"][0], 512 * n)) for n in range(4)]
        PIECES += [("ab", n, (2 * (n % 2), 4), cols512(ab_in, 512 * n)) for n in range(7)]
        PIECES += [("about", n, (2 * n, 4), cols512(a["ab_w_out_2"][0], 512 * n)) for n in range(2)]

        RING = 4
        UP_BODIES = FT // RING

        def ffn_and_ple(l):
            off = 2 * l
            down = [(f"down{l}", n, ((off + FT + n) % RING, 2), down_w[l, n * 2 * P:(n + 1) * 2 * P].rearrange("(c p) n -> p c n", p=P))
                    for n in range(FP)]
            up = [(f"up{l}", n, ((off + n) % RING, 2), None) for n in range(FT)]
            return up + down + [(f"gate{l}", n, (2 * ((n + 1 - l) % 2), 4), cols512(a["ple_gate_2"][l], 512 * n)) for n in range(2)] + [
                (f"proj{l}", 0, (2 - 2 * l, 2), a["ple_proj_2"][l].rearrange("(c p) n -> p c n", p=P))]

        PIECES += ffn_and_ple(0)
        PIECES += [("c", n, (2 * (n % 2), 4), cols512(c_in, 512 * n)) for n in range(3)]
        PIECES += [("cout", n, (2 - 2 * n, 4), cols512(a["c_w_out_2"][0], 512 * n)) for n in range(2)]
        PIECES += ffn_and_ple(1)

        class Piece:
            pass

        pieces, holder, uses, dmas = {}, [None] * 4, [0] * 4, [0] * 4
        for name, n, (h, size), src in PIECES:
            w = Piece()
            w.h, w.src, w.cols = h, src, slice(h * HALF, h * HALF + (SLOT if size == 4 else HALF))
            covered = range(h, h + (2 if size == 4 else 1))
            w.before = [x for x in dict.fromkeys(holder[c] for c in covered) if x is not None]
            uses[h] += 1
            dmas[h] += 2 if name.startswith("up") else 1
            w.count, w.landed = uses[h], 16 * dmas[h]
            if name.startswith("down"):
                w.used = (sem("down_used"), (FP - 1) * int(name[-1]) + n + 1) if n < FP - 1 else (pe_done, END[name])
            elif name.startswith("up"):
                w.used = (pe_done, J[name] + n + 1)
            elif name == "query":
                w.used = (pe_done, query_job(2 * n + 1) + 1)
            else:
                w.used = (pe_done, min(J[name] + 2 * n + 2, END[name]) if not name.startswith("proj") else END[name])
            for c in covered:
                holder[c] = (name, n)
            pieces[name, n] = w

        def part(t, w, c=KC):
            return t[:, w.cols].rearrange("p (c n) -> p c n", c=c)

        def split_hi(eng, copy, name, n):
            w = pieces[name, n]
            eng.wait_ge(raw_loaded[w.h], w.landed)
            for b in w.before:
                eng.wait_ge(*pieces[b].used)
            copy(WHI[:, w.cols], RAW[:, w.cols]).then_inc(hi_ready[w.h], 1)

        def split_lo(eng, name, n):
            w = pieces[name, n]
            eng.wait_ge(raw_loaded[w.h], w.landed)
            eng.wait_ge(hi_ready[w.h], w.count)
            eng.tensor_tensor(WLO[:, w.cols], RAW[:, w.cols], WHI[:, w.cols].bitcast(F32), ALU.subtract).then_inc(lo_ready[w.h], 1)

        def ATT(u):
            return SS[:, 8 + 24 * (u % 2):32 + 24 * (u % 2)]

        block = ctx.enter_context(nc.Block())

        @block.sync
        def _(sp):
            def free(name, n):
                for b in pieces[name, n].before:
                    sp.wait_ge(hi_ready[pieces[b].h], pieces[b].count)
                    sp.wait_ge(lo_ready[pieces[b].h], pieces[b].count)

            def load(name, n):
                w = pieces[name, n]
                free(name, n)
                sp.dma_start(part(RAW, w, w.src.shape[1]), w.src).then_inc(raw_loaded[w.h], 16)

            sp.dma_start(X[:, :, :], a["x"][0].rearrange("(t p) d -> p t d", p=P)).then_inc(sem("x_loaded"), 16)
            sp.dma_start(C[:, :], a["c_small"]).then_inc(sem("const_loaded"), 16)
            rows = [("norm1_w", 8), ("mix_norm_2", 16), ("ffn_norm_2", 16), ("ple_norm_2", 16), ("mix_scale", 8)]
            r = 0
            for name, n in rows:
                sp.dma_start(VROW[r:r + n, :], a[name].rearrange("l (c p) -> (l c) p", p=P)).then_inc(sem("vec_loaded"), 16)
                r += n
            load("win", 0)
            for l in range(2):
                taps = a["ffn_conv_2"][l].rearrange("k (c p) -> (k c) p", p=P)
                sp.dma_start(CROW[2 * l][:, :], taps[0:4 * FT, :]).then_inc(sem("conv_loaded"), 16)
                sp.dma_start(CROW[2 * l + 1][0:2 * FT, :], taps[4 * FT:6 * FT, :]).then_inc(sem("conv_loaded"), 16)
                sp.dma_start(CROW[2 * l + 1][2 * FT:4 * FT, :],
                             a["ffn_conv_b_2"][l:l + 1, :].rearrange("k (c p) -> (k c) p", p=P)).then_inc(sem("conv_loaded"), 16)
            sp.dma_start(OH, a["c_onehot"]).then_inc(sem("rel_loaded"), 16)
            sp.dma_start(RB, a["rel_bias_2"]).then_inc(sem("rel_loaded"), 16)
            sp.dma_start(OUTSIDE, a["c_outside"]).then_inc(sem("rel_loaded"), 16)
            load("win", 1)
            sp.dma_start(W_GR, cols512(w_in, 1536, GRANK)).then_inc(sem("gr_loaded"), 16)
            sp.dma_start(W_ALPHA, a["gla_w_alpha"][0]).then_inc(sem("gr_loaded"), 16)
            for dst, src in ((LB_GAIN, a["gla_out_norm_w"]), (HG_GAIN, a["hg_out_norm_2"]), (QK_GAIN[0], a["moba_q_norm_w"]),
                             (QK_GAIN[1], a["moba_k_norm_w"]), (QK_GAIN[2], a["q_norm_2"]), (QK_GAIN[3], a["k_norm_2"]),
                             (ALB[:, :], a["gla_b_alpha"]), (SINK[:, :], a["sinks_2"])):
                sp.dma_start(dst, src[0].partition_broadcast(P)).then_inc(sem("gain_loaded"), 16)
            sp.dma_start(SCR[:, 3328:4096], a["c_levels"]).then_inc(sem("levels_loaded"), 16)
            for n in range(2, 4):
                load("win", n)
            sp.wait_ge(evac_done, END["relb"])
            sp.dma_start(bias_scratch.rearrange("h (t u) -> h t u", u=PER),
                         BROW[:, 0:PER].unsqueeze(1).broadcast_to([SWH, P, PER])).then_inc(sem("bias_written"), 16)
            for n in range(4, 6):
                load("win", n)
            load("wout", 0)
            sp.wait_ge(pe_done, END["gla_A"])
            sp.wait_ge(sem("g_exp"), 4)
            load("wout", 1)
            for n in range(2):
                load("query", n)
            sp.wait_ge(evac_done, END["mb_O1"])
            sp.dma_start(N2W, a["norm2_w"][0].partition_broadcast(P)).then_inc(sem("n2w_loaded"), 16)
            sp.dma_start(SKN, a["peer_subkeys"][0].rearrange("h q k d -> k (h q) d")).then_inc(sem("subkeys_loaded"), 16)
            for n in range(2, 4):
                load("query", n)
            sp.wait_ge(sem("dots_done"), 4 * UNITS)
            for n in range(7):
                load("ab", n)
            load("about", 0)
            sp.wait_ge(pe_done, END["hg_L5"])
            sp.wait_ge(sem("h_bexp"), 1)
            load("about", 1)

            def ffn_loads(l):
                def load_up(h, col):
                    src = up_w[l].rearrange("(c p) (g n) -> p c g n", p=P, g=2)
                    dst = RAW[:, h * HALF:(h + 1) * HALF].rearrange("p (c g n) -> p c g n", c=KC, g=2)
                    for g in range(2):
                        sp.dma_start(dst[:, :, g, :], src[:, :, g, bass.ds(col, P)]).then_inc(raw_loaded[h], 16)

                def peeled(n):
                    free(f"up{l}", n)
                    load_up(pieces[f"up{l}", n].h, n * P)

                for n in range(RING):
                    peeled(n)
                with sp.Fori(1, UP_BODIES) as i:
                    for q in range(RING):
                        w = pieces[f"up{l}", q]
                        sp.wait_ge(hi_ready[w.h], i + (w.count - 1))
                        sp.wait_ge(lo_ready[w.h], i + (w.count - 1))
                        load_up(w.h, i * (RING * P) + q * P)
                for n in range(RING * UP_BODIES, FT):
                    peeled(n)
                for n in range(FP):
                    load(f"down{l}", n)
                load(f"gate{l}", 0)

            def ple_loads(l):
                sp.dma_start(PIN[:, l], a["p_2"][l, 0].rearrange("(t p) n -> p t n", p=P)).then_inc(sem("p_loaded"), 16)
                load(f"gate{l}", 1)
                load(f"proj{l}", 0)

            ffn_loads(0)
            ple_loads(0)
            for n in range(3):
                load("c", n)
            sp.wait_ge(sem("bias_written"), 16)
            sp.wait_ge(pe_done, END["down0"])
            sp.dma_start(BIAS, bass.AP(bias_scratch.tensor, P - 1, [[PER - 1, P], [P * PER, SWH], [1, 2 * P]])
                         ).then_inc(sem("bias_loaded"), 16)
            for n in range(2):
                load("cout", n)
            ffn_loads(1)
            ple_loads(1)
            for t in range(TT):
                sp.wait_ge(sem("x_final"), t + 1)
                sp.dma_start(out[0, t * P:(t + 1) * P, :], X[:, t, :]).then_inc(sem("out_written"), 16)
            sp.wait_ge(sem("out_written"), 16 * TT)

        @block.gpsimd
        def _(pool):
            def split(name, n):
                split_lo(pool, name, n)

            split("win", 1)
            split("wout", 0)
            pool.wait_ge(sem("mixed"), TT)
            split("wout", 1)
            for n in range(2):
                split("query", n)

            def unit(u, q, first=False):
                def hold(s, value):
                    pool.wait_ge(sem(s), value)
                    if not isinstance(value, int):
                        pool.sem_inc(sem("gather_holds"))

                hold("idx_ready", u + 1)
                if first:
                    for n in (2, 3):
                        w = pieces["query", n]
                        pool.wait_ge(hi_ready[w.h], w.count)
                        pool.wait_ge(lo_ready[w.h], w.count)
                for b in range(4):
                    if not (first and b < 2):
                        hold("dots_done", u * 4 + (b - 1))
                    for k in range(4):
                        n = (4 * b + k) % NU
                        nc.gpsimd.indirect_dma_start(
                            out=ubuf[n], out_offset=None, in_=a["peer_u"][0],
                            in_offset=bass.IndirectOffsetOnAxis(ap=r_idx[:, q, 4 * b + k:4 * b + k + 1], axis=0)
                        ).then_inc(u_loaded[n], 16)
                    if not first:
                        hold("rows_summed", u * 4 + (b - 3))
                    elif b < 2:
                        pool.wait_ge(*pieces["query", 2 + b].used)
                    for k in range(4):
                        n = 4 * b + k
                        nc.gpsimd.indirect_dma_start(
                            out=vbuf[n], out_offset=None, in_=a["peer_v"][0],
                            in_offset=bass.IndirectOffsetOnAxis(ap=r_idx[:, q, n:n + 1], axis=0)
                        ).then_inc(v_loaded[n], 16)

            unit(0, 0, first=True)
            unit(1, 1)
            with pool.Fori(1, UNITS // 2) as i:
                unit(i * 2, 0)
                unit(i * 2 + 1, 1)

            pool.wait_ge(pe_done, END["peer"])
            for n in range(2):
                split("ab", n)
            split("about", 0)
            pool.wait_ge(sem("mixed"), 2 * TT)
            split("about", 1)
            for l in range(2):
                for n in range(RING):
                    split(f"up{l}", n)

                def hidden(i, tiles):
                    for q in range(tiles):
                        pool.wait_ge(sem("silu_done"), i * RING + (FT * l + q + 1))
                        g, u = CT[:, q, 0:S], CT[:, q, S:2 * S]
                        hi = HHI[:, :, :].rearrange("p c t -> p (c t)")[:, bass.ds(i * (RING * S) + q * S, S)]
                        lo = HLO[:, :, :].rearrange("p c t -> p (c t)")[:, bass.ds(i * (RING * S) + q * S, S)]
                        pool.tensor_tensor(hi, g, u, ALU.mult).then_inc(sem("hidden_hi_ready"), 1)
                        pool.tensor_tensor(g, g, u, ALU.mult).then_inc(sem("hidden_full"), 1)
                        pool.wait_ge(sem("hidden_full"), i * RING + (FT * l + q + 1))
                        pool.wait_ge(sem("hidden_hi_ready"), i * RING + (FT * l + q + 1))
                        pool.tensor_tensor(lo, g, hi.bitcast(F32), ALU.subtract).then_inc(sem("hidden_ready"), 1)

                with pool.Fori(0, UP_BODIES) as i:
                    hidden(i, RING)
                hidden(UP_BODIES, FT % RING)
                for n in range(2):
                    split(f"gate{l}", n)
                split(f"proj{l}", 0)
                if l == 0:
                    for name in ("c", "cout"):
                        for n in range(2):
                            split(name, n)

        @block.scalar
        def _(act):
            own = [0]

            def link(ins):
                own[0] += 1
                ins.then_inc(sem("act_chain"), 1)
                act.wait_ge(sem("act_chain"), own[0])

            root_no, rstd = [0], sem("root_done")

            def root(dst, src, n):
                root_no[0] += 1
                act.wait_ge(sem("sumsq_ready"), root_no[0])
                nc.scalar.activation(dst, src, ACT.Sqrt, bias=eps_col, scale=1.0 / n).then_inc(rstd, 1)

            def x_hi(j, col=None):
                for m in range(4):
                    act.wait_ge(pe_done, j + m + 1)
                    for c in range(2):
                        f = 2 * m + c
                        ins = nc.scalar.activation(XHI[:, f, :], PS[:, (j + m) % 8, c * S:(c + 1) * S], ACT.Copy,
                                                   scale=1.0 if col is None else VEC[:, col + f:col + f + 1])
                    ins.then_inc(sem("x_hi_ready"), 1)

            def sqrt_table():
                nc.scalar.activation(SS[:, 94:95], eps_col, ACT.Sqrt)

            rstd_no = [0]

            def norm(k, between=()):
                root(SS[:, 2:4], SS[:, 0:2], D)
                if NORM_COL[k] is not None:
                    rstd_no[0] += 1
                    act.wait_ge(sem("rstd_ready"), rstd_no[0])
                    nc.scalar.activation(XN[:, 1], X[:, 1], ACT.Copy, scale=SS[:, 3:4]).then_inc(sem("xn_ready"), 1)
                for piece in between:
                    split(*piece)
                x_hi(J[f"norm{k}"], NORM_COL[k])

            def split(name, n):
                split_hi(act, act.copy, name, n)

            eps_col = SS[:, 95:96]
            act.wait_ge(sem("eps_ready"), 1)
            sqrt_table()
            norm(0, between=[("win", 0)])
            for n in range(1, 6):
                split("win", n)
            for n in range(2):
                root(SS[:, 56 + 16 * n:72 + 16 * n], SS[:, 8 + 16 * n:24 + 16 * n], HD)

            act.wait_ge(sem("g_abs"), 1)
            link(nc.scalar.activation(gE, gE, ACT.Exp, scale=-1.0))
            nc.scalar.activation(gE, gE, ACT.Ln, bias=1.0).then_inc(sem("g_log"), 1)
            att_no = [0]

            def exp_unit(t, sink=None):
                u, cols = att_no[0], (t + 1) * P
                att_no[0] += 1
                neg_max = ATT(u)[:, 8:16]
                act.wait_ge(sem("att_max"), u + 1)
                for h in range(8):
                    w = PB[u % 2][:, h * cols:(h + 1) * cols]
                    ins = nc.scalar.activation(w, w, ACT.Exp, bias=neg_max[:, h:h + 1])
                ins.then_inc(sem("att_exp"), 1)
                if sink:
                    nc.scalar.activation(ATT(u)[:, 0:8], ATT(u)[:, 0:8], ACT.Exp).then_inc(sem("sink_exp"), 1)

            exp_unit(0)
            act.wait_ge(evac_done, END["gla_cum"])
            nc.scalar.activation(gE, gB_, ACT.Exp).then_inc(sem("g_exp"), 1)
            nc.scalar.activation(gB_, gB_, ACT.Exp, scale=-1.0).then_inc(sem("g_exp"), 1)
            nc.scalar.activation(gS, gS, ACT.Exp).then_inc(sem("g_exp"), 1)
            act.wait_ge(evac_done, END["gla_dec"])
            nc.scalar.activation(DEC, gDECR, ACT.Exp).then_inc(sem("g_exp"), 1)
            exp_unit(1)
            nc.scalar.activation(proj_in[:, :, 1024:1536], proj_in[:, :, 1024:1536], ACT.Silu).then_inc(sem("silu_gate"), 1)
            split("wout", 0)
            sqrt_table()
            root(SS[:, 16:24], SS[:, 8:16], GDV)
            split("wout", 1)
            x_hi(J["mix0"], MIX_COL[0])
            sqrt_table()
            for n in range(2):
                split("query", n)
            norm(1)

            def gate_exp(u):
                act.wait_ge(sem("top_ready"), u + 1)
                nc.scalar.activation(r_e, r_e, ACT.Exp).then_inc(sem("gate_exp"), 1)

            def gelu(u, b):
                act.wait_ge(sem("dots_done"), u * 4 + (b + 1))
                nc.scalar.activation(r_act[:, b % 2], r_dot[:, b % 2], ACT.Gelu).then_inc(sem("gelu_done"), 1)

            def diag(u, b, wait=True):
                act.wait_ge(sem("weights_ready"), u * 4 + (b + 1))
                if wait:
                    act.wait_ge(sem("rows_summed"), u * 4 + (b - 1))
                for k in range(4):
                    ins = nc.scalar.activation(DIAG[:, b % 2, k, :], ident, ACT.Copy, scale=r_wt[:, b % 2, k:k + 1])
                ins.then_inc(sem("diag_ready"), 1)

            def act_unit(u, first=False, last=False):
                for b in range(4):
                    gelu(u, b)
                    if b > 0:
                        diag(u, b - 1, wait=not (first and b <= 2))
                    elif not first:
                        diag(u - 1, 3)
                    if b == 1 and not last:
                        gate_exp(u + 1)

            for n in range(2, 4):
                split("query", n)
            gate_exp(0)
            act_unit(0, first=True)
            act_unit(1)
            with act.Fori(1, UNITS // 2 - 1) as i:
                act_unit(i * 2)
                act_unit(i * 2 + 1)
            act_unit(UNITS - 2)
            act_unit(UNITS - 1, last=True)
            diag(UNITS - 1, 3)

            sqrt_table()
            act.wait_ge(pe_done, END["peer"])
            for n in range(2):
                split("ab", n)
            norm(2)
            for n in range(2, 7):
                split("ab", n)
            hq, hf, hg = proj_ab[:, :, 1536:2048], proj_ab[:, :, 2048:2560], proj_ab[:, :, 3072:3584]
            act.wait_ge(sem("h_abs"), 1)
            nc.scalar.activation(hKK, hf, ACT.Sigmoid, scale=-1.0).then_inc(sem("h_sig"), 1)
            link(nc.scalar.activation(hLN, hLN, ACT.Exp, scale=-1.0))
            nc.scalar.activation(hLN, hLN, ACT.Ln, bias=1.0).then_inc(sem("h_log"), 1)
            nc.scalar.activation(hq, hq, ACT.Silu).then_inc(sem("h_silu"), 1)
            act.wait_ge(evac_done, END["ab"])
            nc.scalar.activation(hg, hg, ACT.Silu).then_inc(sem("h_silu"), 1)
            act.wait_ge(sem("sb_abs"), 1)
            for t in (L0, L1):
                link(nc.scalar.activation(t, t, ACT.Exp, scale=-1.0))
            nc.scalar.activation(L0, L0, ACT.Ln, bias=1.0).then_inc(sem("sb_log"), 1)
            nc.scalar.activation(L1, L1, ACT.Ln, bias=1.0).then_inc(sem("sb_log"), 1)
            act.wait_ge(evac_done, END["hg_suf"])
            nc.scalar.activation(hSF, hSF, ACT.Exp).then_inc(sem("h_sufexp"), 1)
            nc.scalar.activation(hT0, hBT, ACT.Exp).then_inc(sem("h_bexp"), 1)
            for n, L in enumerate(LEVELS):
                act.wait_ge(sem("h_rel"), n + 1)
                e = (hE0 if n % 2 == 0 else hE1).rearrange("p (b i) -> p b i", i=2 * L)
                nc.scalar.activation(e[:, :, L:2 * L], e[:, :, L:2 * L], ACT.Exp).then_inc(sem("h_relexp"), 1)
                nc.scalar.activation(e[:, :, 0:L], e[:, :, 0:L], ACT.Exp, scale=-1.0).then_inc(sem("h_relexp"), 1)
                if n == 1:
                    act.wait_ge(sem("sb_arg"), 2)
                    nc.scalar.activation(Z0, Z0, ACT.Exp).then_inc(sem("sb_exp"), 1)
                    nc.scalar.activation(Z1, Z1, ACT.Exp).then_inc(sem("sb_exp"), 1)
            split("about", 0)
            sqrt_table()
            root(SS[:, 16:24], SS[:, 8:16], GDV)
            split("about", 1)

            def act_ffn(l, k):
                j0 = J[f"up{l}"]
                sqrt_table()
                for n in range(RING):
                    split(f"up{l}", n)
                norm(k)

                def step(i, tiles, more):
                    def silu(q):
                        act.wait_ge(evac_done, i * RING + (j0 + q + 1))
                        nc.scalar.activation(CT[:, q, 0:S], CT[:, q, 0:S], ACT.Silu).then_inc(sem("silu_done"), 1)

                    for q in range(tiles):
                        act.wait_ge(pe_done, i * RING + (j0 + q + 1))
                        for g in range(2):
                            ins = nc.scalar.activation(CT2(q, g, S), PS[:, (j0 + q) % 8, g * S:(g + 1) * S], ACT.Identity,
                                                       bias=CONV[:, l, bass.ds(i * RING + (3 * 2 * FT + g * FT + q), 1)],
                                                       scale=CONV[:, l, bass.ds(i * RING + (2 * 2 * FT + g * FT + q), 1)])
                        ins.then_inc(sem("tap2_done"), 1)
                        if more is None:
                            w = pieces[f"up{l}", q]
                            act.wait_ge(raw_loaded[w.h], i * 32 + (w.landed + 32))
                            act.copy(WHI[:, w.cols], RAW[:, w.cols]).then_inc(hi_ready[w.h], 1)
                        else:
                            split(*more[q])
                        if q:
                            silu(q - 1)
                    silu(tiles - 1)
                    act.wait_ge(sem("hidden_ready"), i * RING + (FT * l + tiles))

                with act.Fori(0, UP_BODIES - 1) as i:
                    step(i, RING, None)
                ring = [(f"up{l}", n) for n in range(FT)] + [(f"down{l}", n) for n in range(FP)]
                step(UP_BODIES - 1, RING, ring[RING * UP_BODIES:])
                step(UP_BODIES, FT % RING, ring[RING * UP_BODIES + RING:])
                for n in range(RING, FP):
                    split(f"down{l}", n)
                sqrt_table()
                for n in range(2):
                    split(f"gate{l}", n)

            def CT2(q, g, n):
                return CT[:, q, g * S:g * S + n]

            def act_ple(l, k):
                norm(k)
                split(f"proj{l}", 0)
                act.wait_ge(evac_done, END[f"gate{l}"])
                nc.scalar.activation(GATE, GATE, ACT.Sigmoid).then_inc(sem("ple_sigmoid"), 1)

            x_hi(J["mix1"])
            act_ffn(0, 3)
            act_ple(0, 4)
            sqrt_table()
            for n in range(2):
                split("c", n)
            norm(5)
            split("c", 2)
            for n in range(2):
                root(SS[:, 56 + 16 * n:72 + 16 * n], SS[:, 8 + 16 * n:24 + 16 * n], HD)
            root(SS[:, 48:56], SS[:, 40:48], HD)
            for n in range(2):
                split("cout", n)
            for u in range(SW_UNITS):
                exp_unit(u // 2, sink=True)
            x_hi(J["mix2"])
            act_ffn(1, 6)
            act_ple(1, 7)

        @block.vector
        def _(v):
            own, counts = [0], {}

            def step(ins, s=None, wait=True):
                s = s or "dve_chain"
                counts[s] = counts.get(s, 0) + 1
                ins.then_inc(sem(s), 1)
                if wait:
                    v.wait_ge(sem(s), counts[s])

            def bank(j):
                v.wait_ge(pe_done, j + 1)
                return PS[:, j % 8, :]

            def freed(ins, j, wait=False):
                ins.then_inc(evac_done, 1)
                if wait:
                    v.wait_ge(evac_done, j + 1)

            def bc(ap, n, axis=2):
                x = ap.unsqueeze(axis)
                shape = list(x.shape)
                shape[axis] = n
                return x.broadcast_to(shape)

            norm_no = [0]

            def reciprocal_root(dst, src):
                norm_no[0] += 1
                v.wait_ge(sem("root_done"), norm_no[0])
                step(nc.vector.reciprocal(dst, src))

            def transposed(j, n, dst, col=None):
                for m in range(n):
                    src = bank(j + m)[:, :].rearrange("p (c t) -> p c t", c=2)
                    d = dst[:, 2 * m:2 * m + 2, :]
                    if col is None:
                        freed(nc.vector.tensor_copy(d, src), j + m)
                    else:
                        freed(nc.vector.tensor_tensor(d, src, bc(VEC[:, col + 2 * m:col + 2 * m + 2], S), ALU.mult), j + m)
                v.wait_ge(evac_done, j + n)

            def key_pairs(j, n, dst):
                for m in range(n):
                    src = bank(j + m).rearrange("p (c t) -> p c t", c=2)
                    for par in range(2):
                        d = dst[:, 4 * m:4 * m + 4, :].rearrange("p (c h) t -> p c h t", h=2)[:, :, par, :]
                        ins = nc.vector.tensor_scalar(d, src, const("head_rows")[:, par:par + 1], None, ALU.mult)
                    freed(ins, j + m)
                v.wait_ge(evac_done, j + n)

            hi_no = [0]

            def x_lo(j, col=None):
                for m in range(4):
                    src = bank(j + m)
                    hi_no[0] += 1
                    v.wait_ge(sem("x_hi_ready"), hi_no[0])
                    for c in range(2):
                        f = 2 * m + c
                        ins = nc.vector.scalar_tensor_tensor(out=XLO[:, f, :], in0=src[:, c * S:(c + 1) * S],
                                                             scalar=1.0 if col is None else VEC[:, col + f:col + f + 1],
                                                             in1=XHI[:, f, :].bitcast(F32), op0=ALU.mult, op1=ALU.subtract)
                    freed(ins, j + m)
                v.wait_ge(evac_done, j + 4)

            def norm(k, gain=None):
                if k == 0:
                    for t in range(TT):
                        step(nc.vector.tensor_tensor_reduce(out=XN[:, t], in0=X[:, t], in1=X[:, t], scale=1.0, scalar=0.0,
                                                            op0=ALU.mult, op1=ALU.add, accum_out=SS[:, t:t + 1]),
                             "sumsq_ready" if t == TT - 1 else None)
                else:
                    step(nc.vector.tensor_tensor(SS[:, 0:2], SS[:, 96:100:2], SS[:, 97:100:2], ALU.add), "sumsq_ready")
                norm_no[0] += 1
                v.wait_ge(sem("root_done"), norm_no[0])
                step(nc.vector.reciprocal(SS[:, 2:4], SS[:, 2:4]), None if gain is not None else "rstd_ready")
                if gain is None:
                    step(nc.vector.tensor_scalar(XN[:, 0], X[:, 0], SS[:, 2:3], None, ALU.mult), "xn_ready", False)
                else:
                    for t in range(TT):
                        step(nc.vector.scalar_tensor_tensor(out=XN[:, t], in0=X[:, t], scalar=SS[:, 2 + t:3 + t], in1=gain,
                                                            op0=ALU.mult, op1=ALU.mult), "xn_ready", False)
                x_lo(J[f"norm{k}"], NORM_COL[k])

            def evac_cols(name, n, dst, behind=None):
                j = J[name]
                for m in range(n):
                    for t in range(TT):
                        freed(nc.vector.tensor_copy(dst[:, t, m * BANK:(m + 1) * BANK], bank(j + 2 * m + t)), j + 2 * m + t)
                    if m + 2 < n:
                        split_lo(v, name, m + 2)
                    if behind and m in behind:
                        v.wait_ge(evac_done, j + 2 * m + 2)
                        behind[m]()
                v.wait_ge(evac_done, j + 2 * n)

            def sum_squares(t, m):
                d, k = X[:, t, m * BANK:(m + 1) * BANK], 2 * t + m
                step(nc.vector.tensor_tensor_reduce(out=A[:, k * BANK:(k + 1) * BANK], in0=d, in1=d, scale=1.0, scalar=0.0,
                                                    op0=ALU.mult, op1=ALU.add, accum_out=SS[:, 96 + k:97 + k]), "sumsq_part",
                     wait=(k == 3))

            def add_residual(j, by_tile=False):
                for n in range(4):
                    t, m = (n // 2, n % 2) if by_tile else (n % 2, n // 2)
                    d = X[:, t, m * BANK:(m + 1) * BANK]
                    freed(nc.vector.tensor_tensor(d, bank(j + n), d, ALU.add), j + n, True)
                    sum_squares(t, m)

            step(nc.vector.memset(SS[:, 95:96], EPS), "eps_ready")
            v.wait_ge(sem("const_loaded"), 16)
            freed(nc.vector.tensor_copy(VEC[:, 0:64], bank(J["vecs"])[:, 0:64]), J["vecs"])
            v.wait_ge(sem("x_loaded"), 16)
            norm(0)
            split_lo(v, "win", 0)
            freed(nc.vector.tensor_copy(CONV[:, :, :], bank(J["conv"])[:, 0:8 * 2 * FT].rearrange("p (l n) -> p l n", l=2)),
                  J["conv"])
            v.wait_ge(sem("rel_loaded"), 48)
            freed(nc.vector.tensor_tensor(BROW, bank(J["relb"])[0:SWH, 0:384], OUTSIDE, ALU.add), J["relb"], wait=True)
            v.wait_ge(sem("gain_loaded"), 16 * 8)

            half = HD // 2

            def head_norms(view, n, ss, rs, gain, rope=False):
                sq = A[:, 0:TT * n * HD].rearrange("p (t h n) -> p t h n", t=TT, n=HD)
                step(nc.vector.tensor_tensor(sq, view, view, ALU.mult))
                for t in range(TT):
                    step(nc.vector.tensor_reduce(ss[:, t * n:(t + 1) * n], sq[:, t], AX, ALU.add),
                         "sumsq_ready" if t == TT - 1 else None)
                reciprocal_root(rs, rs)
                for t in range(TT):
                    x = view[:, t]
                    step(nc.vector.tensor_tensor(x, x, bc(rs[:, t * n:(t + 1) * n], HD), ALU.mult))
                    step(nc.vector.tensor_tensor(x, x, bc(gain, n, 1), ALU.mult))
                    if not rope:
                        continue
                    x1, x2 = x[:, :, 0:half], x[:, :, half:HD]
                    cos = bc(const("cos")[:, t * half:(t + 1) * half], n, 1)
                    sin = bc(const("sin")[:, t * half:(t + 1) * half], n, 1)
                    x1c, x2s, x2c, x1s = (A[:, k * n * half:(k + 1) * n * half].rearrange("p (h n) -> p h n", h=n)
                                          for k in range(4 * t, 4 * t + 4))
                    step(nc.vector.tensor_tensor(x1c, x1, cos, ALU.mult), wait=False)
                    step(nc.vector.tensor_tensor(x2s, x2, sin, ALU.mult), wait=False)
                    step(nc.vector.tensor_tensor(x2c, x2, cos, ALU.mult), wait=False)
                    step(nc.vector.tensor_tensor(x1s, x1, sin, ALU.mult))
                    step(nc.vector.tensor_tensor(x1, x1c, x2s, ALU.subtract), wait=False)
                    step(nc.vector.tensor_tensor(x2, x2c, x1s, ALU.add))

            def heads_of(proj, c0, n):
                return proj[:, :, c0:c0 + n * HD].rearrange("p t (h n) -> p t h n", n=HD)

            def moba_qk(n):
                head_norms(heads_of(proj_in, 1536 + 512 * n, 8), 8, SS[:, 8 + 16 * n:24 + 16 * n],
                           SS[:, 56 + 16 * n:72 + 16 * n], QK_GAIN[n], rope=True)

            evac_cols("win", 6, proj_in, {3: lambda: moba_qk(0), 4: lambda: moba_qk(1)})

            def gated_gain(gain, gates):
                for t in range(TT):
                    g4 = gates[:, t].rearrange("p (h n) -> p h n", n=GDV)
                    step(nc.vector.tensor_tensor(g4, g4, bc(gain, 4, 1), ALU.mult))

            def head_norm(first_job, gates, dst):
                for t in range(TT):
                    freed(nc.vector.tensor_copy(OUTN[:, t], bank(first_job + t)), first_job + t, True)
                    step(nc.vector.tensor_tensor(SQ[:, t], OUTN[:, t], OUTN[:, t], ALU.mult), wait=(t == 1))
                step(nc.vector.tensor_reduce(SS[:, 8:16], SQ.rearrange("p t (h n) -> p (t h) n", n=GDV), AX, ALU.add), "sumsq_ready")
                step(nc.vector.tensor_tensor(OUTN, OUTN, gates, ALU.mult))
                reciprocal_root(SS[:, 16:24], SS[:, 16:24])
                for t in range(TT):
                    o4, d4 = (x[:, t].rearrange("p (h n) -> p h n", n=GDV) for x in (OUTN, dst))
                    step(nc.vector.tensor_tensor(d4, o4, bc(SS[:, 16 + 4 * t:20 + 4 * t], GDV), ALU.mult), "mixed", t == 1)

            att_no = [0]

            def logits(j, t, add, sink=None):
                u, cols = att_no[0], (t + 1) * P
                att_no[0] += 1
                per = BANK // cols
                st = ATT(u)
                for m in range(8 // per):
                    src = bank(j + m).rearrange("p (h s) -> p h s", h=per)
                    d = PB[u % 2][:, m * BANK:(m + 1) * BANK].rearrange("p (h s) -> p h s", h=per)
                    freed(nc.vector.scalar_tensor_tensor(out=d, in0=src, scalar=HD ** -0.5, in1=add(m * per, per, cols),
                                                         op0=ALU.mult, op1=ALU.add), j + m, m == 8 // per - 1)
                view = PB[u % 2][:, 0:8 * cols].rearrange("p (h s) -> p h s", h=8)
                step(nc.vector.tensor_reduce(st[:, 8:16], view, AX, ALU.max))
                if sink is not None:
                    step(nc.vector.tensor_tensor(st[:, 8:16], st[:, 8:16], sink, ALU.max))
                    step(nc.vector.tensor_tensor(st[:, 0:8], sink, st[:, 8:16], ALU.subtract))
                step(nc.vector.tensor_scalar(st[:, 8:16], st[:, 8:16], -1.0, None, ALU.mult), "att_max")

            def attended(u, jp, jo, t, dst, sinks=None):
                nk = t + 1
                st = ATT(u)
                den = st[:, 16:24]
                v.wait_ge(sem("att_exp"), u + 1)
                view = PB[u % 2][:, 0:8 * nk * P].rearrange("p (h s) -> p h s", h=8)
                step(nc.vector.tensor_reduce(den, view, AX, ALU.add))
                if sinks is not None:
                    v.wait_ge(sem("sink_exp"), sinks)
                    step(nc.vector.tensor_tensor(den, den, st[:, 0:8], ALU.add))
                step(nc.vector.reciprocal(den, den))
                for m in range(2 * nk):
                    freed(nc.vector.tensor_copy(PT[:, 4 * m:4 * m + 4, :], bank(jp + m).rearrange("p (b t) -> p b t", b=4)), jp + m)
                src = bank(jo).rearrange("p (h n) -> p h n", h=8)
                freed(nc.vector.tensor_tensor(dst.rearrange("p (h n) -> p h n", h=8), src, bc(den, HD), ALU.mult), jo, True)

            def causal(h0, n, cols):
                return bc(causal_add[:, 2 * P - cols:2 * P], n, 1)

            def moba_out(t):
                attended(t, J[f"mb_P{t}"], J[f"mb_O{t}"], t, XN[:, t, 512:1024])

            freed(nc.vector.tensor_copy(GRT, bank(J["gr"])[0:GRANK, 0:S]), J["gr"], wait=True)
            g2 = gG.rearrange("p (t n) -> p t n", t=TT)
            freed(nc.vector.tensor_tensor(g2, bank(J["alpha"]).rearrange("p (t n) -> p t n", t=TT),
                                          bc(ALB[:, :], TT, 1), ALU.add), J["alpha"], wait=True)
            step(nc.vector.scalar_tensor_tensor(out=gE, in0=gG, scalar=-1.0, in1=gG, op0=ALU.mult, op1=ALU.max), "g_abs")
            v.wait_ge(sem("bias_written"), 16)
            transposed(J["mb_T"], 2, QT)
            key_pairs(J["mb_T"] + 2, 2, KZT)
            v.wait_ge(sem("g_log"), 1)
            step(nc.vector.scalar_tensor_tensor(out=gG, in0=gG, scalar=0.0, in1=gE, op0=ALU.min, op1=ALU.subtract))
            step(nc.vector.tensor_scalar(gG, gG, 1.0 / 16.0, None, ALU.mult), "g_ready")
            logits(J["mb_L0"], 0, causal)
            freed(nc.vector.tensor_copy(gB_, bank(J["gla_cum"])), J["gla_cum"])
            freed(nc.vector.tensor_copy(gS, bank(J["gla_cum"] + 1)), J["gla_cum"] + 1)
            freed(nc.vector.tensor_copy(gDECR, bank(J["gla_dec"])[:, 0:8]), J["gla_dec"], wait=True)
            logits(J["mb_L1"], 1, causal)
            q_, k_ = proj_in[:, :, 0:256], proj_in[:, :, 256:512]
            v.wait_ge(sem("g_exp"), 3)
            e3, n3, s3 = (x.rearrange("p (t n) -> p t n", t=TT) for x in (gE, gB_, gS))
            step(nc.vector.tensor_tensor(gKN, k_, n3, ALU.mult), "g_qk")
            step(nc.vector.scalar_tensor_tensor(out=q_, in0=q_, scalar=GDK ** -0.5, in1=e3, op0=ALU.mult, op1=ALU.mult), "g_qk")
            step(nc.vector.tensor_tensor(gKST, k_, s3, ALU.mult))
            for c in range(3):
                step(nc.vector.tensor_scalar(KSC[:, c, 0:256], gKST[:, c // 2], const("chunk_rows")[:, c % 2:c % 2 + 1], None,
                                             ALU.mult), "kst_ready", wait=False)
            key_pairs(J["gla_T"], 1, gKZT)
            transposed(J["gla_T"] + 1, 1, gQT)
            moba_out(0)
            for t in range(TT):
                j = J["gla_A"] + t
                freed(nc.vector.tensor_tensor(AT[:, t], bank(j).rearrange("p (h n) -> p h n", h=4), bc(cum, 4, 1), ALU.mult), j, True)
            v.wait_ge(sem("g_exp"), 4)
            gdec = DEC.rearrange("p (j c) -> p j c", j=2)
            for c in range(3):
                j = J["gla_U"] + c
                u = bank(j).rearrange("p (h n) -> p h n", h=4)
                freed(nc.vector.tensor_tensor(ST[:, c], u, bc(const("head_rows"), GDV), ALU.mult), j, True)
                for pair in range(2 if c else 0):
                    step(nc.vector.scalar_tensor_tensor(
                        out=ST[:, c, 2 * pair:2 * pair + 2], in0=ST[:, c - 1, 2 * pair:2 * pair + 2],
                        scalar=gdec[:, pair, c:c + 1], in1=ST[:, c, 2 * pair:2 * pair + 2],
                        op0=ALU.mult, op1=ALU.add), "state_ready" if c == 2 and pair == 1 else None)
            v.wait_ge(sem("silu_gate"), 1)
            gated_gain(LB_GAIN, proj_in[:, :, 1024:1536])
            moba_out(1)
            head_norm(J["gla_O"], proj_in[:, :, 1024:1536], XN[:, :, 0:512])
            x_lo(J["mix0"], MIX_COL[0])
            add_residual(J["wout"])

            for m in range(4):
                j = J["subk"] + m
                freed(nc.vector.tensor_copy(SKT[:, 4 * m:4 * m + 4, :], bank(j).rearrange("p (b t) -> p b t", b=4)), j)
            v.wait_ge(sem("n2w_loaded"), 16)
            norm(1, gain=N2W)
            def routed(u, q):
                n = [0]
                v.sem_clear(sem("route_step"))

                def then(ins):
                    n[0] += 1
                    ins.then_inc(sem("route_step"), 1)
                    v.wait_ge(sem("route_step"), n[0])

                def top16(vals, best, index, width):
                    then(nc.vector.max(best[:, 0:8], vals))
                    then(nc.vector.max_index(index[:, 0:8], best[:, 0:8], vals))
                    then(nc.vector.match_replace(r_w[:, 0:width], best[:, 0:8], vals, NEG))
                    then(nc.vector.max(best[:, 8:16], r_w[:, 0:width]))
                    then(nc.vector.max_index(index[:, 8:16], best[:, 8:16], r_w[:, 0:width]))

                then(nc.vector.tensor_copy(R[:, 0:256], PROJ[:, bass.ds(u * 256, 256)]))
                for p_ in range(2):
                    top16(r_s[:, p_], r_sv[:, p_], r_si[:, p_], NKEYS)
                cand = r_cand.rearrange("p (i j) -> p i j", i=TOPK)
                then(nc.vector.tensor_tensor(cand, bc(r_sv[:, 0], TOPK), bc(r_sv[:, 1], TOPK, 1), ALU.add))
                top16(r_cand, r_top, r_pos, TOPK * TOPK)
                then(nc.vector.tensor_scalar(r_ab[:, 0:16], r_pos, 4, None, ALU.logical_shift_right))
                then(nc.vector.tensor_scalar(r_ab[:, 16:32], r_pos, 15, None, ALU.bitwise_and))
                hot = r_w[:, 0:256].rearrange("p (k j) -> p k j", k=TOPK)
                for p_ in range(2):
                    then(nc.vector.tensor_tensor(hot, bc(r_ab[:, 16 * p_:16 * p_ + 16], TOPK), bc(const("iota"), TOPK, 1),
                                                 ALU.is_equal))
                    then(nc.vector.tensor_tensor(hot, hot, bc(r_si[:, p_], TOPK, 1), ALU.mult))
                    then(nc.vector.tensor_reduce(r_i[:, p_], hot, AX, ALU.add))
                then(nc.vector.tensor_scalar(r_e, r_top, r_top[:, 0:1], None, ALU.subtract))
                nc.vector.scalar_tensor_tensor(out=r_idx[:, q], in0=r_i[:, 0], scalar=float(NKEYS), in1=r_i[:, 1],
                                               op0=ALU.mult, op1=ALU.add).then_inc(sem("idx_ready"), 1)
                then(nc.vector.memset(SS[:, 6:7], 0.0))
                nc.vector.memset(SS[:, 7:8], 0.0).then_inc(sem("top_ready"), 1)
                v.wait_ge(sem("gate_exp"), u + 1)
                then(nc.vector.tensor_reduce(r_sum, r_e, AX, ALU.add))
                then(nc.vector.reciprocal(r_rs, r_sum))
                then(nc.vector.tensor_scalar(r_gate[:, q], r_e, r_rs, None, ALU.mult))

            def dots(u, q, t, b):
                for k in range(4):
                    n = (4 * b + k) % NU
                    v.wait_ge(u_loaded[n], u * 32 + 16 * (1 + b // 2))
                    ins = nc.vector.tensor_tensor_reduce(out=ubuf[n], in0=ubuf[n], in1=XN[:, t], scale=1.0, scalar=0.0,
                                                         op0=ALU.mult, op1=ALU.add, accum_out=r_dot[:, b % 2, k:k + 1])
                ins.then_inc(sem("dots_done"), 1)

            def weights(u, q, b):
                v.wait_ge(sem("gelu_done"), u * 4 + (b + 1))
                nc.vector.tensor_tensor(r_wt[:, b % 2], r_act[:, b % 2], r_gate[:, q, 4 * b:4 * b + 4],
                                        ALU.mult).then_inc(sem("weights_ready"), 1)

            def vec_unit(u, q, t, first=False, last=False):
                for b in range(4):
                    if not (first and b < 2):
                        v.wait_ge(sem("gelu_done"), u * 4 + (b - 1))
                    dots(u, q, t, b)
                    if not (first and b < 3):
                        v.wait_ge(sem("diag_ready"), u * 4 + (b - 2))
                    if b > 0:
                        weights(u, q, b - 1)
                    elif not first:
                        weights(u - 1, 1 - q, 3)
                    if b == 1 and not last:
                        routed(u + 1, 1 - q)

            def query_cols(m):
                transposed(query_job(m), 1, qT[:, 2 * m:2 * m + 2, :])

            def scores(m):
                j = score_job(m)
                freed(nc.vector.tensor_copy(SCORE[:, m * BANK:(m + 1) * BANK], bank(j)), j, wait=True)

            query_cols(0)
            query_cols(1)
            split_lo(v, "query", 2)
            query_cols(2)
            scores(0)
            routed(0, 0)
            split_lo(v, "query", 3)
            for m in range(3, 8):
                query_cols(m)
            for m in range(1, 8):
                scores(m)
            vec_unit(0, 0, 0, first=True)
            vec_unit(1, 1, 0)
            with v.Fori(1, PH // 2) as i:
                vec_unit(i * 2, 0, 0)
                vec_unit(i * 2 + 1, 1, 0)
            with v.Fori(PH // 2, UNITS // 2 - 1) as i:
                vec_unit(i * 2, 0, 1)
                vec_unit(i * 2 + 1, 1, 1)
            vec_unit(UNITS - 2, 0, 1)
            vec_unit(UNITS - 1, 1, 1, last=True)
            v.wait_ge(sem("diag_ready"), 4 * UNITS - 2)
            weights(UNITS - 1, 1, 3)
            v.wait_ge(sem("dots_done"), 4 * UNITS)
            add_residual(J["peer"], by_tile=True)

            norm(2)
            hq, hf, hi, hg = (proj_ab[:, :, 1536 + 512 * n:2048 + 512 * n] for n in range(4))

            def h_abs():
                step(nc.vector.scalar_tensor_tensor(out=hLN, in0=hf, scalar=-1.0, in1=hf, op0=ALU.mult, op1=ALU.max), "h_abs")

            def h_log_f():
                v.wait_ge(sem("h_log"), 1)
                v.wait_ge(sem("h_sig"), 1)
                step(nc.vector.scalar_tensor_tensor(out=hf, in0=hf, scalar=0.0, in1=hLN, op0=ALU.min, op1=ALU.subtract), "h_logf")

            evac_cols("ab", 7, proj_ab, {4: h_abs, 5: h_log_f})
            transposed(J["sb_T"], 2, QT)
            key_pairs(J["sb_T"] + 2, 2, KZT)
            for m in range(6):
                j = J["sb_Z"] + m
                freed(nc.vector.tensor_scalar(A[:, m * BANK:(m + 1) * BANK], bank(j), HD ** -0.5, None, ALU.mult), j, m == 5)
            step(nc.vector.scalar_tensor_tensor(out=L0, in0=Z0, scalar=-1.0, in1=Z0, op0=ALU.mult, op1=ALU.max))
            step(nc.vector.scalar_tensor_tensor(out=L1, in0=Z1, scalar=-1.0, in1=Z1, op0=ALU.mult, op1=ALU.max), "sb_abs")
            transposed(J["hg_B"], 2, hBT.rearrange("p (h t) -> p h t", h=4))
            for t in range(TT):
                j = J["hg_suf"] + t
                freed(nc.vector.tensor_copy(hSF[:, t], bank(j)), j, True)
            transposed(J["hg_T"], 2, hQT.rearrange("p (h t) -> p h t", h=4))
            transposed(J["hg_T"] + 2, 2, hKT.rearrange("p (h t) -> p h t", h=4))
            v.wait_ge(sem("sb_log"), 2)
            for z, l in ((Z0, L0), (Z1, L1)):
                step(nc.vector.scalar_tensor_tensor(out=l, in0=z, scalar=0.0, in1=l, op0=ALU.max, op1=ALU.add))
            for l in (L0[:, :, 0:P], L1):
                step(nc.vector.tensor_tensor(l, l, bc(const("before"), 8, 1), ALU.mult), "sb_plus")

            def level(n):
                L, e = LEVELS[n], hE0 if n % 2 == 0 else hE1
                return (L, *(x.rearrange("p (b i) -> p b i", i=2 * L) for x in (hBT, e, hQT, hKT)))

            def relative(n):
                L, bt, e, _, _ = level(n)
                ref = bt[:, :, L - 1:L].broadcast_to([P, 4 * S // (2 * L), 2 * L])
                step(nc.vector.tensor_tensor(e, bt, ref, ALU.subtract), "h_rel")

            def operands(n):
                L, _, e, qv, kv = level(n)
                v.wait_ge(sem("h_relexp"), 2 * n + 2)
                step(nc.vector.tensor_tensor(e[:, :, L:2 * L], e[:, :, L:2 * L], qv[:, :, L:2 * L], ALU.mult), "h_lev", False)
                step(nc.vector.tensor_tensor(e[:, :, 0:L], e[:, :, 0:L], kv[:, :, 0:L], ALU.mult), "h_lev")

            def add_level(n):
                for t in range(TT):
                    j = J[f"hg_L{n}"] + t
                    freed(nc.vector.tensor_tensor(hTMP[:, t], bank(j).rearrange("p (h n) -> p h n", h=4),
                                                  bc(LEV[:, n], 4, 1), ALU.mult), j, t == 1)
                step(nc.vector.tensor_tensor(AT, AT, hTMP, ALU.add), "state_ready" if n == len(LEVELS) - 1 else None)

            for t in range(TT):
                j = J["hg_D"] + t
                freed(nc.vector.tensor_tensor(AT[:, t], bank(j).rearrange("p (h n) -> p h n", h=4), bc(ident, 4, 1), ALU.mult), j, True)
            relative(0)
            relative(1)
            v.wait_ge(sem("h_sufexp"), 1)
            step(nc.vector.tensor_tensor(hKST, hKK, hSF, ALU.mult))
            operands(0)
            for m in range(6):
                j = J["sb_C"] + m
                d = A[:, m * BANK:(m + 1) * BANK]
                freed(nc.vector.tensor_tensor(d, d, bank(j), ALU.subtract), j, m == 5)
            for z in (Z0[:, :, 0:P], Z1):
                step(nc.vector.tensor_tensor(z, z, bc(const("before_add"), 8, 1), ALU.add), "sb_arg", False)
            operands(1)
            add_level(0)
            relative(2)
            for c in range(3):
                step(nc.vector.tensor_scalar(KSC[:, c], hKST[:, c // 2], const("chunk_rows")[:, c % 2:c % 2 + 1], None,
                                             ALU.mult), "kst_ready", wait=False)
            v.wait_ge(sem("h_bexp"), 1)
            step(nc.vector.tensor_tensor(hQB, hQT, hT0, ALU.mult), "h_qb")
            operands(2)
            add_level(1)
            relative(3)
            for t in range(TT):
                j = J["sb_O"] + t
                freed(nc.vector.tensor_copy(XN[:, t, 0:512], bank(j)), j)
            for n in (3, 4, 5):
                operands(n)
                add_level(n - 1)
                if n < 5:
                    relative(n + 1)
            hdec = hT0.rearrange("p (h c i) -> p h c i", h=4, c=4)
            for c in range(3):
                j = J["hg_U"] + c
                freed(nc.vector.tensor_copy(ST[:, c], bank(j).rearrange("p (h n) -> p h n", h=4)), j, True)
                for h in range(4 if c else 0):
                    step(nc.vector.scalar_tensor_tensor(out=ST[:, c, h], in0=ST[:, c - 1, h],
                                                        scalar=hdec[:, h, c, CH - 1:CH], in1=ST[:, c, h],
                                                        op0=ALU.mult, op1=ALU.add), wait=(h == 3))
            add_level(5)
            v.wait_ge(sem("h_silu"), 2)
            gated_gain(HG_GAIN, hg)
            head_norm(J["hg_O"], hg, XN[:, :, 512:1024])
            x_lo(J["mix1"])
            add_residual(J["about"])

            def vec_ffn(l, k):
                norm(k)
                j0 = J[f"up{l}"]

                def conv(i, tiles, more):
                    for q in range(tiles):
                        v.wait_ge(sem("tap2_done"), i * RING + (FT * l + q + 1))
                        for tap in (1, 0):
                            n = 2 - tap
                            if tap == 0:
                                v.wait_ge(sem("tap1_done"), i * RING + (FT * l + q + 1))
                            for g in range(2):
                                d = CT[:, q, g * S + n:(g + 1) * S]
                                ins = nc.vector.scalar_tensor_tensor(
                                    out=d, in0=PS[:, (j0 + q) % 8, g * S:(g + 1) * S - n],
                                    scalar=CONV[:, l, bass.ds(i * RING + (tap * 2 * FT + g * FT + q), 1)], in1=d,
                                    op0=ALU.mult, op1=ALU.add)
                            ins.then_inc(sem("tap1_done") if tap else evac_done, 1)
                        if more is None:
                            w = pieces[f"up{l}", q]
                            v.wait_ge(hi_ready[w.h], i + (w.count + 1))
                            nc.vector.tensor_tensor(WLO[:, w.cols], RAW[:, w.cols], WHI[:, w.cols].bitcast(F32),
                                                    ALU.subtract).then_inc(lo_ready[w.h], 1)
                        else:
                            split_lo(v, *more[q])

                with v.Fori(0, UP_BODIES - 1) as i:
                    conv(i, RING, None)
                ring = [(f"up{l}", n) for n in range(FT)] + [(f"down{l}", n) for n in range(FP)]
                conv(UP_BODIES - 1, RING, ring[RING * UP_BODIES:])
                conv(UP_BODIES, FT % RING, ring[RING * UP_BODIES + RING:])
                for n in range(RING, FP):
                    split_lo(v, f"down{l}", n)
                add_residual(J[f"down{l}"], by_tile=True)

            def vec_ple(l, k):
                norm(k)
                j = J[f"pT{l}"]
                src = bank(j).rearrange("p (c t) -> p c t", c=2)
                step(nc.vector.tensor_copy(PHI[:, :, :], src))
                freed(nc.vector.tensor_tensor(PLO[:, :, :], src, PHI[:, :, :].bitcast(F32), ALU.subtract), j)
                evac_cols(f"gate{l}", 2, GATE)
                v.wait_ge(sem("ple_sigmoid"), l + 1)
                for t in range(TT):
                    for m in range(2):
                        j = J[f"proj{l}"] + 2 * t + m
                        g = GATE[:, t, m * BANK:(m + 1) * BANK]
                        freed(nc.vector.tensor_tensor(g, bank(j), g, ALU.mult), j, True)
                        d = X[:, t, m * BANK:(m + 1) * BANK]
                        step(nc.vector.tensor_tensor(d, d, g, ALU.add), "x_final" if l == 1 and m == 1 else None)
                        if l == 0:
                            sum_squares(t, m)

            vec_ffn(0, 3)
            vec_ple(0, 4)

            norm(5)

            def window_q(n):
                head_norms(heads_of(proj_c, 512 * n, 8), 8, SS[:, 8 + 16 * n:24 + 16 * n],
                           SS[:, 56 + 16 * n:72 + 16 * n], QK_GAIN[2])

            def window_k():
                keys = heads_of(proj_c, 1024, SWKV)
                head_norms(keys, SWKV, SS[:, 40:48], SS[:, 48:56], QK_GAIN[3])
                for t in range(TT):
                    step(nc.vector.tensor_copy(KDUP[:, t], bc(keys[:, t], 2)), "keys_ready")

            evac_cols("c", 3, proj_c, {0: lambda: window_q(0), 1: lambda: window_q(1), 2: window_k})
            transposed(J["sw_T"], 4, QT)
            key_pairs(J["sw_T"] + 4, 2, KZT)
            v.wait_ge(sem("bias_loaded"), 16)
            first = att_no[0]

            def window_logits(u):
                def biased(h0, n, cols, base=8 * (u % 2)):
                    return BIAS[:, base + h0:base + h0 + n, 2 * P - cols:2 * P]

                logits(J[f"sw_L{u}"], u // 2, biased, sink=SINK[:, 8 * (u % 2):8 * (u % 2) + 8])

            window_logits(0)
            for u in range(SW_UNITS):
                if u + 1 < SW_UNITS:
                    window_logits(u + 1)
                t, g = u // 2, u % 2
                attended(first + u, J[f"sw_P{u}"], J[f"sw_O{u}"], t, XN[:, t, g * 512:(g + 1) * 512], sinks=u + 1)
            x_lo(J["mix2"])
            add_residual(J["cout"])
            vec_ffn(1, 6)
            vec_ple(1, 7)

        @block.tensor
        def _(pe):
            def bank(j):
                if j >= 8:
                    pe.wait_ge(evac_done, j - 7)
                return PS[:, j % 8, :]

            def transposes(j, blocks):
                b = bank(j)
                for n, src in enumerate(blocks):
                    ins = pe.transpose(b[:, n * P:(n + 1) * P], src, ident)
                ins.then_inc(pe_done, 1)

            def norm_T(j, src=None):
                s = src if src is not None else XN
                for m in range(4):
                    transposes(j + m, [s[:, t, (2 * m + c) * P:(2 * m + c + 1) * P] for c in range(2) for t in range(TT)])

            xn_no = [0]

            def norm(k):
                xn_no[0] += TT
                pe.wait_ge(sem("xn_ready"), xn_no[0])
                norm_T(J[f"norm{k}"])

            def product(o, x, w, first, last):
                pe.matmul(o, x[0], w[0], start=first, stop=False)
                pe.matmul(o, x[0], w[1], start=False, stop=False)
                return pe.matmul(o, x[1], w[0], start=False, stop=last)

            def xs(c, rows):
                return XHI[:, c, rows], XLO[:, c, rows]

            def split_weights(name, n, c=KC):
                w = pieces[name, n]
                pe.wait_ge(lo_ready[w.h], w.count)
                return part(WHI, w, c), part(WLO, w, c)

            def dense(name, chunks, ready):
                pe.wait_ge(evac_done, ready)
                for n in range(chunks):
                    hi, lo = split_weights(name, n)
                    for t in range(TT):
                        b = bank(J[name] + 2 * n + t)
                        for c in range(KC):
                            ins = product(b, xs(c, slice(t * P, (t + 1) * P)), (hi[:, c, :], lo[:, c, :]), c == 0, c == KC - 1)
                        ins.then_inc(pe_done, 1)

            pe.wait_ge(sem("const_loaded"), 16)
            pe.wait_ge(sem("vec_loaded"), 16 * 5)
            pe.transpose(PS[:, J["vecs"], 0:64], VROW[0:64, :], ident[0:64, 0:64]).then_inc(pe_done, 1)
            norm(0)
            pe.wait_ge(sem("conv_loaded"), 16 * 6)
            for n in range(4):
                ins = pe.transpose(PS[:, J["conv"], n * 4 * FT:(n + 1) * 4 * FT], CROW[n][:, :], ident[0:4 * FT, 0:4 * FT])
            ins.then_inc(pe_done, 1)
            pe.wait_ge(sem("rel_loaded"), 48)
            pe.matmul(PS[0:SWH, J["relb"], 0:384], RB, OH, start=True, stop=True).then_inc(pe_done, 1)
            dense("win", 6, END["norm0"])
            b = bank(J["gr"])
            pe.wait_ge(sem("gr_loaded"), 32)
            for c in range(KC):
                for n, x in enumerate((XHI, XLO)):
                    ins = pe.matmul(b[0:GRANK, 0:S], W_GR[:, c, :], x[:, c, :].bitcast(F32), start=(c == n == 0),
                                    stop=(c == KC - 1 and n == 1))
            ins.then_inc(pe_done, 1)

            def updates(j, count, kcols, values):
                for c in range(3):
                    pe.wait_ge(sem("kst_ready"), 3 * count + c + 1)
                    b = bank(j + c)
                    for h in range(4):
                        ins = pe.matmul(b[:, h * P:(h + 1) * P], kcols(c, h), values(c // 2, h), start=True, stop=True)
                    ins.then_inc(pe_done, 1)

            def outputs(j, count, values, queries):
                pe.wait_ge(sem("state_ready"), count + 1)
                for t in range(TT):
                    b = bank(j + t)
                    for h in range(4):
                        o = b[:, h * P:(h + 1) * P]
                        pe.matmul(o, AT[:, t, h, :], values(t, h), start=True, stop=False, skip_group_check=True)
                        for par in range(2):
                            c = 2 * t + par
                            if c:
                                ins = pe.matmul(o[par * CH:(par + 1) * CH, :], queries(t, h, par), ST[:, c - 1, h, :],
                                                start=False, stop=True, skip_group_check=True)
                    ins.then_inc(pe_done, 1)

            def qk_T(j, sources):
                for m in range(len(sources) // 2):
                    transposes(j + m, [sources[2 * m + c](t) for c in range(2) for t in range(TT)])
                pe.wait_ge(evac_done, j + len(sources) // 2)

            def columns(proj, c0, n):
                return [lambda t, c=c: proj[:, t, c0 + c * P:c0 + (c + 1) * P] for c in range(n)]

            def logits(j, t, pair, variant):
                cols = (t + 1) * P
                per = BANK // cols
                for m in range(8 // per):
                    b = bank(j + m)
                    for h in range(per):
                        hh = m * per + h
                        ins = pe.matmul(b[:, h * cols:(h + 1) * cols], QT[:, pair(hh), t * P:(t + 1) * P],
                                        KZT[:, variant(hh), 0:cols], start=True, stop=True)
                    ins.then_inc(pe_done, 1)

            def attended(u, jp, jo, t, values):
                nk = t + 1
                pe.wait_ge(sem("att_exp"), u + 1)
                for m in range(2 * nk):
                    transposes(jp + m, [PB[u % 2][:, (4 * m + n) * P:(4 * m + n + 1) * P] for n in range(4)])
                pe.wait_ge(evac_done, jp + 2 * nk)
                b = bank(jo)
                for h in range(8):
                    for k in range(nk):
                        ins = pe.matmul(b[:, h * HD:(h + 1) * HD], PT[:, h * nk + k, :], values(k, h),
                                        start=(k == 0), stop=(k == nk - 1))
                ins.then_inc(pe_done, 1)

            def moba_logits(t):
                logits(J[f"mb_L{t}"], t, lambda h: h // 2, lambda h: h)

            def moba_out(t):
                attended(t, J[f"mb_P{t}"], J[f"mb_O{t}"], t,
                         lambda k, h: proj_in[:, k, 2560 + h * HD:2560 + (h + 1) * HD])

            def gla_values(t, h):
                return proj_in[:, t, 512 + h * P:512 + (h + 1) * P]

            pe.wait_ge(evac_done, END["gr"])
            b = bank(J["alpha"])
            for t in range(TT):
                ins = pe.matmul(b[:, t * 256:(t + 1) * 256], GRT[:, t * P:(t + 1) * P], W_ALPHA, start=True, stop=True)
            ins.then_inc(pe_done, 1)
            qk_T(J["mb_T"], columns(proj_in, 1536, 8))
            moba_logits(0)
            pe.wait_ge(sem("g_ready"), 1)
            for n, m in enumerate((cum, suf)):
                b = bank(J["gla_cum"] + n)
                for t in range(TT):
                    ins = pe.matmul(b[:, t * 256:(t + 1) * 256], m, gG[:, t * 256:(t + 1) * 256], start=True, stop=True)
                ins.then_inc(pe_done, 1)
            b = bank(J["gla_dec"])
            for pair in range(2):
                for t in range(TT):
                    ins = pe.matmul(b[:, pair * 4 + 2 * t:pair * 4 + 2 * t + 2], gG[:, t * 256 + pair * P:t * 256 + (pair + 1) * P],
                                    cum[:, CH - 1:P:CH], start=True, stop=True)
            ins.then_inc(pe_done, 1)
            moba_logits(1)
            pe.wait_ge(sem("g_qk"), 2)
            transposes(J["gla_T"], [gKN[:, t, j * P:(j + 1) * P] for j in range(2) for t in range(TT)])
            transposes(J["gla_T"] + 1, [proj_in[:, t, j * P:(j + 1) * P] for j in range(2) for t in range(TT)])
            moba_out(0)
            pe.wait_ge(evac_done, END["gla_T"])
            for t in range(TT):
                b = bank(J["gla_A"] + t)
                for h in range(4):
                    ins = pe.matmul(b[:, h * P:(h + 1) * P], gKZT[:, h, t * P:(t + 1) * P], gQT[:, h // 2, t * P:(t + 1) * P],
                                    start=True, stop=True)
                ins.then_inc(pe_done, 1)
            updates(J["gla_U"], 0, lambda c, h: KSC[:, c, (h // 2) * P:(h // 2 + 1) * P], gla_values)
            moba_out(1)
            outputs(J["gla_O"], 0, gla_values, lambda t, h, par: gQT[:, h // 2, t * P + par * CH:t * P + (par + 1) * CH])
            pe.wait_ge(sem("mixed"), TT)
            norm_T(J["mix0"])
            dense("wout", 2, END["mix0"])

            pe.wait_ge(sem("subkeys_loaded"), 16)
            for m in range(4):
                transposes(J["subk"] + m, [SKN[:, 4 * m + n, :] for n in range(4)])
            norm(1)
            pe.wait_ge(evac_done, END["norm1"])
            def queries(m):
                hi, lo = split_weights("query", m // 2)
                b = bank(query_job(m))
                for q in range(2):
                    w0 = (m % 2) * 256 + q * P
                    for c in range(KC):
                        ins = product(b[:, q * S:(q + 1) * S], (hi[:, c, w0:w0 + P], lo[:, c, w0:w0 + P]), xs(c, slice(0, S)),
                                      c == 0, c == KC - 1)
                ins.then_inc(pe_done, 1)

            def scores(m):
                t, h0 = m // 4, (m % 4) * 2
                pe.wait_ge(evac_done, query_job(h0 + 1) + 1)
                b = bank(score_job(m))
                for n in range(4):
                    u = 2 * h0 + n
                    ins = pe.matmul(b[:, n * P:(n + 1) * P], qT[:, u, t * P:(t + 1) * P], SKT[:, u, :], start=True, stop=True)
                ins.then_inc(pe_done, 1)

            for m in range(3):
                queries(m)
            scores(0)
            for m in range(3, 8):
                queries(m)
            for m in range(1, 8):
                scores(m)

            def sum_rows(u, t):
                for b in range(4):
                    pe.wait_ge(sem("diag_ready"), u * 4 + (b + 1))
                    for k in range(4):
                        n = 4 * b + k
                        pe.wait_ge(v_loaded[n], u * 16 + 16)
                        for m in range(2):
                            ins = pe.matmul(PS[:, (J["peer"] + 2 * t + m) % 8, :], DIAG[:, b % 2, k, :],
                                            vbuf[n][:, m * BANK:(m + 1) * BANK], start=False, stop=False, skip_group_check=True)
                    ins.then_inc(sem("rows_summed"), 1)

            for t in range(TT):
                accs = [bank(J["peer"] + 2 * t + m) for m in range(2)]
                for acc in accs:
                    pe.matmul(acc, zeros, C[:, 0:BANK], start=True, stop=False, skip_group_check=True)
                with pe.Fori(t * PH // 2, (t + 1) * PH // 2) as i:
                    sum_rows(i * 2, t)
                    sum_rows(i * 2 + 1, t)
                for acc in accs:
                    pe.matmul(acc[:, 0:P], zeros, ident, start=False, stop=True, skip_group_check=True).then_inc(pe_done, 1)

            norm(2)
            dense("ab", 7, END["norm2"])
            pe.wait_ge(evac_done, END["ab"])
            qk_T(J["sb_T"], columns(proj_ab, 0, 8))
            for m in range(4):
                b = bank(J["sb_Z"] + m)
                for n in range(2):
                    h = 2 * m + n
                    ins = pe.matmul(b[:, n * S:(n + 1) * S], KZT[:, h, 0:P], QT[:, h // 2, :], start=True, stop=True)
                ins.then_inc(pe_done, 1)
            for m in range(2):
                b = bank(J["sb_Z"] + 4 + m)
                for n in range(4):
                    h = 4 * m + n
                    ins = pe.matmul(b[:, n * P:(n + 1) * P], KZT[:, h, P:S], QT[:, h // 2, P:S], start=True, stop=True)
                ins.then_inc(pe_done, 1)
            pe.wait_ge(sem("h_logf"), 1)
            for m in range(2):
                b = bank(J["hg_B"] + m)
                for n in range(2):
                    for t in range(TT):
                        h = 2 * m + n
                        ins = pe.matmul(b[:, n * S + t * P:n * S + (t + 1) * P], proj_ab[:, t, 2048 + h * P:2048 + (h + 1) * P],
                                        cum, start=True, stop=True)
                ins.then_inc(pe_done, 1)
            for t in range(TT):
                pe.matmul(bank(J["hg_suf"] + t), suf, proj_ab[:, t, 2048:2560], start=True, stop=True).then_inc(pe_done, 1)
            pe.wait_ge(sem("h_silu"), 1)
            for m in range(2):
                transposes(J["hg_T"] + m, [proj_ab[:, t, 1536 + (2 * m + c) * P:1536 + (2 * m + c + 1) * P]
                                           for c in range(2) for t in range(TT)])
            for m in range(2):
                transposes(J["hg_T"] + 2 + m, [hKK[:, t, (2 * m + c) * P:(2 * m + c + 1) * P] for c in range(2) for t in range(TT)])
            pe.wait_ge(evac_done, END["hg_T"])
            for t in range(TT):
                b = bank(J["hg_D"] + t)
                for h in range(4):
                    o = h * S + t * P
                    ins = pe.matmul(b[:, h * P:(h + 1) * P], hKT[:, o:o + P], hQT[:, o:o + P], start=True, stop=True)
                ins.then_inc(pe_done, 1)
            pe.wait_ge(sem("sb_plus"), 2)
            for m in range(4):
                b = bank(J["sb_C"] + m)
                pe.matmul(b, incl, B[:, m * BANK:(m + 1) * BANK], start=True, stop=False, skip_group_check=True)
                pe.matmul(b.rearrange("p (h t) -> p h t", h=2)[:, :, P:S], ones, L1[:, 2 * m:2 * m + 2, :],
                          start=False, stop=True, skip_group_check=True).then_inc(pe_done, 1)
            for m in range(2):
                b = bank(J["sb_C"] + 4 + m)
                pe.matmul(b, incl, B[:, 2048 + m * BANK:2048 + (m + 1) * BANK], start=True, stop=True).then_inc(pe_done, 1)

            def level(n):
                pe.wait_ge(sem("h_lev"), 2 * n + 2)
                e = hE0 if n % 2 == 0 else hE1
                for t in range(TT):
                    b = bank(J[f"hg_L{n}"] + t)
                    for h in range(4):
                        o = h * S + t * P
                        ins = pe.matmul(b[:, h * P:(h + 1) * P], e[:, o:o + P], e[:, o:o + P], start=True, stop=True)
                    ins.then_inc(pe_done, 1)

            def hgrn_values(t, h):
                return proj_ab[:, t, 2560 + h * P:2560 + (h + 1) * P]

            level(0)
            level(1)
            pe.wait_ge(sem("sb_exp"), 2)
            for t in range(TT):
                b = bank(J["sb_O"] + t)
                for h in range(8):
                    vals = lambda k: proj_ab[:, k, 1024 + h * HD:1024 + (h + 1) * HD]
                    ins = pe.matmul(b[:, h * HD:(h + 1) * HD], Z0[:, h, t * P:(t + 1) * P], vals(0), start=True, stop=(t == 0))
                    if t:
                        ins = pe.matmul(b[:, h * HD:(h + 1) * HD], Z1[:, h, :], vals(1), start=False, stop=True)
                ins.then_inc(pe_done, 1)

            for n in (2, 3, 4):
                level(n)
            updates(J["hg_U"], 1, lambda c, h: KSC[:, c, h * P:(h + 1) * P], hgrn_values)
            level(5)
            pe.wait_ge(sem("h_qb"), 1)
            outputs(J["hg_O"], 1, hgrn_values, lambda t, h, par: hQB[:, h * S + t * P + par * CH:h * S + t * P + (par + 1) * CH])
            pe.wait_ge(sem("mixed"), 2 * TT)
            norm_T(J["mix1"])
            dense("about", 2, END["mix1"])

            def ffn(l, k):
                norm(k)
                pe.wait_ge(evac_done, END[f"norm{k}"])
                j0 = J[f"up{l}"]

                def up_tiles(i, tiles):
                    for q in range(tiles):
                        w = pieces[f"up{l}", q]
                        pe.wait_ge(lo_ready[w.h], i + w.count)
                        hi, lo = (part(t, w).rearrange("p c (g n) -> p c g n", g=2) for t in (WHI, WLO))
                        pe.wait_ge(evac_done, i * RING + (j0 + q - RING + 1))
                        for g in range(2):
                            for c in range(KC):
                                ins = product(PS[:, (j0 + q) % 8, g * S:(g + 1) * S], (hi[:, c, g, :], lo[:, c, g, :]),
                                              xs(c, slice(0, S)), c == 0, c == KC - 1)
                        ins.then_inc(pe_done, 1)

                with pe.Fori(0, UP_BODIES) as i:
                    up_tiles(i, RING)
                up_tiles(UP_BODIES, FT % RING)
                j1 = J[f"down{l}"]
                for n in range(FP):
                    pe.wait_ge(sem("hidden_ready"), FT * l + 2 * n + 2)
                    hi, lo = split_weights(f"down{l}", n, 2)
                    for t in range(TT):
                        if n == 0 and t == 1:
                            pe.wait_ge(evac_done, END[f"up{l}"])
                        for r in range(2):
                            c = 2 * n + r
                            rows = slice(t * P, (t + 1) * P)
                            for m in range(2):
                                cols = slice(m * BANK, (m + 1) * BANK)
                                ins = product(PS[:, (j1 + 2 * t + m) % 8, :], (HHI[:, c, rows], HLO[:, c, rows]),
                                              (hi[:, r, cols], lo[:, r, cols]), c == 0, c == FT - 1)
                                if c == FT - 1:
                                    ins.then_inc(pe_done, 1)
                    if n < FP - 1:
                        ins.then_inc(sem("down_used"), 1)

            def ple(l, k):
                norm(k)
                pe.wait_ge(sem("p_loaded"), 16 + 16 * l)
                transposes(J[f"pT{l}"], [PIN[:, l, t, c * P:(c + 1) * P] for c in range(2) for t in range(TT)])
                dense(f"gate{l}", 2, END[f"norm{k}"])
                hi, lo = split_weights(f"proj{l}", 0, 2)
                pe.wait_ge(evac_done, END[f"pT{l}"])
                for t in range(TT):
                    rows = slice(t * P, (t + 1) * P)
                    for m in range(2):
                        cols = slice(m * BANK, (m + 1) * BANK)
                        b = bank(J[f"proj{l}"] + 2 * t + m)
                        for c in range(2):
                            ins = product(b, (PHI[:, c, rows], PLO[:, c, rows]), (hi[:, c, cols], lo[:, c, cols]), c == 0, c == 1)
                        ins.then_inc(pe_done, 1)

            ffn(0, 3)
            ple(0, 4)
            norm(5)
            dense("c", 3, END["norm5"])
            pe.wait_ge(sem("keys_ready"), TT)
            qk_T(J["sw_T"], columns(proj_c, 0, 8) + [lambda t, h=h: KDUP[:, t, h].rearrange("p d n -> p (d n)")
                                                     for h in range(SWKV)])

            def window_logits(u):
                g = u % 2
                logits(J[f"sw_L{u}"], u // 2, lambda h: (8 * g + h) // 2, lambda h: ((8 * g + h) // 4) * 2 + h % 2)

            window_logits(0)
            for u in range(SW_UNITS):
                if u + 1 < SW_UNITS:
                    window_logits(u + 1)
                g = u % 2
                attended(TT + u, J[f"sw_P{u}"], J[f"sw_O{u}"], u // 2,
                         lambda k, h, g=g: proj_c[:, k, 1280 + ((8 * g + h) // 4) * HD:1280 + ((8 * g + h) // 4 + 1) * HD])
            pe.wait_ge(evac_done, END["sw_O3"])
            norm_T(J["mix2"])
            dense("cout", 2, END["mix2"])
            ffn(1, 6)
            ple(1, 7)


_INS = ['x', 'norm1_w', 'w_in', 'gla_w_alpha', 'gla_b_alpha', 'gla_out_norm_w', 'moba_q_norm_w', 'moba_k_norm_w',
        'mix_scale', 'w_out', 'norm2_w', 'peer_w_query', 'peer_subkeys', 'peer_u', 'peer_v', 'p_2', 'mix_norm_2',
        'ab_w_in_2', 'hg_out_norm_2', 'ab_w_out_2', 'c_w_in_2', 'q_norm_2', 'k_norm_2', 'sinks_2',
        'rel_bias_2', 'c_w_out_2', 'ffn_norm_2', 'ffn_up_2', 'ffn_conv_2', 'ffn_conv_b_2', 'ffn_down_2',
        'ple_norm_2', 'ple_gate_2', 'ple_proj_2']


def kernel(**inputs):
    import numpy as _np
    import concourse.bacc as _bacc
    from concourse.bass_utils import run_bass_kernel_spmd as _run

    nc = _bacc.Bacc("TRN2", target_bir_lowering=False, num_devices=1)
    small, at, levels, onehot, outside = shape_constants()
    arrays, aps = {}, {}
    given = [(n, _np.ascontiguousarray(inputs[n])) for n in _INS]
    given += [("c_small", small), ("c_levels", levels), ("c_onehot", onehot), ("c_outside", outside)]
    for name, arr in given:
        arrays[f"in_{name}"] = arr
        aps[name] = nc.dram_tensor(f"in_{name}", arr.shape, mybir.dt.from_np(arr.dtype), kind="ExternalInput").ap()
    out = nc.dram_tensor("out_0", (1, S, D), F32, kind="ExternalOutput").ap()
    build(nc, aps, out, at)
    r = _run(nc, [arrays], core_ids=[0])
    return r.results[0]["out_0"]
```

```python
from contextlib import ExitStack

import numpy as np

import concourse.bass as bass
from concourse import mybir

F32 = mybir.dt.float32
F32R = mybir.dt.float32r
U32 = mybir.dt.uint32
ALU = mybir.AluOpType
ACT = mybir.ActivationFunctionType
AX = mybir.AxisListType.X

P = 128
D = 1024
S = 256
TT = S // P
KC = D // P
EPS = 1e-6
NEG = -1e30
GH, GDK, GDV, GRANK, CH = 4, 64, 128, 16, 64
HD = 64
PH, NKEYS, TOPK = 8, 128, 16
UNITS = TT * PH
SWH, SWKV, WIN, NBUCK = 16, 4, 128, 32
DFF = 2816
FT = DFF // P
LEVELS = [1, 2, 4, 8, 16, 32]
BANK = 512

PLAN = [("vecs", 1), ("norm0", 4), ("conv", 1), ("relb", 1), ("gr", 1), ("win", 2), ("alpha", 1),
        ("win_1", 4), ("gla_cum", 2), ("gla_dec", 1), ("win_3", 6), ("gla_T", 2), ("mb_T", 4), ("mb_L0", 2), ("mb_L1", 4),
        ("gla_A", 2), ("mb_P0", 2), ("mb_O0", 1), ("gla_U", 3), ("mb_P1", 4), ("mb_O1", 1), ("gla_O", 2),
        ("mix0", 4), ("wout", 4), ("subk", 4), ("norm1", 4), ("query", 3), ("score", 1), ("query_rest", 5), ("score_rest", 7),
        ("peer", 4),
        ("norm2", 4), ("ab", 14), ("sb_T", 4), ("sb_Z", 6), ("hg_B", 2), ("hg_suf", 2), ("hg_T", 4), ("hg_D", 2), ("sb_C", 6),
        ("hg_L0", 2), ("hg_L1", 2), ("sb_O", 2), ("hg_L2", 2), ("hg_L3", 2), ("hg_L4", 2), ("hg_U", 3), ("hg_L5", 2), ("hg_O", 2),
        ("mix1", 4), ("about", 4), ("norm3", 4), ("up0", FT), ("down0", 4), ("norm4", 4), ("pT0", 1), ("gate0", 4),
        ("proj0", 4),
        ("norm5", 4), ("c", 6), ("sw_T", 6)]
SW_UNITS = 4
PLAN += [("sw_L0", 2)]
for _u in range(SW_UNITS):
    PLAN += [(f"sw_L{_u + 1}", 2 if _u + 1 < 2 else 4)] if _u + 1 < SW_UNITS else []
    PLAN += [(f"sw_P{_u}", 2 if _u < 2 else 4), (f"sw_O{_u}", 1)]
PLAN += [("mix2", 4), ("cout", 4), ("norm6", 4), ("up1", FT), ("down1", 4), ("norm7", 4), ("pT1", 1), ("gate1", 4),
         ("proj1", 4)]
J, N = {}, {}
_at = 0
for _name, _n in PLAN:
    J[_name], N[_name] = _at, _n
    _at += _n

END = {k: J[k] + N[k] for k in J}


def chunk_job(name, n):
    if name == "win" and n:
        return J["win_1"] + 2 * (n - 1) if n < 3 else J["win_3"] + 2 * (n - 3)
    return J[name] + 2 * n


def query_job(m):
    return J["query"] + m if m < 3 else J["query_rest"] + m - 3


def score_job(m):
    return J["score"] if m == 0 else J["score_rest"] + m - 1


def shape_constants():
    i = np.arange(P)
    s, t = i[:, None], i[None, :]
    same = (s // CH) == (t // CH)
    cols, at = [], {}

    def put(name, a):
        at[name] = (sum(c.shape[1] for c in cols), a.shape[1])
        cols.append(a.astype(np.float32))

    put("ident", np.eye(P))
    put("cum", same & (s <= t))
    put("suf", same & (s > t))
    put("incl", s >= t)
    put("ones", np.ones((P, P)))
    put("before", s < t)
    put("before_add", np.where(s < t, 0.0, NEG))
    put("causal_add", np.concatenate([np.zeros((P, P)), np.where(t <= s, 0.0, NEG)], 1))
    half = HD // 2
    inv = (np.float32(10000.0) ** (-np.arange(half, dtype=np.float32) / np.float32(half))).astype(np.float32)
    pos = np.arange(S, dtype=np.float32).reshape(TT, P)
    ang = pos[:, :, None] * inv[None, None, :]
    put("cos", np.cos(ang).transpose(1, 0, 2).reshape(P, -1))
    put("sin", np.sin(ang).transpose(1, 0, 2).reshape(P, -1))
    put("head_rows", np.stack([(i // GDK) == (h % 2) for h in range(GH)], 1))
    put("chunk_rows", np.stack([(i // CH) == c for c in range(2)], 1))
    put("iota", np.tile(np.arange(TOPK), (P, 1)))
    small = np.concatenate(cols, 1)
    levels = []
    for half_block in LEVELS:
        b = 2 * half_block
        levels.append((s // b == t // b) & (s % b < half_block) & (t % b >= half_block))
    levels = np.concatenate(levels, 1).astype(np.float32)
    u = np.arange(3 * P)
    dist = 2 * WIN - 1 - u
    band = (dist >= 0) & (dist < WIN)
    exact = NBUCK // 2
    large = exact + (np.log(np.maximum(dist, exact) / exact) / np.log(WIN / exact) * (NBUCK - exact)).astype(np.int32)
    bucket = np.where(dist < exact, np.maximum(dist, 0), np.minimum(large, NBUCK - 1))
    onehot = ((np.arange(NBUCK)[:, None] == bucket[None, :]) & band[None, :]).astype(np.float32)
    outside = np.tile(np.where(band, 0.0, NEG), (SWH, 1)).astype(np.float32)
    return small, at, levels, onehot, outside


def build(nc, a, out, at):
    ctx = ExitStack()
    with ctx:
        sems = {}

        def sem(name):
            if name not in sems:
                sems[name] = ctx.enter_context(nc.semaphore(name))
            return sems[name]

        def sb(name, shape, dt=F32):
            return ctx.enter_context(nc.sbuf_tensor(name, shape, dt))

        SLOT, HALF = 4096, 2048
        O_RAW, O_HI, O_LO, O_SCR, O_XN, O_X, O_T, O_PROJ, O_A, O_B, O_END = np.cumsum(
            [0, 2 * SLOT, 2 * SLOT, 2 * SLOT, 4096, TT * D, TT * D, KC * S, 7168, 4096, 4096]).tolist()
        base = -(-nc.sbuf_base // 64) * 64
        sb("arena", [P, O_END])

        def place(name, shape, col, dt=F32):
            return nc.alloc_sbuf_tensor_at(name, shape, dt, offset=base + 4 * col)

        RAW = place("weights_raw", [P, 2 * SLOT], O_RAW)
        WHI = place("weights_hi", [P, 2 * SLOT], O_HI, F32R)
        WLO = place("weights_lo", [P, 2 * SLOT], O_LO, F32R)
        ROWS = place("expert_rows", [P, 6 * SLOT], O_RAW)
        SCR = place("scratch", [P, 4096], O_SCR)
        XN = place("x_norm", [P, TT, D], O_XN)
        X = place("x_res", [P, TT, D], O_X)
        T = place("work_t", [P, KC * S], O_T)
        XHI = place("x_normT_hi", [P, KC, S], O_T, F32R)
        XLO = place("x_normT_lo", [P, KC, S], O_B + 2048, F32R)
        PROJ = place("proj", [P, 7168], O_PROJ)
        HHI = place("hidden_hi", [P, FT, S], O_PROJ, F32R)
        HLO = place("hidden_lo", [P, FT, S], O_SCR, F32R)
        A = place("work_a", [P, 4096], O_A)
        B = place("work_b", [P, 4096], O_B)
        PHI = place("ple_hi", [P, 2, S], O_B + 1024, F32R)
        PLO = place("ple_lo", [P, 2, S], O_B + 1536, F32R)
        C = sb("consts", [P, sum(n for _, n in at.values())])
        VEC = sb("vec_cols", [P, 72])
        CONV = sb("conv_cols", [P, 2, 4 * 2 * FT])
        GAIN = sb("gain_rows", [P, 2 * GDV + 4 * HD])
        ALB = sb("alpha_bias", [P, GH * GDK])
        SINK = sb("sink_rows", [P, SWH])
        SS = sb("stats", [P, 120])
        PS = ctx.enter_context(nc.psum_tensor("ps", [P, 8, BANK], F32))

        def const(name):
            o, n = at[name]
            return C[:, o:o + n]

        ident, cum, suf, incl, ones = (const(n) for n in ("ident", "cum", "suf", "incl", "ones"))
        causal_add = const("causal_add")
        zeros = causal_add[:, 0:P]
        NORM_COL = {0: 0, 1: None, 2: 8, 3: 24, 4: 40, 5: 16, 6: 32, 7: 48}
        MIX_COL = {0: 56, 1: None, 2: None}
        PAIRS = (0, 1, 2, 3)
        MIX_PAIRS = {0: (2, 3, 0, 1), 1: PAIRS, 2: PAIRS}
        LB_GAIN, HG_GAIN = GAIN[:, 0:GDV], GAIN[:, GDV:2 * GDV]
        QK_GAIN = [GAIN[:, 2 * GDV + n * HD:2 * GDV + (n + 1) * HD] for n in range(4)]

        proj_in = PROJ[:, 0:6144].rearrange("p (t n) -> p t n", t=TT)
        proj_ab = PROJ[:, 0:7168].rearrange("p (t n) -> p t n", t=TT)
        proj_c = PROJ[:, 0:3072].rearrange("p (t n) -> p t n", t=TT)
        BIAS = PROJ[:, 3072:7168].rearrange("p (h s) -> p h s", h=SWH)
        KDUP = T[:, 0:1024].rearrange("p (t h d n) -> p t h d n", t=TT, h=SWKV, d=2)
        KZT = B[:, 0:2048].rearrange("p (v t) -> p v t", v=8)
        QT = B[:, 2048:4096].rearrange("p (v t) -> p v t", v=8)
        PB = [A[:, 0:2048], SCR[:, 0:2048]]
        PT = A[:, 2048:4096].rearrange("p (b t) -> p b t", t=P)
        M0, M1, M2 = (ROWS[:, n * SLOT:(n + 1) * SLOT] for n in (1, 3, 5))
        ST = M1[:, 0:1536].rearrange("p (c h v) -> p c h v", c=3, h=4)
        KSC = M1[:, 1536:3072].rearrange("p (c n) -> p c n", c=3)
        LEV = SCR[:, 3328:4096].rearrange("p (l t) -> p l t", l=6)
        AT = M2[:, 0:1024].rearrange("p (t h n) -> p t h n", t=TT, h=4)
        OUTN = M2[:, 1024:2048].rearrange("p (t n) -> p t n", t=TT)
        SQ = M2[:, 2048:3072].rearrange("p (t n) -> p t n", t=TT)
        DEC = SS[:, 104:112]
        W_GR = SCR[:, 2048:2048 + KC * GRANK].rearrange("p (c n) -> p c n", c=KC)
        W_ALPHA = SCR[0:GRANK, 2176:2432]
        GRT = SCR[0:GRANK, 2432:2688]
        gG, gE = (A[:, n:n + 512] for n in (2048, 2560))
        gB_, gS = (PROJ[:, n:n + 512] for n in (6144, 6656))
        gKST = T[:, 1024:1536].rearrange("p (t n) -> p t n", t=TT)
        gKN = T[:, 0:512].rearrange("p (t n) -> p t n", t=TT)
        gKZT = M0[:, 2048:3072].rearrange("p (h t) -> p h t", h=4)
        gQT = M2[:, 3072:3584].rearrange("p (j t) -> p j t", j=2)
        gDECR = SS[:, 112:120]
        OH = B[0:NBUCK, 0:384]
        RB = B[0:NBUCK, 384:400]
        OUTSIDE = B[0:SWH, 400:784]
        BROW = B[0:SWH, 784:1168]
        VROW = B[0:72, 1200:1328]
        CROW = [B[0:2 * 2 * FT, 1328 + P * n:1328 + P * (n + 1)] for n in range(4)]
        qT = A[:, :].rearrange("p (u t) -> p u t", u=16)
        SKN = SCR[:, 0:2048].rearrange("p (u n) -> p u n", u=16)
        SKT = B[:, 0:2048].rearrange("p (u n) -> p u n", u=16)
        SCORE = PROJ[:, 0:4096]
        N2W = PROJ[:, 4096:5120]
        DIAG = PROJ[:, 5120:6144].rearrange("p (q k n) -> p q k n", q=2, k=4)
        R = PROJ[:, 6144:7168]
        r_s = R[:, 0:256].rearrange("p (q n) -> p q n", q=2)
        r_w = R[:, 256:512]
        r_cand = R[:, 512:768]
        r_sv = R[:, 768:800].rearrange("p (q n) -> p q n", q=2)
        r_top = R[:, 800:816]
        r_sum = R[:, 816:817]
        r_rs = R[:, 817:818]
        r_e = R[:, 820:836]
        r_gate = R[:, 836:868].rearrange("p (q n) -> p q n", q=2)
        r_dot = R[:, 868:876].rearrange("p (q n) -> p q n", q=2)
        r_act = R[:, 876:884].rearrange("p (q n) -> p q n", q=2)
        r_wt = R[:, 884:892].rearrange("p (q n) -> p q n", q=2)
        r_i = R[:, 892:924].rearrange("p (q n) -> p q n", q=2)
        RI = sb("route_idx", [P, 96], U32)
        r_si = RI[:, 0:32].rearrange("p (q n) -> p q n", q=2)
        r_pos = RI[:, 32:48]
        r_ab = sb("route_ab", [P, 32], U32)
        r_idx = RI[:, 64:96].rearrange("p (q n) -> p q n", q=2)
        NU, NV = 8, 16
        ubuf = [ROWS[:, n * D:(n + 1) * D] for n in range(NU)]
        vbuf = [ROWS[:, (NU + n) * D:(NU + n + 1) * D] for n in range(NV)]
        Z0 = A[:, 0:2048].rearrange("p (h t) -> p h t", h=8)
        Z1 = A[:, 2048:3072].rearrange("p (h t) -> p h t", h=8)
        L0 = proj_ab[:, :, 0:1024]
        ZL0 = A[:, 0:2048].rearrange("p (g n) -> p g n", g=2)
        L1 = SCR[:, 0:1024].rearrange("p (h t) -> p h t", h=8)
        SP_BANKS = [L0[:, m // 2, (m % 2) * BANK:(m % 2 + 1) * BANK] for m in range(4)] + [
            SCR[:, m * BANK:(m + 1) * BANK] for m in range(2)]
        hBT, hKT, hE0, hE1 = (M0[:, n * 1024:(n + 1) * 1024] for n in range(4))
        hQT = M1[:, 3072:4096]
        hQB = B[:, 3072:4096]
        hTMP = [x.rearrange("p (t h n) -> p t h n", t=TT, h=4) for x in (M2[:, 3072:4096], SCR[:, 0:1024])]
        hLN = SCR[:, 0:1024].rearrange("p (t n) -> p t n", t=TT)
        hT0 = SCR[:, 1024:2048]
        hKK = A[:, 3072:4096].rearrange("p (t n) -> p t n", t=TT)
        hKST = T[:, 0:1024].rearrange("p (t n) -> p t n", t=TT)
        hSF = T[:, 1024:2048].rearrange("p (t n) -> p t n", t=TT)
        CT = A[:, 0:2048].rearrange("p (q n) -> p q n", q=4)
        GATE = A[:, 2048:4096].rearrange("p (t n) -> p t n", t=TT)
        PIN = B[:, 0:1024].rearrange("p (l t n) -> p l t n", l=2, t=TT)

        PER = 3 * P - 1
        bias_scratch = nc.dram_tensor("bias_scratch", (SWH, P * PER), F32, kind="Internal").ap()

        pe_done, evac_done = sem("pe_done"), sem("evac_done")
        raw_loaded = [sem(f"raw_loaded{h}") for h in range(4)]
        hi_ready = [sem(f"hi_ready{h}") for h in range(4)]
        lo_ready = [sem(f"lo_ready{h}") for h in range(4)]
        xn_ready = [sem(f"xn_ready{t}") for t in range(TT)]
        u_loaded = [sem(f"u_loaded{n}") for n in range(NU)]
        v_loaded = [sem(f"v_loaded{n}") for n in range(NV)]

        def cols512(m, c0, n=512):
            return m[:, c0:c0 + n].rearrange("(c p) n -> p c n", p=P)

        w_in, ab_in, c_in = a["w_in"][0], a["ab_w_in_2"][0], a["c_w_in_2"][0]
        up_w, down_w = a["ffn_up_2"], a["ffn_down_2"]
        FP = FT // 2
        in_cols = [0, 512, 1024, 1552, 2064, 2576]
        WIN_ORDER = [0, 3, 4, 1, 2, 5]
        PIECES = [("win", n, (2 * (n % 2), 4), cols512(w_in, in_cols[c])) for n, c in enumerate(WIN_ORDER)]
        PIECES += [("wout", n, (2 * (n % 2), 4), cols512(a["w_out"][0], 512 * n)) for n in range(2)]
        PIECES += [("query", n, (2 * (n % 2), 4), cols512(a["peer_w_query"][0], 512 * n)) for n in range(4)]
        PIECES += [("ab", n, (2 * (n % 2), 4), cols512(ab_in, 512 * n)) for n in range(7)]
        PIECES += [("about", n, (2 * n, 4), cols512(a["ab_w_out_2"][0], 512 * n)) for n in range(2)]

        RING = 4
        UP_BODIES = FT // RING

        def ffn_and_ple(l):
            off = 2 * l
            down = [(f"down{l}", n, ((off + FT + n) % RING, 2), down_w[l, n * 2 * P:(n + 1) * 2 * P].rearrange("(c p) n -> p c n", p=P))
                    for n in range(FP)]
            up = [(f"up{l}", n, ((off + n) % RING, 2), None) for n in range(FT)]
            return up + down + [(f"gate{l}", n, (2 * ((n + 1 - l) % 2), 4), cols512(a["ple_gate_2"][l], 512 * n)) for n in range(2)] + [
                (f"proj{l}", 0, (2 - 2 * l, 2), a["ple_proj_2"][l].rearrange("(c p) n -> p c n", p=P))]

        PIECES += ffn_and_ple(0)
        PIECES += [("c", n, (2 * (n % 2), 4), cols512(c_in, 512 * n)) for n in range(3)]
        PIECES += [("cout", n, (2 - 2 * n, 4), cols512(a["c_w_out_2"][0], 512 * n)) for n in range(2)]
        PIECES += ffn_and_ple(1)

        class Piece:
            pass

        pieces, holder, uses, dmas = {}, [None] * 4, [0] * 4, [0] * 4
        for name, n, (h, size), src in PIECES:
            w = Piece()
            w.h, w.src, w.cols = h, src, slice(h * HALF, h * HALF + (SLOT if size == 4 else HALF))
            covered = range(h, h + (2 if size == 4 else 1))
            w.before = [x for x in dict.fromkeys(holder[c] for c in covered) if x is not None]
            uses[h] += 1
            dmas[h] += 2 if name.startswith("up") else 1
            w.count, w.landed = uses[h], 16 * dmas[h]
            if name.startswith("down"):
                w.used = (sem("down_used"), (FP - 1) * int(name[-1]) + n + 1) if n < FP - 1 else (pe_done, END[name])
            elif name.startswith("up"):
                w.used = (pe_done, J[name] + n + 1)
            elif name == "query":
                w.used = (pe_done, query_job(2 * n + 1) + 1)
            else:
                w.used = (pe_done, END[name] if name.startswith("proj") else chunk_job(name, n) + 2)
            for c in covered:
                holder[c] = (name, n)
            pieces[name, n] = w

        def part(t, w, c=KC):
            return t[:, w.cols].rearrange("p (c n) -> p c n", c=c)

        def split_hi(eng, copy, name, n):
            w = pieces[name, n]
            eng.wait_ge(raw_loaded[w.h], w.landed)
            for b in w.before:
                eng.wait_ge(*pieces[b].used)
            copy(WHI[:, w.cols], RAW[:, w.cols]).then_inc(hi_ready[w.h], 1)

        def split_lo(eng, name, n):
            w = pieces[name, n]
            eng.wait_ge(raw_loaded[w.h], w.landed)
            eng.wait_ge(hi_ready[w.h], w.count)
            eng.tensor_tensor(WLO[:, w.cols], RAW[:, w.cols], WHI[:, w.cols].bitcast(F32), ALU.subtract).then_inc(lo_ready[w.h], 1)

        def ATT(u):
            return SS[:, 8 + 24 * (u % 2):32 + 24 * (u % 2)]

        block = ctx.enter_context(nc.Block())

        @block.sync
        def _(sp):
            def free(name, n):
                for b in pieces[name, n].before:
                    sp.wait_ge(hi_ready[pieces[b].h], pieces[b].count)
                    sp.wait_ge(lo_ready[pieces[b].h], pieces[b].count)

            def load(name, n):
                w = pieces[name, n]
                free(name, n)
                sp.dma_start(part(RAW, w, w.src.shape[1]), w.src).then_inc(raw_loaded[w.h], 16)

            sp.dma_start(X[:, :, :], a["x"][0].rearrange("(t p) d -> p t d", p=P)).then_inc(sem("x_loaded"), 16)
            sp.dma_start(C[:, :], a["c_small"]).then_inc(sem("const_loaded"), 16)
            rows = [("norm1_w", 8), ("mix_norm_2", 16), ("ffn_norm_2", 16), ("ple_norm_2", 16), ("mix_scale", 8)]
            r = 0
            for name, n in rows:
                sp.dma_start(VROW[r:r + n, :], a[name].rearrange("l (c p) -> (l c) p", p=P)).then_inc(sem("vec_loaded"), 16)
                r += n
            load("win", 0)
            sp.dma_start(W_GR, cols512(w_in, 1536, GRANK)).then_inc(sem("gr_loaded"), 16)
            sp.dma_start(W_ALPHA, a["gla_w_alpha"][0]).then_inc(sem("gr_loaded"), 16)
            for l in range(2):
                taps = a["ffn_conv_2"][l].rearrange("k (c p) -> (k c) p", p=P)
                sp.dma_start(CROW[2 * l][:, :], taps[0:4 * FT, :]).then_inc(sem("conv_loaded"), 16)
                sp.dma_start(CROW[2 * l + 1][0:2 * FT, :], taps[4 * FT:6 * FT, :]).then_inc(sem("conv_loaded"), 16)
                sp.dma_start(CROW[2 * l + 1][2 * FT:4 * FT, :],
                             a["ffn_conv_b_2"][l:l + 1, :].rearrange("k (c p) -> (k c) p", p=P)).then_inc(sem("conv_loaded"), 16)
            sp.dma_start(OH, a["c_onehot"]).then_inc(sem("rel_loaded"), 16)
            sp.dma_start(RB, a["rel_bias_2"]).then_inc(sem("rel_loaded"), 16)
            sp.dma_start(OUTSIDE, a["c_outside"]).then_inc(sem("rel_loaded"), 16)
            load("win", 1)
            for dst, src in ((LB_GAIN, a["gla_out_norm_w"]), (HG_GAIN, a["hg_out_norm_2"]), (QK_GAIN[0], a["moba_q_norm_w"]),
                             (QK_GAIN[1], a["moba_k_norm_w"]), (QK_GAIN[2], a["q_norm_2"]), (QK_GAIN[3], a["k_norm_2"]),
                             (ALB[:, :], a["gla_b_alpha"]), (SINK[:, :], a["sinks_2"])):
                sp.dma_start(dst, src[0].partition_broadcast(P)).then_inc(sem("gain_loaded"), 16)
            sp.dma_start(SCR[:, 3328:4096], a["c_levels"]).then_inc(sem("levels_loaded"), 16)
            for n in range(2, 4):
                load("win", n)
            sp.wait_ge(evac_done, END["relb"])
            sp.dma_start(bias_scratch.rearrange("h (t u) -> h t u", u=PER),
                         BROW[:, 0:PER].unsqueeze(1).broadcast_to([SWH, P, PER])).then_inc(sem("bias_written"), 16)
            for n in range(4, 6):
                load("win", n)
            load("wout", 0)
            sp.wait_ge(pe_done, END["gla_A"])
            load("wout", 1)
            for n in range(2):
                load("query", n)
            sp.wait_ge(evac_done, END["mb_O1"])
            sp.dma_start(N2W, a["norm2_w"][0].partition_broadcast(P)).then_inc(sem("n2w_loaded"), 16)
            sp.dma_start(SKN, a["peer_subkeys"][0].rearrange("h q k d -> k (h q) d")).then_inc(sem("subkeys_loaded"), 16)
            for n in range(2, 4):
                load("query", n)
            sp.wait_ge(sem("dots_done"), 4 * UNITS)
            for n in range(7):
                load("ab", n)
            load("about", 0)
            sp.wait_ge(pe_done, END["hg_L5"])
            sp.wait_ge(sem("h_bexp"), 1)
            load("about", 1)

            def ffn_loads(l):
                def load_up(h, col):
                    src = up_w[l].rearrange("(c p) (g n) -> p c g n", p=P, g=2)
                    dst = RAW[:, h * HALF:(h + 1) * HALF].rearrange("p (c g n) -> p c g n", c=KC, g=2)
                    for g in range(2):
                        sp.dma_start(dst[:, :, g, :], src[:, :, g, bass.ds(col, P)]).then_inc(raw_loaded[h], 16)

                def peeled(n):
                    free(f"up{l}", n)
                    load_up(pieces[f"up{l}", n].h, n * P)

                for n in range(RING):
                    peeled(n)
                with sp.Fori(1, UP_BODIES) as i:
                    for q in range(RING):
                        w = pieces[f"up{l}", q]
                        sp.wait_ge(hi_ready[w.h], i + (w.count - 1))
                        sp.wait_ge(lo_ready[w.h], i + (w.count - 1))
                        load_up(w.h, i * (RING * P) + q * P)
                for n in range(RING * UP_BODIES, FT):
                    peeled(n)
                for n in range(FP):
                    load(f"down{l}", n)
                load(f"gate{l}", 0)

            def ple_loads(l):
                sp.dma_start(PIN[:, l], a["p_2"][l, 0].rearrange("(t p) n -> p t n", p=P)).then_inc(sem("p_loaded"), 16)
                load(f"gate{l}", 1)
                load(f"proj{l}", 0)

            ffn_loads(0)
            ple_loads(0)
            for n in range(3):
                load("c", n)
            sp.wait_ge(sem("bias_written"), 16)
            sp.wait_ge(pe_done, END["down0"])
            sp.dma_start(BIAS, bass.AP(bias_scratch.tensor, P - 1, [[PER - 1, P], [P * PER, SWH], [1, 2 * P]])
                         ).then_inc(sem("bias_loaded"), 16)
            for n in range(2):
                load("cout", n)
            ffn_loads(1)
            ple_loads(1)
            for t in range(TT):
                sp.wait_ge(sem("x_final"), t + 1)
                sp.dma_start(out[0, t * P:(t + 1) * P, :], X[:, t, :]).then_inc(sem("out_written"), 16)
            sp.wait_ge(sem("out_written"), 16 * TT)

        @block.gpsimd
        def _(pool):
            def split(name, n):
                split_lo(pool, name, n)

            def chunk_keys(keys, decay, width, part):
                pool.tensor_tensor(keys, part, decay, ALU.mult).then_inc(sem("keys_decayed"), 1)
                pool.wait_ge(sem("keys_decayed"), 1 if width == 256 else 2)
                for c in range(3):
                    rows = const("chunk_rows")[:, c % 2:c % 2 + 1].broadcast_to([P, width])
                    pool.tensor_tensor(KSC[:, c, 0:width], keys[:, c // 2], rows, ALU.mult).then_inc(sem("kst_ready"), 1)

            def gated_gain(gain, gates):
                for t in range(TT):
                    g4 = gates[:, t].rearrange("p (h n) -> p h n", n=GDV)
                    pool.tensor_tensor(g4, g4, gain.unsqueeze(1).broadcast_to([P, 4, GDV]), ALU.mult).then_inc(sem("gates_gained"), 1)

            split("win", 1)
            split("win", 3)
            pool.wait_ge(sem("g_exp"), 3)
            pool.wait_ge(pe_done, END["win_3"])
            chunk_keys(gKST, gS.rearrange("p (t n) -> p t n", t=TT), 256, proj_in[:, :, 256:512])
            pool.wait_ge(sem("silu_gate"), 1)
            gated_gain(LB_GAIN, proj_in[:, :, 1024:1536])
            split("wout", 0)
            for n in range(2):
                split("query", n)

            def unit(u, q, first=False):
                def hold(s, value):
                    pool.wait_ge(sem(s), value)
                    if not isinstance(value, int):
                        pool.sem_inc(sem("gather_holds"))

                hold("idx_ready", u + 1)
                for b in range(4):
                    if first and b < 2:
                        w = pieces["query", 2 + b]
                        pool.wait_ge(hi_ready[w.h], w.count)
                        pool.wait_ge(lo_ready[w.h], w.count)
                    else:
                        hold("dots_done", u * 4 + (b - 1))
                    for k in range(4):
                        n = (4 * b + k) % NU
                        nc.gpsimd.indirect_dma_start(
                            out=ubuf[n], out_offset=None, in_=a["peer_u"][0],
                            in_offset=bass.IndirectOffsetOnAxis(ap=r_idx[:, q, 4 * b + k:4 * b + k + 1], axis=0)
                        ).then_inc(u_loaded[n], 16)
                    if not first:
                        hold("rows_summed", u * 4 + (b - 3))
                    elif b < 2:
                        pool.wait_ge(*pieces["query", 2 + b].used)
                    for k in range(4):
                        n = 4 * b + k
                        nc.gpsimd.indirect_dma_start(
                            out=vbuf[n], out_offset=None, in_=a["peer_v"][0],
                            in_offset=bass.IndirectOffsetOnAxis(ap=r_idx[:, q, n:n + 1], axis=0)
                        ).then_inc(v_loaded[n], 16)

            unit(0, 0, first=True)
            unit(1, 1)
            with pool.Fori(1, UNITS // 2) as i:
                unit(i * 2, 0)
                unit(i * 2 + 1, 1)

            pool.wait_ge(pe_done, END["peer"])
            for n in range(2):
                split("ab", n)
            pool.wait_ge(sem("h_sufexp"), 1)
            chunk_keys(hKST, hSF, 512, hKK)
            pool.wait_ge(sem("sb_plus"), 3)
            for z in (Z0[:, :, 0:P], Z1):
                pool.tensor_tensor(z, z, const("before_add").unsqueeze(1).broadcast_to([P, 8, P]), ALU.add).then_inc(sem("z_masked"), 1)
            pool.wait_ge(evac_done, END["hg_T"])
            pool.wait_ge(sem("h_bexp"), 1)
            pool.tensor_tensor(hQB, hQT, hT0, ALU.mult).then_inc(sem("h_qb"), 1)
            pool.wait_ge(sem("h_silu"), 2)
            gated_gain(HG_GAIN, proj_ab[:, :, 3072:3584])
            for n in range(len(LEVELS) - 1):
                pool.wait_ge(sem("level_masked"), n + 1)
                pool.tensor_tensor(AT, AT, hTMP[n % 2], ALU.add).then_inc(sem("level_added"), 1)
                pool.wait_ge(sem("level_added"), n + 1)
            split("about", 0)
            for l in range(2):
                for n in range(RING):
                    split(f"up{l}", n)

                def hidden(i, tiles):
                    for q in range(tiles):
                        pool.wait_ge(sem("silu_done"), i * RING + (FT * l + q + 1))
                        g, u = CT[:, q, 0:S], CT[:, q, S:2 * S]
                        hi = HHI[:, :, :].rearrange("p c t -> p (c t)")[:, bass.ds(i * (RING * S) + q * S, S)]
                        lo = HLO[:, :, :].rearrange("p c t -> p (c t)")[:, bass.ds(i * (RING * S) + q * S, S)]
                        pool.tensor_tensor(hi, g, u, ALU.mult).then_inc(sem("hidden_hi_ready"), 1)
                        pool.tensor_tensor(g, g, u, ALU.mult).then_inc(sem("hidden_full"), 1)
                        pool.wait_ge(sem("hidden_full"), i * RING + (FT * l + q + 1))
                        pool.wait_ge(sem("hidden_hi_ready"), i * RING + (FT * l + q + 1))
                        pool.tensor_tensor(lo, g, hi.bitcast(F32), ALU.subtract).then_inc(sem("hidden_ready"), 1)

                with pool.Fori(0, UP_BODIES) as i:
                    hidden(i, RING)
                hidden(UP_BODIES, FT % RING)
                for n in range(2):
                    split(f"gate{l}", n)
                split(f"proj{l}", 0)
                if l == 0:
                    for name in ("c", "cout"):
                        for n in range(2):
                            split(name, n)

        @block.scalar
        def _(act):
            own = [0]

            def link(ins):
                own[0] += 1
                ins.then_inc(sem("act_chain"), 1)
                act.wait_ge(sem("act_chain"), own[0])

            root_no, rstd = [0], sem("root_done")

            def root(dst, src, n):
                root_no[0] += 1
                act.wait_ge(sem("sumsq_ready"), root_no[0])
                nc.scalar.activation(dst, src, ACT.Sqrt, bias=eps_col, scale=1.0 / n).then_inc(rstd, 1)

            def x_hi(j, col=None, pairs=PAIRS, jobs=(0, 1, 2, 3)):
                for n in jobs:
                    m = pairs[n]
                    act.wait_ge(pe_done, j + n + 1)
                    if col is None:
                        ins = act.copy(XHI[:, 2 * m:2 * m + 2, :], PS[:, (j + n) % 8, :].rearrange("p (c t) -> p c t", c=2))
                    for c in range(0 if col is None else 2):
                        f = 2 * m + c
                        ins = nc.scalar.activation(XHI[:, f, :], PS[:, (j + n) % 8, c * S:(c + 1) * S], ACT.Copy,
                                                   scale=VEC[:, col + f:col + f + 1])
                    ins.then_inc(sem("x_hi_ready"), 1)

            def sqrt_table():
                nc.scalar.activation(SS[:, 94:95], eps_col, ACT.Sqrt)

            rstd_no = [0]

            def norm(k, between=()):
                root(SS[:, 2:4], SS[:, 0:2], D)
                if NORM_COL[k] is not None:
                    rstd_no[0] += 1
                    act.wait_ge(sem("rstd_ready"), rstd_no[0])
                    for m in range(2):
                        cols = slice(m * BANK, (m + 1) * BANK)
                        nc.scalar.activation(XN[:, 1, cols], X[:, 1, cols], ACT.Copy, scale=SS[:, 3:4]).then_inc(xn_ready[1], 1)
                for piece in between:
                    split(*piece)
                x_hi(J[f"norm{k}"], NORM_COL[k])

            def split(name, n):
                split_hi(act, act.copy, name, n)

            eps_col = SS[:, 95:96]
            act.wait_ge(sem("eps_ready"), 1)
            sqrt_table()
            norm(0, between=[("win", 0)])
            for n in range(1, 3):
                split("win", n)
            act.wait_ge(sem("g_abs"), 1)
            link(nc.scalar.activation(gE, gE, ACT.Exp, scale=-1.0))
            nc.scalar.activation(gE, gE, ACT.Ln, bias=1.0).then_inc(sem("g_log"), 1)
            def moba_root(n):
                root(SS[:, 56 + 16 * n:72 + 16 * n], SS[:, 8 + 16 * n:24 + 16 * n], HD)

            split("win", 3)
            moba_root(0)
            split("win", 4)
            act.wait_ge(evac_done, END["gla_cum"])
            nc.scalar.activation(gE, gB_, ACT.Exp).then_inc(sem("g_exp"), 1)
            nc.scalar.activation(gB_, gB_, ACT.Exp, scale=-1.0).then_inc(sem("g_exp"), 1)
            nc.scalar.activation(gS, gS, ACT.Exp).then_inc(sem("g_exp"), 1)
            act.wait_ge(evac_done, END["gla_dec"])
            nc.scalar.activation(DEC, gDECR, ACT.Exp).then_inc(sem("g_exp"), 1)
            split("win", 5)
            moba_root(1)
            act.wait_ge(evac_done, chunk_job("win", 4) + 2)
            nc.scalar.activation(proj_in[:, :, 1024:1536], proj_in[:, :, 1024:1536], ACT.Silu).then_inc(sem("silu_gate"), 1)

            att_no = [0]

            def exp_unit(t, sink=None):
                u, cols = att_no[0], (t + 1) * P
                att_no[0] += 1
                neg_max = ATT(u)[:, 8:16]
                act.wait_ge(sem("att_max"), u + 1)
                for h in range(8):
                    w = PB[u % 2][:, h * cols:(h + 1) * cols]
                    ins = nc.scalar.activation(w, w, ACT.Exp, bias=neg_max[:, h:h + 1])
                ins.then_inc(sem("att_exp"), 1)
                if sink:
                    nc.scalar.activation(ATT(u)[:, 0:8], ATT(u)[:, 0:8], ACT.Exp).then_inc(sem("sink_exp"), 1)

            def weights_out(j, t):
                for m in range(2 * (t + 1)):
                    act.wait_ge(pe_done, j + m + 1)
                    act.wait_ge(evac_done, j + m)
                    act.copy(PT[:, 4 * m:4 * m + 4, :], PS[:, (j + m) % 8, :].rearrange("p (b t) -> p b t", b=4)).then_inc(evac_done, 1)

            exp_unit(0)
            exp_unit(1)
            weights_out(J["mb_P0"], 0)
            weights_out(J["mb_P1"], 1)
            split("wout", 0)

            def mixed(k, second):
                sqrt_table()
                x_hi(J[f"mix{k}"], MIX_COL[k], MIX_PAIRS[k], (0, 1))
                root(SS[:, 16:24], SS[:, 8:16], GDV)
                split(second, 1)
                x_hi(J[f"mix{k}"], MIX_COL[k], MIX_PAIRS[k], (2, 3))

            mixed(0, "wout")
            sqrt_table()
            for n in range(2):
                split("query", n)
            norm(1)

            def gate_exp(u):
                act.wait_ge(sem("top_ready"), u + 1)
                nc.scalar.activation(r_e, r_e, ACT.Exp).then_inc(sem("gate_exp"), 1)

            def gelu(u, b):
                act.wait_ge(sem("dots_done"), u * 4 + (b + 1))
                nc.scalar.activation(r_act[:, b % 2], r_dot[:, b % 2], ACT.Gelu).then_inc(sem("gelu_done"), 1)

            def diag(u, b, wait=True):
                act.wait_ge(sem("weights_ready"), u * 4 + (b + 1))
                if wait:
                    act.wait_ge(sem("rows_summed"), u * 4 + (b - 1))
                for k in range(4):
                    ins = nc.scalar.activation(DIAG[:, b % 2, k, :], ident, ACT.Copy, scale=r_wt[:, b % 2, k:k + 1])
                ins.then_inc(sem("diag_ready"), 1)

            def act_unit(u, first=False, last=False):
                for b in range(4):
                    gelu(u, b)
                    if b > 0:
                        diag(u, b - 1, wait=not (first and b <= 2))
                    elif not first:
                        diag(u - 1, 3)
                    if b == 1 and not last:
                        gate_exp(u + 1)

            for n in range(2, 4):
                split("query", n)
            gate_exp(0)
            act_unit(0, first=True)
            act_unit(1)
            with act.Fori(1, UNITS // 2 - 1) as i:
                act_unit(i * 2)
                act_unit(i * 2 + 1)
            act_unit(UNITS - 2)
            act_unit(UNITS - 1, last=True)
            diag(UNITS - 1, 3)

            sqrt_table()
            act.wait_ge(pe_done, END["peer"])
            for n in range(2):
                split("ab", n)
            norm(2)
            for n in range(2, 7):
                split("ab", n)
            hq, hf, hg = proj_ab[:, :, 1536:2048], proj_ab[:, :, 2048:2560], proj_ab[:, :, 3072:3584]
            act.wait_ge(sem("h_abs"), 1)
            nc.scalar.activation(hKK, hf, ACT.Sigmoid, scale=-1.0).then_inc(sem("h_sig"), 1)
            link(nc.scalar.activation(hLN, hLN, ACT.Exp, scale=-1.0))
            nc.scalar.activation(hLN, hLN, ACT.Ln, bias=1.0).then_inc(sem("h_log"), 1)
            nc.scalar.activation(hq, hq, ACT.Silu).then_inc(sem("h_silu"), 1)
            act.wait_ge(evac_done, END["ab"])
            nc.scalar.activation(hg, hg, ACT.Silu).then_inc(sem("h_silu"), 1)
            for t, banks in ((L0, 4), (L1, 6)):
                act.wait_ge(sem("sb_abs"), banks)
                link(nc.scalar.activation(t, t, ACT.Exp, scale=-1.0))
            nc.scalar.activation(L0, L0, ACT.Ln, bias=1.0).then_inc(sem("sb_log"), 1)
            nc.scalar.activation(L1, L1, ACT.Ln, bias=1.0).then_inc(sem("sb_log"), 1)
            act.wait_ge(evac_done, END["hg_suf"])
            nc.scalar.activation(hSF, hSF, ACT.Exp).then_inc(sem("h_sufexp"), 1)
            nc.scalar.activation(hT0, hBT, ACT.Exp).then_inc(sem("h_bexp"), 1)
            for n, L in enumerate(LEVELS):
                act.wait_ge(sem("h_rel"), n + 1)
                e = (hE0 if n % 2 == 0 else hE1).rearrange("p (b i) -> p b i", i=2 * L)
                nc.scalar.activation(e[:, :, L:2 * L], e[:, :, L:2 * L], ACT.Exp).then_inc(sem("h_relexp"), 1)
                nc.scalar.activation(e[:, :, 0:L], e[:, :, 0:L], ACT.Exp, scale=-1.0).then_inc(sem("h_relexp"), 1)
                if n == 1:
                    act.wait_ge(evac_done, END["sb_C"])
                    nc.scalar.activation(Z0, Z0, ACT.Exp).then_inc(sem("sb_exp"), 1)
                    nc.scalar.activation(Z1, Z1, ACT.Exp).then_inc(sem("sb_exp"), 1)
            split("about", 0)
            mixed(1, "about")

            def act_ffn(l, k):
                j0 = J[f"up{l}"]
                sqrt_table()
                for n in range(RING):
                    split(f"up{l}", n)
                norm(k)

                def step(i, tiles, more):
                    def silu(q):
                        act.wait_ge(evac_done, i * RING + (j0 + q + 1))
                        nc.scalar.activation(CT[:, q, 0:S], CT[:, q, 0:S], ACT.Silu).then_inc(sem("silu_done"), 1)

                    for q in range(tiles):
                        act.wait_ge(pe_done, i * RING + (j0 + q + 1))
                        for g in range(2):
                            ins = nc.scalar.activation(CT[:, q, g * S:(g + 1) * S], PS[:, (j0 + q) % 8, g * S:(g + 1) * S], ACT.Identity,
                                                       bias=CONV[:, l, bass.ds(i * RING + (3 * 2 * FT + g * FT + q), 1)],
                                                       scale=CONV[:, l, bass.ds(i * RING + (2 * 2 * FT + g * FT + q), 1)])
                        ins.then_inc(sem("tap2_done"), 1)
                        if more is None:
                            w = pieces[f"up{l}", q]
                            act.wait_ge(raw_loaded[w.h], i * 32 + (w.landed + 32))
                            act.copy(WHI[:, w.cols], RAW[:, w.cols]).then_inc(hi_ready[w.h], 1)
                        else:
                            split(*more[q])
                        if q:
                            silu(q - 1)
                    silu(tiles - 1)
                    act.wait_ge(sem("hidden_ready"), i * RING + (FT * l + tiles))

                with act.Fori(0, UP_BODIES - 1) as i:
                    step(i, RING, None)
                ring = [(f"up{l}", n) for n in range(FT)] + [(f"down{l}", n) for n in range(FP)]
                step(UP_BODIES - 1, RING, ring[RING * UP_BODIES:])
                step(UP_BODIES, FT % RING, ring[RING * UP_BODIES + RING:])
                for n in range(RING, FP):
                    split(f"down{l}", n)
                sqrt_table()
                for n in range(2):
                    split(f"gate{l}", n)

            def act_ple(l, k):
                norm(k)
                split(f"proj{l}", 0)
                act.wait_ge(evac_done, END[f"gate{l}"])
                nc.scalar.activation(GATE, GATE, ACT.Sigmoid).then_inc(sem("ple_sigmoid"), 1)

            act_ffn(0, 3)
            act_ple(0, 4)
            sqrt_table()
            for n in range(2):
                split("c", n)
            norm(5)
            split("c", 2)
            for n in range(2):
                root(SS[:, 56 + 16 * n:72 + 16 * n], SS[:, 8 + 16 * n:24 + 16 * n], HD)
            root(SS[:, 48:56], SS[:, 40:48], HD)
            for n in range(2):
                split("cout", n)
            exp_unit(0, sink=True)
            for u in range(SW_UNITS):
                weights_out(J[f"sw_P{u}"], u // 2)
                if u + 1 < SW_UNITS:
                    exp_unit((u + 1) // 2, sink=True)
            x_hi(J["mix2"])
            act_ffn(1, 6)
            act_ple(1, 7)

        @block.vector
        def _(v):
            own, counts = [0], {}

            def step(ins, s=None, wait=True):
                s = s or "dve_chain"
                counts[s] = counts.get(s, 0) + 1
                ins.then_inc(sem(s), 1)
                if wait:
                    v.wait_ge(sem(s), counts[s])

            def bank(j):
                v.wait_ge(pe_done, j + 1)
                return PS[:, j % 8, :]

            def freed(ins, j, wait=False):
                ins.then_inc(evac_done, 1)
                if wait:
                    v.wait_ge(evac_done, j + 1)

            def bc(ap, n, axis=2):
                x = ap.unsqueeze(axis)
                shape = list(x.shape)
                shape[axis] = n
                return x.broadcast_to(shape)

            norm_no = [0]

            def reciprocal_root(dst, src):
                norm_no[0] += 1
                v.wait_ge(sem("root_done"), norm_no[0])
                step(nc.vector.reciprocal(dst, src))

            def transposed(j, n, dst, col=None):
                for m in range(n):
                    src = bank(j + m)[:, :].rearrange("p (c t) -> p c t", c=2)
                    d = dst[:, 2 * m:2 * m + 2, :]
                    if col is None:
                        freed(nc.vector.tensor_copy(d, src), j + m)
                    else:
                        freed(nc.vector.tensor_tensor(d, src, bc(VEC[:, col + 2 * m:col + 2 * m + 2], S), ALU.mult), j + m)
                v.wait_ge(evac_done, j + n)

            def key_pairs(j, n, dst):
                for m in range(n):
                    src = bank(j + m).rearrange("p (c t) -> p c t", c=2)
                    for par in range(2):
                        d = dst[:, 4 * m:4 * m + 4, :].rearrange("p (c h) t -> p c h t", h=2)[:, :, par, :]
                        ins = nc.vector.tensor_scalar(d, src, const("head_rows")[:, par:par + 1], None, ALU.mult)
                    freed(ins, j + m)
                v.wait_ge(evac_done, j + n)

            hi_no = [0]

            def x_lo(j, col=None, pairs=PAIRS):
                for n, m in enumerate(pairs):
                    src = bank(j + n)
                    hi_no[0] += 1
                    v.wait_ge(sem("x_hi_ready"), hi_no[0])
                    if col is None:
                        ins = nc.vector.tensor_tensor(XLO[:, 2 * m:2 * m + 2, :], src.rearrange("p (c t) -> p c t", c=2),
                                                      XHI[:, 2 * m:2 * m + 2, :].bitcast(F32), ALU.subtract)
                    for c in range(0 if col is None else 2):
                        f = 2 * m + c
                        ins = nc.vector.scalar_tensor_tensor(out=XLO[:, f, :], in0=src[:, c * S:(c + 1) * S],
                                                             scalar=VEC[:, col + f:col + f + 1],
                                                             in1=XHI[:, f, :].bitcast(F32), op0=ALU.mult, op1=ALU.subtract)
                    freed(ins, j + n)
                v.wait_ge(evac_done, j + 4)

            def norm(k, gain=None):
                if k == 0:
                    for t in range(TT):
                        step(nc.vector.tensor_tensor_reduce(out=XN[:, t], in0=X[:, t], in1=X[:, t], scale=1.0, scalar=0.0,
                                                            op0=ALU.mult, op1=ALU.add, accum_out=SS[:, t:t + 1]),
                             "sumsq_ready" if t == TT - 1 else None)
                else:
                    step(nc.vector.tensor_tensor(SS[:, 0:2], SS[:, 96:100:2], SS[:, 97:100:2], ALU.add), "sumsq_ready")
                norm_no[0] += 1
                v.wait_ge(sem("root_done"), norm_no[0])
                step(nc.vector.reciprocal(SS[:, 2:4], SS[:, 2:4]), None if gain is not None else "rstd_ready")
                for m in range(2):
                    cols = slice(m * BANK, (m + 1) * BANK)
                    if gain is None:
                        step(nc.vector.tensor_scalar(XN[:, 0, cols], X[:, 0, cols], SS[:, 2:3], None, ALU.mult), "xn_ready0", False)
                        continue
                    for t in range(TT):
                        step(nc.vector.scalar_tensor_tensor(out=XN[:, t, cols], in0=X[:, t, cols], scalar=SS[:, 2 + t:3 + t],
                                                            in1=gain[:, cols], op0=ALU.mult, op1=ALU.mult), f"xn_ready{t}", False)
                x_lo(J[f"norm{k}"], NORM_COL[k])

            def evac_cols(name, n, dst, behind=None, order=None):
                for m in range(n):
                    j = chunk_job(name, m)
                    for t in range(TT):
                        c = order[m] if order else m
                        freed(nc.vector.tensor_copy(dst[:, t, c * BANK:(c + 1) * BANK], bank(j + t)), j + t)
                    if m + 2 < n and (name, m + 2) != ("win", 3):
                        split_lo(v, name, m + 2)
                    if behind and m in behind:
                        v.wait_ge(evac_done, j + 2)
                        behind[m]()
                v.wait_ge(evac_done, j + 2)

            def sum_squares(t, m):
                d, k = X[:, t, m * BANK:(m + 1) * BANK], 2 * t + m
                step(nc.vector.tensor_tensor_reduce(out=A[:, k * BANK:(k + 1) * BANK], in0=d, in1=d, scale=1.0, scalar=0.0,
                                                    op0=ALU.mult, op1=ALU.add, accum_out=SS[:, 96 + k:97 + k]), "sumsq_part",
                     wait=(k == 3))

            def add_residual(j, by_tile=False):
                for n in range(4):
                    t, m = (n // 2, n % 2) if by_tile else (n % 2, n // 2)
                    d = X[:, t, m * BANK:(m + 1) * BANK]
                    freed(nc.vector.tensor_tensor(d, bank(j + n), d, ALU.add), j + n, True)
                    sum_squares(t, m)

            step(nc.vector.memset(SS[:, 95:96], EPS), "eps_ready")
            v.wait_ge(sem("const_loaded"), 16)
            freed(nc.vector.tensor_copy(VEC[:, 0:64], bank(J["vecs"])[:, 0:64]), J["vecs"])
            v.wait_ge(sem("x_loaded"), 16)
            norm(0)
            split_lo(v, "win", 0)
            freed(nc.vector.tensor_copy(CONV[:, :, :], bank(J["conv"])[:, 0:8 * 2 * FT].rearrange("p (l n) -> p l n", l=2)),
                  J["conv"])
            v.wait_ge(sem("rel_loaded"), 48)
            freed(nc.vector.tensor_tensor(BROW, bank(J["relb"])[0:SWH, 0:384], OUTSIDE, ALU.add), J["relb"], wait=True)
            v.wait_ge(sem("gain_loaded"), 16 * 8)

            half = HD // 2

            def head_norms(view, n, ss, rs, gain, rope=False, ready=None):
                sq = A[:, 0:TT * n * HD].rearrange("p (t h n) -> p t h n", t=TT, n=HD)
                step(nc.vector.tensor_tensor(sq, view, view, ALU.mult))
                for t in range(TT):
                    step(nc.vector.tensor_reduce(ss[:, t * n:(t + 1) * n], sq[:, t], AX, ALU.add),
                         "sumsq_ready" if t == TT - 1 else None)
                reciprocal_root(rs, rs)
                for t in range(TT):
                    x = view[:, t]
                    step(nc.vector.tensor_tensor(x, x, bc(rs[:, t * n:(t + 1) * n], HD), ALU.mult))
                    step(nc.vector.tensor_tensor(x, x, bc(gain, n, 1), ALU.mult), ready if t == TT - 1 else None)
                    if not rope:
                        continue
                    x1, x2 = x[:, :, 0:half], x[:, :, half:HD]
                    cos = bc(const("cos")[:, t * half:(t + 1) * half], n, 1)
                    sin = bc(const("sin")[:, t * half:(t + 1) * half], n, 1)
                    x1c, x2s, x2c, x1s = (A[:, k * n * half:(k + 1) * n * half].rearrange("p (h n) -> p h n", h=n)
                                          for k in range(4 * t, 4 * t + 4))
                    step(nc.vector.tensor_tensor(x1c, x1, cos, ALU.mult), wait=False)
                    step(nc.vector.tensor_tensor(x2s, x2, sin, ALU.mult), wait=False)
                    step(nc.vector.tensor_tensor(x2c, x2, cos, ALU.mult), wait=False)
                    step(nc.vector.tensor_tensor(x1s, x1, sin, ALU.mult))
                    step(nc.vector.tensor_tensor(x1, x1c, x2s, ALU.subtract), wait=False)
                    step(nc.vector.tensor_tensor(x2, x2c, x1s, ALU.add))

            def heads_of(proj, c0, n):
                return proj[:, :, c0:c0 + n * HD].rearrange("p t (h n) -> p t h n", n=HD)

            def moba_qk(n):
                head_norms(heads_of(proj_in, 1536 + 512 * n, 8), 8, SS[:, 8 + 16 * n:24 + 16 * n],
                           SS[:, 56 + 16 * n:72 + 16 * n], QK_GAIN[n], rope=True)

            def gla_gate():
                g2 = gG.rearrange("p (t n) -> p t n", t=TT)
                freed(nc.vector.tensor_tensor(g2, bank(J["alpha"]).rearrange("p (t n) -> p t n", t=TT),
                                              bc(ALB[:, :], TT, 1), ALU.add), J["alpha"], wait=True)
                step(nc.vector.scalar_tensor_tensor(out=gE, in0=gG, scalar=-1.0, in1=gG, op0=ALU.mult, op1=ALU.max), "g_abs")

            def gla_log_gate():
                v.wait_ge(sem("g_log"), 1)
                step(nc.vector.scalar_tensor_tensor(out=gG, in0=gG, scalar=0.0, in1=gE, op0=ALU.min, op1=ALU.subtract))
                step(nc.vector.tensor_scalar(gG, gG, 1.0 / 16.0, None, ALU.mult), "g_ready")

            def gla_sums():
                freed(nc.vector.tensor_copy(gB_, bank(J["gla_cum"])), J["gla_cum"])
                freed(nc.vector.tensor_copy(gS, bank(J["gla_cum"] + 1)), J["gla_cum"] + 1)
                freed(nc.vector.tensor_copy(gDECR, bank(J["gla_dec"])[:, 0:8]), J["gla_dec"], wait=True)

            freed(nc.vector.tensor_copy(GRT, bank(J["gr"])[0:GRANK, 0:S]), J["gr"], wait=True)
            def moba_queries():
                gla_log_gate()
                moba_qk(0)

            evac_cols("win", 6, proj_in, {0: gla_gate, 1: moba_queries, 2: gla_sums, 3: lambda: moba_qk(1)}, WIN_ORDER)

            def head_norm(first_job, gates, dst):
                for t in range(TT):
                    freed(nc.vector.tensor_copy(OUTN[:, t], bank(first_job + t)), first_job + t, True)
                    step(nc.vector.tensor_tensor(SQ[:, t], OUTN[:, t], OUTN[:, t], ALU.mult), wait=(t == 1))
                step(nc.vector.tensor_reduce(SS[:, 8:16], SQ.rearrange("p t (h n) -> p (t h) n", n=GDV), AX, ALU.add), "sumsq_ready")
                step(nc.vector.tensor_tensor(OUTN, OUTN, gates, ALU.mult))
                reciprocal_root(SS[:, 16:24], SS[:, 16:24])
                for t in range(TT):
                    o4, d4 = (x[:, t].rearrange("p (h n) -> p h n", n=GDV) for x in (OUTN, dst))
                    step(nc.vector.tensor_tensor(d4, o4, bc(SS[:, 16 + 4 * t:20 + 4 * t], GDV), ALU.mult), "mixed", t == 1)

            att_no = [0]

            def logits(j, t, add, sink=None):
                u, cols = att_no[0], (t + 1) * P
                att_no[0] += 1
                per = BANK // cols
                st = ATT(u)
                for m in range(8 // per):
                    src = bank(j + m).rearrange("p (h s) -> p h s", h=per)
                    d = PB[u % 2][:, m * BANK:(m + 1) * BANK].rearrange("p (h s) -> p h s", h=per)
                    freed(nc.vector.scalar_tensor_tensor(out=d, in0=src, scalar=HD ** -0.5, in1=add(m * per, per, cols),
                                                         op0=ALU.mult, op1=ALU.add), j + m, m == 8 // per - 1)
                view = PB[u % 2][:, 0:8 * cols].rearrange("p (h s) -> p h s", h=8)
                step(nc.vector.tensor_reduce(st[:, 8:16], view, AX, ALU.max))
                if sink is not None:
                    step(nc.vector.tensor_tensor(st[:, 8:16], st[:, 8:16], sink, ALU.max))
                    step(nc.vector.tensor_tensor(st[:, 0:8], sink, st[:, 8:16], ALU.subtract))
                step(nc.vector.tensor_scalar(st[:, 8:16], st[:, 8:16], -1.0, None, ALU.mult), "att_max")

            def attended(u, jo, t, dst, sinks=None):
                nk = t + 1
                st = ATT(u)
                den = st[:, 16:24]
                v.wait_ge(sem("att_exp"), u + 1)
                view = PB[u % 2][:, 0:8 * nk * P].rearrange("p (h s) -> p h s", h=8)
                step(nc.vector.tensor_reduce(den, view, AX, ALU.add))
                if sinks is not None:
                    v.wait_ge(sem("sink_exp"), sinks)
                    step(nc.vector.tensor_tensor(den, den, st[:, 0:8], ALU.add))
                step(nc.vector.reciprocal(den, den))
                src = bank(jo).rearrange("p (h n) -> p h n", h=8)
                freed(nc.vector.tensor_tensor(dst.rearrange("p (h n) -> p h n", h=8), src, bc(den, HD), ALU.mult), jo, True)

            def causal(h0, n, cols):
                return bc(causal_add[:, 2 * P - cols:2 * P], n, 1)

            def moba_out(t):
                attended(t, J[f"mb_O{t}"], t, XN[:, t, 512:1024])

            q_, k_ = proj_in[:, :, 0:256], proj_in[:, :, 256:512]
            v.wait_ge(sem("g_exp"), 3)
            e3, n3 = (x.rearrange("p (t n) -> p t n", t=TT) for x in (gE, gB_))
            step(nc.vector.tensor_tensor(gKN, k_, n3, ALU.mult), "g_qk", False)
            step(nc.vector.scalar_tensor_tensor(out=q_, in0=q_, scalar=GDK ** -0.5, in1=e3, op0=ALU.mult, op1=ALU.mult), "g_qk")
            key_pairs(J["gla_T"], 1, gKZT)
            transposed(J["gla_T"] + 1, 1, gQT)
            v.wait_ge(sem("bias_written"), 16)
            transposed(J["mb_T"], 2, QT)
            key_pairs(J["mb_T"] + 2, 2, KZT)
            for t in range(TT):
                logits(J[f"mb_L{t}"], t, causal)
            for t in range(TT):
                j = J["gla_A"] + t
                freed(nc.vector.tensor_tensor(AT[:, t], bank(j).rearrange("p (h n) -> p h n", h=4), bc(cum, 4, 1), ALU.mult), j, True)
            moba_out(0)
            v.wait_ge(sem("g_exp"), 4)
            gdec = DEC.rearrange("p (j c) -> p j c", j=2)
            for c in range(3):
                j = J["gla_U"] + c
                u = bank(j).rearrange("p (h n) -> p h n", h=4)
                freed(nc.vector.tensor_tensor(ST[:, c], u, bc(const("head_rows"), GDV), ALU.mult), j, True)
                for pair in range(2 if c else 0):
                    step(nc.vector.scalar_tensor_tensor(
                        out=ST[:, c, 2 * pair:2 * pair + 2], in0=ST[:, c - 1, 2 * pair:2 * pair + 2],
                        scalar=gdec[:, pair, c:c + 1], in1=ST[:, c, 2 * pair:2 * pair + 2],
                        op0=ALU.mult, op1=ALU.add), "state_ready" if c == 2 and pair == 1 else None)
            moba_out(1)
            v.wait_ge(sem("gates_gained"), TT)
            head_norm(J["gla_O"], proj_in[:, :, 1024:1536], XN[:, :, 0:512])
            x_lo(J["mix0"], MIX_COL[0], MIX_PAIRS[0])
            split_lo(v, "wout", 1)
            add_residual(J["wout"])

            for m in range(4):
                j = J["subk"] + m
                freed(nc.vector.tensor_copy(SKT[:, 4 * m:4 * m + 4, :], bank(j).rearrange("p (b t) -> p b t", b=4)), j)
            v.wait_ge(sem("n2w_loaded"), 16)
            norm(1, gain=N2W)
            def routed(u, q):
                n = [0]
                v.sem_clear(sem("route_step"))

                def then(ins):
                    n[0] += 1
                    ins.then_inc(sem("route_step"), 1)
                    v.wait_ge(sem("route_step"), n[0])

                def top16(vals, best, index, width):
                    then(nc.vector.max(best[:, 0:8], vals))
                    then(nc.vector.max_index(index[:, 0:8], best[:, 0:8], vals))
                    then(nc.vector.match_replace(r_w[:, 0:width], best[:, 0:8], vals, NEG))
                    then(nc.vector.max(best[:, 8:16], r_w[:, 0:width]))
                    then(nc.vector.max_index(index[:, 8:16], best[:, 8:16], r_w[:, 0:width]))

                then(nc.vector.tensor_copy(R[:, 0:256], PROJ[:, bass.ds(u * 256, 256)]))
                for p_ in range(2):
                    top16(r_s[:, p_], r_sv[:, p_], r_si[:, p_], NKEYS)
                cand = r_cand.rearrange("p (i j) -> p i j", i=TOPK)
                then(nc.vector.tensor_tensor(cand, bc(r_sv[:, 0], TOPK), bc(r_sv[:, 1], TOPK, 1), ALU.add))
                top16(r_cand, r_top, r_pos, TOPK * TOPK)
                then(nc.vector.tensor_scalar(r_ab[:, 0:16], r_pos, 4, None, ALU.logical_shift_right))
                then(nc.vector.tensor_scalar(r_ab[:, 16:32], r_pos, 15, None, ALU.bitwise_and))
                hot = r_w[:, 0:256].rearrange("p (k j) -> p k j", k=TOPK)
                for p_ in range(2):
                    then(nc.vector.tensor_tensor(hot, bc(r_ab[:, 16 * p_:16 * p_ + 16], TOPK), bc(const("iota"), TOPK, 1),
                                                 ALU.is_equal))
                    then(nc.vector.tensor_tensor(hot, hot, bc(r_si[:, p_], TOPK, 1), ALU.mult))
                    then(nc.vector.tensor_reduce(r_i[:, p_], hot, AX, ALU.add))
                then(nc.vector.tensor_scalar(r_e, r_top, r_top[:, 0:1], None, ALU.subtract))
                nc.vector.scalar_tensor_tensor(out=r_idx[:, q], in0=r_i[:, 0], scalar=float(NKEYS), in1=r_i[:, 1],
                                               op0=ALU.mult, op1=ALU.add).then_inc(sem("idx_ready"), 1)
                then(nc.vector.memset(SS[:, 6:7], 0.0))
                nc.vector.memset(SS[:, 7:8], 0.0).then_inc(sem("top_ready"), 1)
                v.wait_ge(sem("gate_exp"), u + 1)
                then(nc.vector.tensor_reduce(r_sum, r_e, AX, ALU.add))
                then(nc.vector.reciprocal(r_rs, r_sum))
                then(nc.vector.tensor_scalar(r_gate[:, q], r_e, r_rs, None, ALU.mult))

            def dots(u, q, t, b):
                for k in range(4):
                    n = (4 * b + k) % NU
                    v.wait_ge(u_loaded[n], u * 32 + 16 * (1 + b // 2))
                    ins = nc.vector.tensor_tensor_reduce(out=ubuf[n], in0=ubuf[n], in1=XN[:, t], scale=1.0, scalar=0.0,
                                                         op0=ALU.mult, op1=ALU.add, accum_out=r_dot[:, b % 2, k:k + 1])
                ins.then_inc(sem("dots_done"), 1)

            def weights(u, q, b):
                v.wait_ge(sem("gelu_done"), u * 4 + (b + 1))
                nc.vector.tensor_tensor(r_wt[:, b % 2], r_act[:, b % 2], r_gate[:, q, 4 * b:4 * b + 4],
                                        ALU.mult).then_inc(sem("weights_ready"), 1)

            def vec_unit(u, q, t, first=False, last=False):
                for b in range(4):
                    if not (first and b < 2):
                        v.wait_ge(sem("gelu_done"), u * 4 + (b - 1))
                        dots(u, q, t, b)
                    if not (first and b < 3):
                        v.wait_ge(sem("diag_ready"), u * 4 + (b - 2))
                    if b > 0:
                        weights(u, q, b - 1)
                    elif not first:
                        weights(u - 1, 1 - q, 3)
                    if b == 1 and not last:
                        routed(u + 1, 1 - q)

            def query_cols(m):
                transposed(query_job(m), 1, qT[:, 2 * m:2 * m + 2, :])

            def scores(m):
                j = score_job(m)
                freed(nc.vector.tensor_copy(SCORE[:, m * BANK:(m + 1) * BANK], bank(j)), j, wait=True)

            query_cols(0)
            query_cols(1)
            split_lo(v, "query", 2)
            query_cols(2)
            scores(0)
            routed(0, 0)
            split_lo(v, "query", 3)
            query_cols(3)
            query_cols(4)
            dots(0, 0, 0, 0)
            query_cols(5)
            dots(0, 0, 0, 1)
            query_cols(6)
            query_cols(7)
            for m in range(1, 8):
                scores(m)
            vec_unit(0, 0, 0, first=True)
            vec_unit(1, 1, 0)
            with v.Fori(1, PH // 2) as i:
                vec_unit(i * 2, 0, 0)
                vec_unit(i * 2 + 1, 1, 0)
            with v.Fori(PH // 2, UNITS // 2 - 1) as i:
                vec_unit(i * 2, 0, 1)
                vec_unit(i * 2 + 1, 1, 1)
            vec_unit(UNITS - 2, 0, 1)
            vec_unit(UNITS - 1, 1, 1, last=True)
            v.wait_ge(sem("diag_ready"), 4 * UNITS - 2)
            weights(UNITS - 1, 1, 3)
            v.wait_ge(sem("dots_done"), 4 * UNITS)
            add_residual(J["peer"], by_tile=True)

            norm(2)
            hq, hf, hi, hg = (proj_ab[:, :, 1536 + 512 * n:2048 + 512 * n] for n in range(4))

            def h_abs():
                step(nc.vector.scalar_tensor_tensor(out=hLN, in0=hf, scalar=-1.0, in1=hf, op0=ALU.mult, op1=ALU.max), "h_abs")

            def h_log_f():
                v.wait_ge(sem("h_log"), 1)
                v.wait_ge(sem("h_sig"), 1)
                step(nc.vector.scalar_tensor_tensor(out=hf, in0=hf, scalar=0.0, in1=hLN, op0=ALU.min, op1=ALU.subtract), "h_logf")

            def level(n):
                L, e = LEVELS[n], hE0 if n % 2 == 0 else hE1
                return (L, *(x.rearrange("p (b i) -> p b i", i=2 * L) for x in (hBT, e, hQT, hKT)))

            def relative(n):
                L, bt, e, _, _ = level(n)
                ref = bt[:, :, L - 1:L].broadcast_to([P, 4 * S // (2 * L), 2 * L])
                step(nc.vector.tensor_tensor(e, bt, ref, ALU.subtract), "h_rel")

            def operands(n):
                L, _, e, qv, kv = level(n)
                v.wait_ge(sem("h_relexp"), 2 * n + 2)
                step(nc.vector.tensor_tensor(e[:, :, L:2 * L], e[:, :, L:2 * L], qv[:, :, L:2 * L], ALU.mult), "h_lev", False)
                step(nc.vector.tensor_tensor(e[:, :, 0:L], e[:, :, 0:L], kv[:, :, 0:L], ALU.mult), "h_lev")

            v.wait_ge(sem("levels_loaded"), 16)

            def mask_level(n):
                if n >= 2:
                    v.wait_ge(sem("level_added"), n - 1)
                for t in range(TT):
                    j = J[f"hg_L{n}"] + t
                    freed(nc.vector.tensor_tensor(hTMP[n % 2][:, t], bank(j).rearrange("p (h n) -> p h n", h=4),
                                                  bc(LEV[:, n], 4, 1), ALU.mult), j, t == 1)
                if n < len(LEVELS) - 1:
                    v.sem_inc(sem("level_masked"))
                else:
                    v.wait_ge(sem("level_added"), n)
                    step(nc.vector.tensor_tensor(AT, AT, hTMP[n % 2], ALU.add), "state_ready")

            evac_cols("ab", 7, proj_ab, {4: h_abs, 5: h_log_f})
            transposed(J["sb_T"], 2, QT)
            key_pairs(J["sb_T"] + 2, 2, KZT)
            for m in range(6):
                j = J["sb_Z"] + m
                z = A[:, m * BANK:(m + 1) * BANK]
                freed(nc.vector.tensor_scalar(z, bank(j), HD ** -0.5, None, ALU.mult), j, True)
                step(nc.vector.scalar_tensor_tensor(out=SP_BANKS[m], in0=z, scalar=-1.0, in1=z, op0=ALU.mult,
                                                    op1=ALU.max), "sb_abs", False)
            transposed(J["hg_B"], 2, hBT.rearrange("p (h t) -> p h t", h=4))
            for t in range(TT):
                j = J["hg_suf"] + t
                freed(nc.vector.tensor_copy(hSF[:, t], bank(j)), j, True)
            relative(0)
            relative(1)
            transposed(J["hg_T"], 2, hQT.rearrange("p (h t) -> p h t", h=4))
            transposed(J["hg_T"] + 2, 2, hKT.rearrange("p (h t) -> p h t", h=4))
            v.wait_ge(sem("sb_log"), 2)
            for z, l in ((ZL0, L0), (Z1, L1)):
                step(nc.vector.scalar_tensor_tensor(out=l, in0=z, scalar=0.0, in1=l, op0=ALU.max, op1=ALU.add))
            for l in (*(L0[:, g].rearrange("p (h t) -> p h t", h=4)[:, :, 0:P] for g in range(2)), L1):
                step(nc.vector.tensor_tensor(l, l, bc(const("before"), 4 if l is not L1 else 8, 1), ALU.mult), "sb_plus")

            for t in range(TT):
                j = J["hg_D"] + t
                freed(nc.vector.tensor_tensor(AT[:, t], bank(j).rearrange("p (h n) -> p h n", h=4), bc(ident, 4, 1), ALU.mult), j, True)
            operands(0)
            v.wait_ge(sem("z_masked"), 2)
            for m in range(6):
                j = J["sb_C"] + m
                d = A[:, m * BANK:(m + 1) * BANK]
                freed(nc.vector.tensor_tensor(d, d, bank(j), ALU.subtract), j, m == 5)
            operands(1)
            mask_level(0)
            relative(2)
            operands(2)
            mask_level(1)
            relative(3)
            for t in range(TT):
                j = J["sb_O"] + t
                freed(nc.vector.tensor_copy(XN[:, t, 0:512], bank(j)), j)
            for n in (3, 4, 5):
                operands(n)
                mask_level(n - 1)
                if n < 5:
                    relative(n + 1)
            v.wait_ge(sem("h_bexp"), 1)
            hdec = hT0.rearrange("p (h c i) -> p h c i", h=4, c=4)
            for c in range(3):
                j = J["hg_U"] + c
                freed(nc.vector.tensor_copy(ST[:, c], bank(j).rearrange("p (h n) -> p h n", h=4)), j, True)
                for h in range(4 if c else 0):
                    step(nc.vector.scalar_tensor_tensor(out=ST[:, c, h], in0=ST[:, c - 1, h],
                                                        scalar=hdec[:, h, c, CH - 1:CH], in1=ST[:, c, h],
                                                        op0=ALU.mult, op1=ALU.add), wait=(h == 3))
            mask_level(5)
            v.wait_ge(sem("gates_gained"), 2 * TT)
            head_norm(J["hg_O"], hg, XN[:, :, 512:1024])
            x_lo(J["mix1"])
            split_lo(v, "about", 1)
            add_residual(J["about"])

            def vec_ffn(l, k):
                norm(k)
                j0 = J[f"up{l}"]

                def conv(i, tiles, more):
                    for q in range(tiles):
                        v.wait_ge(sem("tap2_done"), i * RING + (FT * l + q + 1))
                        for tap in (1, 0):
                            n = 2 - tap
                            if tap == 0:
                                v.wait_ge(sem("tap1_done"), i * RING + (FT * l + q + 1))
                            for g in range(2):
                                d = CT[:, q, g * S + n:(g + 1) * S]
                                ins = nc.vector.scalar_tensor_tensor(
                                    out=d, in0=PS[:, (j0 + q) % 8, g * S:(g + 1) * S - n],
                                    scalar=CONV[:, l, bass.ds(i * RING + (tap * 2 * FT + g * FT + q), 1)], in1=d,
                                    op0=ALU.mult, op1=ALU.add)
                            ins.then_inc(sem("tap1_done") if tap else evac_done, 1)
                        if more is None:
                            w = pieces[f"up{l}", q]
                            v.wait_ge(hi_ready[w.h], i + (w.count + 1))
                            nc.vector.tensor_tensor(WLO[:, w.cols], RAW[:, w.cols], WHI[:, w.cols].bitcast(F32),
                                                    ALU.subtract).then_inc(lo_ready[w.h], 1)
                        else:
                            split_lo(v, *more[q])

                with v.Fori(0, UP_BODIES - 1) as i:
                    conv(i, RING, None)
                ring = [(f"up{l}", n) for n in range(FT)] + [(f"down{l}", n) for n in range(FP)]
                conv(UP_BODIES - 1, RING, ring[RING * UP_BODIES:])
                conv(UP_BODIES, FT % RING, ring[RING * UP_BODIES + RING:])
                for n in range(RING, FP):
                    split_lo(v, f"down{l}", n)
                add_residual(J[f"down{l}"], by_tile=True)

            def vec_ple(l, k):
                norm(k)
                j = J[f"pT{l}"]
                src = bank(j).rearrange("p (c t) -> p c t", c=2)
                step(nc.vector.tensor_copy(PHI[:, :, :], src))
                freed(nc.vector.tensor_tensor(PLO[:, :, :], src, PHI[:, :, :].bitcast(F32), ALU.subtract), j)
                evac_cols(f"gate{l}", 2, GATE)
                v.wait_ge(sem("ple_sigmoid"), l + 1)
                for t in range(TT):
                    for m in range(2):
                        j = J[f"proj{l}"] + 2 * t + m
                        g = GATE[:, t, m * BANK:(m + 1) * BANK]
                        freed(nc.vector.tensor_tensor(g, bank(j), g, ALU.mult), j, True)
                        d = X[:, t, m * BANK:(m + 1) * BANK]
                        step(nc.vector.tensor_tensor(d, d, g, ALU.add), "x_final" if l == 1 and m == 1 else None)
                        if l == 0:
                            sum_squares(t, m)

            vec_ffn(0, 3)
            vec_ple(0, 4)

            norm(5)

            def window_q(n):
                head_norms(heads_of(proj_c, 512 * n, 8), 8, SS[:, 8 + 16 * n:24 + 16 * n],
                           SS[:, 56 + 16 * n:72 + 16 * n], QK_GAIN[2], ready="queries_ready")

            def window_k():
                keys = heads_of(proj_c, 1024, SWKV)
                head_norms(keys, SWKV, SS[:, 40:48], SS[:, 48:56], QK_GAIN[3])
                for t in range(TT):
                    step(nc.vector.tensor_copy(KDUP[:, t], bc(keys[:, t], 2)), "keys_ready")

            evac_cols("c", 3, proj_c, {0: lambda: window_q(0), 1: lambda: window_q(1), 2: window_k})
            transposed(J["sw_T"], 4, QT)
            key_pairs(J["sw_T"] + 4, 2, KZT)
            v.wait_ge(sem("bias_loaded"), 16)
            first = att_no[0]

            def window_logits(u):
                def biased(h0, n, cols, base=8 * (u % 2)):
                    return BIAS[:, base + h0:base + h0 + n, 2 * P - cols:2 * P]

                logits(J[f"sw_L{u}"], u // 2, biased, sink=SINK[:, 8 * (u % 2):8 * (u % 2) + 8])

            window_logits(0)
            for u in range(SW_UNITS):
                if u + 1 < SW_UNITS:
                    window_logits(u + 1)
                t, g = u // 2, u % 2
                attended(first + u, J[f"sw_O{u}"], t, XN[:, t, g * 512:(g + 1) * 512], sinks=u + 1)
            x_lo(J["mix2"])
            add_residual(J["cout"])
            vec_ffn(1, 6)
            vec_ple(1, 7)

        @block.tensor
        def _(pe):
            def bank(j):
                if j >= 8:
                    pe.wait_ge(evac_done, j - 7)
                return PS[:, j % 8, :]

            def transposes(j, blocks):
                b = bank(j)
                for n, src in enumerate(blocks):
                    ins = pe.transpose(b[:, n * P:(n + 1) * P], src, ident)
                ins.then_inc(pe_done, 1)

            def mixed_T(k, attended, recurrences):
                pe.wait_ge(evac_done, attended)
                for n, m in enumerate(MIX_PAIRS[k]):
                    if n == 2 and recurrences:
                        pe.wait_ge(sem("mixed"), TT * recurrences)
                    transposes(J[f"mix{k}"] + n, [XN[:, t, (2 * m + c) * P:(2 * m + c + 1) * P] for c in range(2) for t in range(TT)])

            xn_no = [0]

            def norm(k):
                for m in range(4):
                    if m % 2 == 0:
                        xn_no[0] += 1
                        for t in range(TT):
                            pe.wait_ge(xn_ready[t], xn_no[0])
                    transposes(J[f"norm{k}"] + m, [XN[:, t, (2 * m + c) * P:(2 * m + c + 1) * P] for c in range(2) for t in range(TT)])

            def product(o, x, w, first, last):
                pe.matmul(o, x[0], w[0], start=first, stop=False)
                pe.matmul(o, x[0], w[1], start=False, stop=False)
                return pe.matmul(o, x[1], w[0], start=False, stop=last)

            def xs(c, rows):
                return XHI[:, c, rows], XLO[:, c, rows]

            def split_weights(name, n, c=KC):
                w = pieces[name, n]
                pe.wait_ge(lo_ready[w.h], w.count)
                return part(WHI, w, c), part(WLO, w, c)

            def dense_chunk(name, n):
                hi, lo = split_weights(name, n)
                for t in range(TT):
                    b = bank(chunk_job(name, n) + t)
                    for c in range(KC):
                        ins = product(b, xs(c, slice(t * P, (t + 1) * P)), (hi[:, c, :], lo[:, c, :]), c == 0, c == KC - 1)
                    ins.then_inc(pe_done, 1)

            def dense(name, chunks, ready):
                pe.wait_ge(evac_done, ready)
                for n in range(chunks):
                    dense_chunk(name, n)

            pe.wait_ge(sem("const_loaded"), 16)
            pe.wait_ge(sem("vec_loaded"), 16 * 5)
            pe.transpose(PS[:, J["vecs"], 0:64], VROW[0:64, :], ident[0:64, 0:64]).then_inc(pe_done, 1)
            norm(0)
            pe.wait_ge(sem("conv_loaded"), 16 * 6)
            for n in range(4):
                ins = pe.transpose(PS[:, J["conv"], n * 4 * FT:(n + 1) * 4 * FT], CROW[n][:, :], ident[0:4 * FT, 0:4 * FT])
            ins.then_inc(pe_done, 1)
            pe.wait_ge(sem("rel_loaded"), 48)
            pe.matmul(PS[0:SWH, J["relb"], 0:384], RB, OH, start=True, stop=True).then_inc(pe_done, 1)
            pe.wait_ge(evac_done, END["norm0"])
            b = bank(J["gr"])
            pe.wait_ge(sem("gr_loaded"), 32)
            for c in range(KC):
                for n, x in enumerate((XHI, XLO)):
                    ins = pe.matmul(b[0:GRANK, 0:S], W_GR[:, c, :], x[:, c, :].bitcast(F32), start=(c == n == 0),
                                    stop=(c == KC - 1 and n == 1))
            ins.then_inc(pe_done, 1)
            dense_chunk("win", 0)
            pe.wait_ge(evac_done, END["gr"])
            b = bank(J["alpha"])
            for t in range(TT):
                ins = pe.matmul(b[:, t * 256:(t + 1) * 256], GRT[:, t * P:(t + 1) * P], W_ALPHA, start=True, stop=True)
            ins.then_inc(pe_done, 1)
            dense_chunk("win", 1)
            dense_chunk("win", 2)
            pe.wait_ge(sem("g_ready"), 1)
            for n, m in enumerate((cum, suf)):
                b = bank(J["gla_cum"] + n)
                for t in range(TT):
                    ins = pe.matmul(b[:, t * 256:(t + 1) * 256], m, gG[:, t * 256:(t + 1) * 256], start=True, stop=True)
                ins.then_inc(pe_done, 1)
            b = bank(J["gla_dec"])
            for pair in range(2):
                for t in range(TT):
                    ins = pe.matmul(b[:, pair * 4 + 2 * t:pair * 4 + 2 * t + 2], gG[:, t * 256 + pair * P:t * 256 + (pair + 1) * P],
                                    cum[:, CH - 1:P:CH], start=True, stop=True)
            ins.then_inc(pe_done, 1)
            for n in range(3, 6):
                dense_chunk("win", n)

            def updates(j, count, kcols, values):
                for c in range(3):
                    pe.wait_ge(sem("kst_ready"), 3 * count + c + 1)
                    b = bank(j + c)
                    for h in range(4):
                        ins = pe.matmul(b[:, h * P:(h + 1) * P], kcols(c, h), values(c // 2, h), start=True, stop=True)
                    ins.then_inc(pe_done, 1)

            def outputs(j, count, values, queries):
                pe.wait_ge(sem("state_ready"), count + 1)
                for t in range(TT):
                    b = bank(j + t)
                    for h in range(4):
                        o = b[:, h * P:(h + 1) * P]
                        pe.matmul(o, AT[:, t, h, :], values(t, h), start=True, stop=False, skip_group_check=True)
                        for par in range(2):
                            c = 2 * t + par
                            if c:
                                ins = pe.matmul(o[par * CH:(par + 1) * CH, :], queries(t, h, par), ST[:, c - 1, h, :],
                                                start=False, stop=True, skip_group_check=True)
                    ins.then_inc(pe_done, 1)

            def qk_T(j, sources):
                for m in range(len(sources) // 2):
                    transposes(j + m, [sources[2 * m + c](t) for c in range(2) for t in range(TT)])
                pe.wait_ge(evac_done, j + len(sources) // 2)

            def columns(proj, c0, n):
                return [lambda t, c=c: proj[:, t, c0 + c * P:c0 + (c + 1) * P] for c in range(n)]

            def logits(j, t, pair, variant):
                cols = (t + 1) * P
                per = BANK // cols
                for m in range(8 // per):
                    b = bank(j + m)
                    for h in range(per):
                        hh = m * per + h
                        ins = pe.matmul(b[:, h * cols:(h + 1) * cols], QT[:, pair(hh), t * P:(t + 1) * P],
                                        KZT[:, variant(hh), 0:cols], start=True, stop=True)
                    ins.then_inc(pe_done, 1)

            def attended(u, jp, jo, t, values):
                nk = t + 1
                pe.wait_ge(sem("att_exp"), u + 1)
                for m in range(2 * nk):
                    transposes(jp + m, [PB[u % 2][:, (4 * m + n) * P:(4 * m + n + 1) * P] for n in range(4)])
                pe.wait_ge(evac_done, jp + 2 * nk)
                b = bank(jo)
                for h in range(8):
                    for k in range(nk):
                        ins = pe.matmul(b[:, h * HD:(h + 1) * HD], PT[:, h * nk + k, :], values(k, h),
                                        start=(k == 0), stop=(k == nk - 1))
                ins.then_inc(pe_done, 1)

            def moba_logits(t):
                logits(J[f"mb_L{t}"], t, lambda h: h // 2, lambda h: h)

            def moba_out(t):
                attended(t, J[f"mb_P{t}"], J[f"mb_O{t}"], t,
                         lambda k, h: proj_in[:, k, 2560 + h * HD:2560 + (h + 1) * HD])

            def gla_values(t, h):
                return proj_in[:, t, 512 + h * P:512 + (h + 1) * P]

            pe.wait_ge(sem("g_qk"), 2)
            transposes(J["gla_T"], [gKN[:, t, j * P:(j + 1) * P] for j in range(2) for t in range(TT)])
            transposes(J["gla_T"] + 1, [proj_in[:, t, j * P:(j + 1) * P] for j in range(2) for t in range(TT)])
            qk_T(J["mb_T"], columns(proj_in, 1536, 8))
            for t in range(TT):
                moba_logits(t)
            pe.wait_ge(evac_done, END["gla_T"])
            for t in range(TT):
                b = bank(J["gla_A"] + t)
                for h in range(4):
                    ins = pe.matmul(b[:, h * P:(h + 1) * P], gKZT[:, h, t * P:(t + 1) * P], gQT[:, h // 2, t * P:(t + 1) * P],
                                    start=True, stop=True)
                ins.then_inc(pe_done, 1)
            moba_out(0)
            updates(J["gla_U"], 0, lambda c, h: KSC[:, c, (h // 2) * P:(h // 2 + 1) * P], gla_values)
            moba_out(1)
            outputs(J["gla_O"], 0, gla_values, lambda t, h, par: gQT[:, h // 2, t * P + par * CH:t * P + (par + 1) * CH])
            mixed_T(0, END["mb_O1"], 1)
            dense("wout", 2, END["mix0"])

            pe.wait_ge(sem("subkeys_loaded"), 16)
            for m in range(4):
                transposes(J["subk"] + m, [SKN[:, 4 * m + n, :] for n in range(4)])
            norm(1)
            pe.wait_ge(evac_done, END["norm1"])
            def queries(m):
                hi, lo = split_weights("query", m // 2)
                b = bank(query_job(m))
                for q in range(2):
                    w0 = (m % 2) * 256 + q * P
                    for c in range(KC):
                        ins = product(b[:, q * S:(q + 1) * S], (hi[:, c, w0:w0 + P], lo[:, c, w0:w0 + P]), xs(c, slice(0, S)),
                                      c == 0, c == KC - 1)
                ins.then_inc(pe_done, 1)

            def scores(m):
                t, h0 = m // 4, (m % 4) * 2
                pe.wait_ge(evac_done, query_job(h0 + 1) + 1)
                b = bank(score_job(m))
                for n in range(4):
                    u = 2 * h0 + n
                    ins = pe.matmul(b[:, n * P:(n + 1) * P], qT[:, u, t * P:(t + 1) * P], SKT[:, u, :], start=True, stop=True)
                ins.then_inc(pe_done, 1)

            for m in range(3):
                queries(m)
            scores(0)
            for m in range(3, 8):
                queries(m)
            for m in range(1, 8):
                scores(m)

            def sum_rows(u, t):
                for b in range(4):
                    pe.wait_ge(sem("diag_ready"), u * 4 + (b + 1))
                    for k in range(4):
                        n = 4 * b + k
                        pe.wait_ge(v_loaded[n], u * 16 + 16)
                        for m in range(2):
                            ins = pe.matmul(PS[:, (J["peer"] + 2 * t + m) % 8, :], DIAG[:, b % 2, k, :],
                                            vbuf[n][:, m * BANK:(m + 1) * BANK], start=False, stop=False, skip_group_check=True)
                    ins.then_inc(sem("rows_summed"), 1)

            for t in range(TT):
                accs = [bank(J["peer"] + 2 * t + m) for m in range(2)]
                for acc in accs:
                    pe.matmul(acc, zeros, C[:, 0:BANK], start=True, stop=False, skip_group_check=True)
                with pe.Fori(t * PH // 2, (t + 1) * PH // 2) as i:
                    sum_rows(i * 2, t)
                    sum_rows(i * 2 + 1, t)
                for acc in accs:
                    pe.matmul(acc[:, 0:P], zeros, ident, start=False, stop=True, skip_group_check=True).then_inc(pe_done, 1)

            norm(2)
            dense("ab", 7, END["norm2"])
            pe.wait_ge(evac_done, END["ab"])
            qk_T(J["sb_T"], columns(proj_ab, 0, 8))
            for m in range(4):
                b = bank(J["sb_Z"] + m)
                for n in range(2):
                    h = 2 * m + n
                    ins = pe.matmul(b[:, n * S:(n + 1) * S], KZT[:, h, 0:P], QT[:, h // 2, :], start=True, stop=True)
                ins.then_inc(pe_done, 1)
            for m in range(2):
                b = bank(J["sb_Z"] + 4 + m)
                for n in range(4):
                    h = 4 * m + n
                    ins = pe.matmul(b[:, n * P:(n + 1) * P], KZT[:, h, P:S], QT[:, h // 2, P:S], start=True, stop=True)
                ins.then_inc(pe_done, 1)
            pe.wait_ge(sem("h_logf"), 1)
            for m in range(2):
                b = bank(J["hg_B"] + m)
                for n in range(2):
                    for t in range(TT):
                        h = 2 * m + n
                        ins = pe.matmul(b[:, n * S + t * P:n * S + (t + 1) * P], proj_ab[:, t, 2048 + h * P:2048 + (h + 1) * P],
                                        cum, start=True, stop=True)
                ins.then_inc(pe_done, 1)
            for t in range(TT):
                pe.matmul(bank(J["hg_suf"] + t), suf, proj_ab[:, t, 2048:2560], start=True, stop=True).then_inc(pe_done, 1)
            pe.wait_ge(sem("h_silu"), 1)
            for m in range(2):
                transposes(J["hg_T"] + m, [proj_ab[:, t, 1536 + (2 * m + c) * P:1536 + (2 * m + c + 1) * P]
                                           for c in range(2) for t in range(TT)])
            for m in range(2):
                transposes(J["hg_T"] + 2 + m, [hKK[:, t, (2 * m + c) * P:(2 * m + c + 1) * P] for c in range(2) for t in range(TT)])
            pe.wait_ge(evac_done, END["hg_T"])
            for t in range(TT):
                b = bank(J["hg_D"] + t)
                for h in range(4):
                    o = h * S + t * P
                    ins = pe.matmul(b[:, h * P:(h + 1) * P], hKT[:, o:o + P], hQT[:, o:o + P], start=True, stop=True)
                ins.then_inc(pe_done, 1)
            pe.wait_ge(sem("sb_plus"), 3)
            for m in range(4):
                b = bank(J["sb_C"] + m)
                pe.matmul(b, incl, SP_BANKS[m], start=True, stop=False, skip_group_check=True)
                pe.matmul(b.rearrange("p (h t) -> p h t", h=2)[:, :, P:S], ones, L1[:, 2 * m:2 * m + 2, :],
                          start=False, stop=True, skip_group_check=True).then_inc(pe_done, 1)
            for m in range(2):
                b = bank(J["sb_C"] + 4 + m)
                pe.matmul(b, incl, SP_BANKS[4 + m], start=True, stop=True).then_inc(pe_done, 1)

            def level(n):
                pe.wait_ge(sem("h_lev"), 2 * n + 2)
                e = hE0 if n % 2 == 0 else hE1
                for t in range(TT):
                    b = bank(J[f"hg_L{n}"] + t)
                    for h in range(4):
                        o = h * S + t * P
                        ins = pe.matmul(b[:, h * P:(h + 1) * P], e[:, o:o + P], e[:, o:o + P], start=True, stop=True)
                    ins.then_inc(pe_done, 1)

            def hgrn_values(t, h):
                return proj_ab[:, t, 2560 + h * P:2560 + (h + 1) * P]

            level(0)
            level(1)
            pe.wait_ge(sem("sb_exp"), 2)
            for t in range(TT):
                b = bank(J["sb_O"] + t)
                for h in range(8):
                    vals = lambda k: proj_ab[:, k, 1024 + h * HD:1024 + (h + 1) * HD]
                    ins = pe.matmul(b[:, h * HD:(h + 1) * HD], Z0[:, h, t * P:(t + 1) * P], vals(0), start=True, stop=(t == 0))
                    if t:
                        ins = pe.matmul(b[:, h * HD:(h + 1) * HD], Z1[:, h, :], vals(1), start=False, stop=True)
                ins.then_inc(pe_done, 1)

            for n in (2, 3, 4):
                level(n)
            updates(J["hg_U"], 1, lambda c, h: KSC[:, c, h * P:(h + 1) * P], hgrn_values)
            level(5)
            pe.wait_ge(sem("h_qb"), 1)
            outputs(J["hg_O"], 1, hgrn_values, lambda t, h, par: hQB[:, h * S + t * P + par * CH:h * S + t * P + (par + 1) * CH])
            mixed_T(1, END["sb_O"], 2)
            dense("about", 2, END["mix1"])

            def ffn(l, k):
                norm(k)
                pe.wait_ge(evac_done, END[f"norm{k}"])
                j0 = J[f"up{l}"]

                def up_tiles(i, tiles):
                    for q in range(tiles):
                        w = pieces[f"up{l}", q]
                        pe.wait_ge(lo_ready[w.h], i + w.count)
                        hi, lo = (part(t, w).rearrange("p c (g n) -> p c g n", g=2) for t in (WHI, WLO))
                        pe.wait_ge(evac_done, i * RING + (j0 + q - RING + 1))
                        for g in range(2):
                            for c in range(KC):
                                ins = product(PS[:, (j0 + q) % 8, g * S:(g + 1) * S], (hi[:, c, g, :], lo[:, c, g, :]),
                                              xs(c, slice(0, S)), c == 0, c == KC - 1)
                        ins.then_inc(pe_done, 1)

                with pe.Fori(0, UP_BODIES) as i:
                    up_tiles(i, RING)
                up_tiles(UP_BODIES, FT % RING)
                j1 = J[f"down{l}"]
                for n in range(FP):
                    pe.wait_ge(sem("hidden_ready"), FT * l + 2 * n + 2)
                    hi, lo = split_weights(f"down{l}", n, 2)
                    for t in range(TT):
                        if n == 0 and t == 1:
                            pe.wait_ge(evac_done, END[f"up{l}"])
                        for r in range(2):
                            c = 2 * n + r
                            rows = slice(t * P, (t + 1) * P)
                            for m in range(2):
                                cols = slice(m * BANK, (m + 1) * BANK)
                                ins = product(PS[:, (j1 + 2 * t + m) % 8, :], (HHI[:, c, rows], HLO[:, c, rows]),
                                              (hi[:, r, cols], lo[:, r, cols]), c == 0, c == FT - 1)
                                if c == FT - 1:
                                    ins.then_inc(pe_done, 1)
                    if n < FP - 1:
                        ins.then_inc(sem("down_used"), 1)

            def ple(l, k):
                norm(k)
                pe.wait_ge(sem("p_loaded"), 16 + 16 * l)
                transposes(J[f"pT{l}"], [PIN[:, l, t, c * P:(c + 1) * P] for c in range(2) for t in range(TT)])
                dense(f"gate{l}", 2, END[f"norm{k}"])
                hi, lo = split_weights(f"proj{l}", 0, 2)
                pe.wait_ge(evac_done, END[f"pT{l}"])
                for t in range(TT):
                    rows = slice(t * P, (t + 1) * P)
                    for m in range(2):
                        cols = slice(m * BANK, (m + 1) * BANK)
                        b = bank(J[f"proj{l}"] + 2 * t + m)
                        for c in range(2):
                            ins = product(b, (PHI[:, c, rows], PLO[:, c, rows]), (hi[:, c, cols], lo[:, c, cols]), c == 0, c == 1)
                        ins.then_inc(pe_done, 1)

            ffn(0, 3)
            ple(0, 4)
            norm(5)
            dense("c", 3, END["norm5"])
            pe.wait_ge(evac_done, J["c"] + 4)
            pe.wait_ge(sem("queries_ready"), 2)
            for m in range(4):
                transposes(J["sw_T"] + m, [proj_c[:, t, (2 * m + c) * P:(2 * m + c + 1) * P] for c in range(2) for t in range(TT)])
            pe.wait_ge(sem("keys_ready"), TT)
            for m in range(2):
                transposes(J["sw_T"] + 4 + m, [KDUP[:, t, 2 * m + c].rearrange("p d n -> p (d n)") for c in range(2) for t in range(TT)])
            pe.wait_ge(evac_done, END["sw_T"])

            def window_logits(u):
                g = u % 2
                logits(J[f"sw_L{u}"], u // 2, lambda h: (8 * g + h) // 2, lambda h: ((8 * g + h) // 4) * 2 + h % 2)

            window_logits(0)
            for u in range(SW_UNITS):
                if u + 1 < SW_UNITS:
                    window_logits(u + 1)
                g = u % 2
                attended(TT + u, J[f"sw_P{u}"], J[f"sw_O{u}"], u // 2,
                         lambda k, h, g=g: proj_c[:, k, 1280 + ((8 * g + h) // 4) * HD:1280 + ((8 * g + h) // 4 + 1) * HD])
            mixed_T(2, END["sw_O3"], 0)
            dense("cout", 2, END["mix2"])
            ffn(1, 6)
            ple(1, 7)


_INS = ['x', 'norm1_w', 'w_in', 'gla_w_alpha', 'gla_b_alpha', 'gla_out_norm_w', 'moba_q_norm_w', 'moba_k_norm_w',
        'mix_scale', 'w_out', 'norm2_w', 'peer_w_query', 'peer_subkeys', 'peer_u', 'peer_v', 'p_2', 'mix_norm_2',
        'ab_w_in_2', 'hg_out_norm_2', 'ab_w_out_2', 'c_w_in_2', 'q_norm_2', 'k_norm_2', 'sinks_2',
        'rel_bias_2', 'c_w_out_2', 'ffn_norm_2', 'ffn_up_2', 'ffn_conv_2', 'ffn_conv_b_2', 'ffn_down_2',
        'ple_norm_2', 'ple_gate_2', 'ple_proj_2']


def kernel(**inputs):
    import numpy as _np
    import concourse.bacc as _bacc
    from concourse.bass_utils import run_bass_kernel_spmd as _run

    nc = _bacc.Bacc("TRN2", target_bir_lowering=False, num_devices=1)
    small, at, levels, onehot, outside = shape_constants()
    arrays, aps = {}, {}
    given = [(n, _np.ascontiguousarray(inputs[n])) for n in _INS]
    given += [("c_small", small), ("c_levels", levels), ("c_onehot", onehot), ("c_outside", outside)]
    for name, arr in given:
        arrays[f"in_{name}"] = arr
        aps[name] = nc.dram_tensor(f"in_{name}", arr.shape, mybir.dt.from_np(arr.dtype), kind="ExternalInput").ap()
    out = nc.dram_tensor("out_0", (1, S, D), F32, kind="ExternalOutput").ap()
    build(nc, aps, out, at)
    r = _run(nc, [arrays], core_ids=[0])
    return r.results[0]["out_0"]
```
